# Optimizing a Trainium2 kernel written in Bass

```python
import jax, jax.numpy as jnp
from jax import lax
import numpy as np

D_MODEL = 1024
BATCH = 1
SEQ = 1024
DEPTH = 1

CHUNK = 64
RNN_WIDTH = 1024
RNN_HEADS = 8
RNN_HEAD_DIM = RNN_WIDTH // RNN_HEADS
CONV_WIDTH = 4
LRU_C = 8.0
SGU_WIDTH = 1024
SGU_GROUPS = 8
SGU_GROUP_DIM = SGU_WIDTH // SGU_GROUPS
SGU_BLOCK = 2 * CHUNK
D_FF = 3 * D_MODEL
FFN_CONV_WIDTH = 3
N_BRANCHES = 2
N_MOD = 6
EPS = 1e-6
IN_COLS = 2 * RNN_WIDTH + 2 * SGU_WIDTH + N_BRANCHES * D_MODEL

kernel_name = "hybrid_rglru_sgu_convffn_block"

def _rmsnorm(x, g):
    x32 = x.astype(jnp.float32)
    y = x32 * lax.rsqrt(jnp.mean(x32 * x32, axis=-1, keepdims=True) + EPS)
    return (y * g.astype(jnp.float32)).astype(x.dtype)

def _layernorm(x, g, b):
    x32 = x.astype(jnp.float32)
    mu = jnp.mean(x32, axis=-1, keepdims=True)
    var = jnp.mean(jnp.square(x32 - mu), axis=-1, keepdims=True)
    y = (x32 - mu) * lax.rsqrt(var + EPS)
    return (y * g.astype(jnp.float32) + b.astype(jnp.float32)).astype(x.dtype)

def _modulated_norm(x, g, shift, scale):
    return _rmsnorm(x, g) * (1.0 + scale[:, None, :]) + shift[:, None, :]

def _causal_dwconv(x, w, b):
    k_width = w.shape[0]
    seq = x.shape[1]
    xp = jnp.pad(x, ((0, 0), (k_width - 1, 0), (0, 0)))
    y = b + xp[:, 0:seq, :] * w[0]
    for k in range(1, k_width):
        y = y + xp[:, k:k + seq, :] * w[k]
    return y

def _block_diag(x, w, b):
    bsz, seq, _ = x.shape
    xh = x.reshape(bsz, seq, RNN_HEADS, RNN_HEAD_DIM)
    y = jnp.einsum("bshi,hij->bshj", xh, w)
    return y.reshape(bsz, seq, RNN_WIDTH) + b

def _lin_combine(left, right):
    a_l, u_l = left
    a_r, u_r = right
    return a_l * a_r, a_r * u_l + u_r

def _rg_lru(x, w_a, b_a, w_x, b_x, lam):
    r = jax.nn.sigmoid(_block_diag(x, w_a, b_a).astype(jnp.float32))
    i = jax.nn.sigmoid(_block_diag(x, w_x, b_x).astype(jnp.float32))
    log_a = LRU_C * r * jax.nn.log_sigmoid(lam.astype(jnp.float32))
    a = jnp.exp(log_a)
    mult = jnp.sqrt(-jnp.expm1(2.0 * log_a))
    u = mult * (i * x.astype(jnp.float32))
    _, h = lax.associative_scan(_lin_combine, (a, u), axis=1)
    return h.astype(x.dtype)

def _spatial_gating(u, v, ln_g, ln_b, w_s, b_s):
    bsz, seq, _ = v.shape
    n_blk = seq // SGU_BLOCK
    v = _layernorm(v, ln_g, ln_b)
    vb = v.reshape(bsz, n_blk, SGU_BLOCK, SGU_GROUPS, SGU_GROUP_DIM)
    mask = jnp.tril(jnp.ones((SGU_BLOCK, SGU_BLOCK), dtype=w_s.dtype))
    mixed = jnp.einsum("gts,bnsgd->bntgd", w_s * mask, vb)
    mixed = mixed + jnp.transpose(b_s)[None, None, :, :, None]
    return u * mixed.reshape(bsz, seq, SGU_WIDTH)

def setup_inputs(seed: int = 0) -> dict:
    key = jax.random.key(seed)
    ks = jax.random.split(key, 26)

    def nrm(k, shape, scale):
        return jax.random.normal(k, shape, jnp.float32) * scale

    a_c = jax.random.uniform(ks[12], (DEPTH, RNN_WIDTH), jnp.float32, 0.9, 0.999)
    s = a_c ** (1.0 / LRU_C)
    lru_lambda = jnp.log(s) - jnp.log1p(-s)

    return {
        "x": nrm(ks[0], (BATCH, SEQ, D_MODEL), 1.0),
        "c": nrm(ks[1], (BATCH, D_MODEL), 1.0),
        "w_ada": nrm(ks[2], (DEPTH, D_MODEL, N_MOD * D_MODEL), D_MODEL ** -0.5),
        "b_ada": nrm(ks[3], (DEPTH, N_MOD * D_MODEL), 0.02),
        "norm_mix_g": 1.0 + nrm(ks[4], (DEPTH, D_MODEL), 0.05),
        "w_in": nrm(ks[5], (DEPTH, D_MODEL, IN_COLS), D_MODEL ** -0.5),
        "rnn_conv_w": nrm(ks[6], (DEPTH, CONV_WIDTH, RNN_WIDTH), CONV_WIDTH ** -0.5),
        "rnn_conv_b": nrm(ks[7], (DEPTH, RNN_WIDTH), 0.02),
        "lru_w_a": nrm(ks[8], (DEPTH, RNN_HEADS, RNN_HEAD_DIM, RNN_HEAD_DIM), RNN_HEAD_DIM ** -0.5),
        "lru_b_a": nrm(ks[9], (DEPTH, RNN_WIDTH), 0.02),
        "lru_w_x": nrm(ks[10], (DEPTH, RNN_HEADS, RNN_HEAD_DIM, RNN_HEAD_DIM), RNN_HEAD_DIM ** -0.5),
        "lru_b_x": nrm(ks[11], (DEPTH, RNN_WIDTH), 0.02),
        "lru_lambda": lru_lambda,
        "sgu_ln_g": 1.0 + nrm(ks[13], (DEPTH, SGU_WIDTH), 0.05),
        "sgu_ln_b": nrm(ks[14], (DEPTH, SGU_WIDTH), 0.02),
        "sgu_w_s": nrm(ks[15], (DEPTH, SGU_GROUPS, SGU_BLOCK, SGU_BLOCK), SGU_BLOCK ** -0.5),
        "sgu_b_s": 1.0 + nrm(ks[16], (DEPTH, SGU_GROUPS, SGU_BLOCK), 0.1),
        "w_branch_a": nrm(ks[17], (DEPTH, RNN_WIDTH, D_MODEL), RNN_WIDTH ** -0.5),
        "w_branch_b": nrm(ks[18], (DEPTH, SGU_WIDTH, D_MODEL), SGU_WIDTH ** -0.5),
        "w_out": nrm(ks[19], (DEPTH, D_MODEL, D_MODEL), D_MODEL ** -0.5),
        "norm_ffn_g": 1.0 + nrm(ks[20], (DEPTH, D_MODEL), 0.05),
        "w_up": nrm(ks[21], (DEPTH, D_MODEL, 2 * D_FF), D_MODEL ** -0.5),
        "ffn_conv_w": nrm(ks[22], (DEPTH, FFN_CONV_WIDTH, 2 * D_FF), FFN_CONV_WIDTH ** -0.5),
        "ffn_conv_b": nrm(ks[23], (DEPTH, 2 * D_FF), 0.02),
        "w_down": nrm(ks[24], (DEPTH, D_FF, D_MODEL), D_FF ** -0.5),
        "norm_final_g": 1.0 + nrm(ks[25], (D_MODEL,), 0.05),
    }

def reference(x, c, w_ada, b_ada, norm_mix_g, w_in, rnn_conv_w, rnn_conv_b,
              lru_w_a, lru_b_a, lru_w_x, lru_b_x, lru_lambda,
              sgu_ln_g, sgu_ln_b, sgu_w_s, sgu_b_s,
              w_branch_a, w_branch_b, w_out,
              norm_ffn_g, w_up, ffn_conv_w, ffn_conv_b, w_down, norm_final_g):
    split_idx = [RNN_WIDTH, 2 * RNN_WIDTH, 2 * RNN_WIDTH + SGU_WIDTH,
                 2 * RNN_WIDTH + 2 * SGU_WIDTH, 2 * RNN_WIDTH + 2 * SGU_WIDTH + D_MODEL]
    c_act = jax.nn.silu(c)
    for l in range(DEPTH):
        mod = c_act @ w_ada[l] + b_ada[l]
        shift1, scale1, gate1, shift2, scale2, gate2 = jnp.split(mod, N_MOD, axis=-1)

        h = _modulated_norm(x, norm_mix_g[l], shift1, scale1)
        z = h @ w_in[l]
        xr, gr, zu, zv, ga, gb = jnp.split(z, split_idx, axis=-1)

        xr = _causal_dwconv(xr, rnn_conv_w[l], rnn_conv_b[l])
        y_a = _rg_lru(xr, lru_w_a[l], lru_b_a[l], lru_w_x[l], lru_b_x[l], lru_lambda[l])
        y_a = (y_a * jax.nn.gelu(gr)) @ w_branch_a[l]

        y_b = _spatial_gating(jax.nn.gelu(zu), jax.nn.gelu(zv), sgu_ln_g[l], sgu_ln_b[l],
                              sgu_w_s[l], sgu_b_s[l])
        y_b = y_b @ w_branch_b[l]

        merged = jax.nn.sigmoid(ga) * y_a + jax.nn.sigmoid(gb) * y_b
        x = x + gate1[:, None, :] * (merged @ w_out[l])

        h = _modulated_norm(x, norm_ffn_g[l], shift2, scale2)
        hid = _causal_dwconv(h @ w_up[l], ffn_conv_w[l], ffn_conv_b[l])
        act, val = jnp.split(hid, 2, axis=-1)
        x = x + gate2[:, None, :] * ((jax.nn.gelu(act) * val) @ w_down[l])

    return _rmsnorm(x, norm_final_g)


_drawn_inputs = setup_inputs


def setup_inputs(seed=0):
    import zlib

    import numpy as np

    out = dict(_drawn_inputs(seed))
    spreads = {}
    factors = {'lru_b_a': 38.301,
     'lru_b_x': 8.0,
     'sgu_ln_g': 6.996,
     'sgu_ln_b': 28.588,
     'ffn_conv_b': 6.072,
     'rnn_conv_b': 3.577,
     'sgu_b_s': 3.564,
     'norm_ffn_g': 2.725}
    for name, (base, spread) in spreads.items():
        noise = np.random.default_rng([zlib.crc32(name.encode()), seed]).standard_normal(out[name].shape)
        drawn = base * np.exp(spread * noise) if base else spread * noise
        out[name] = __import__('jax').numpy.asarray(drawn.astype(out[name].dtype))
    for name, factor in factors.items():
        out[name] = (out[name] * factor).astype(out[name].dtype)
    return out
```

```python
from contextlib import ExitStack

import concourse.bass as bass
from concourse import mybir

F32 = mybir.dt.float32
F32R = mybir.dt.float32r
ALU = mybir.AluOpType
ACT = mybir.ActivationFunctionType

P = 128
HALF = 512
EPS = 1e-6
LRU_C = 8.0


def build(nc, a, out):
    _, S, D = a["x"].shape
    KT = D // P
    NB = S // P
    G = a["sgu_w_s"].shape[1]
    FT = a["w_down"].shape[1] // P
    NG = FT // KT
    assert S == 2 * HALF and KT == 8 and G == KT and FT % KT == 0 and a["lru_w_a"].shape[2] == P
    CW = a["rnn_conv_w"].shape[1]
    FW = a["ffn_conv_w"].shape[1]

    N_RNN = 0
    N_MA = N_RNN + 2 * KT
    N_ZV = N_MA + 2 * KT
    N_ZU = N_ZV + KT
    N_MB = N_ZU + KT
    N_OUT = N_MB + 2 * KT
    N_FFN = N_OUT + KT
    PER_G = 3 * KT
    N_TILES = N_FFN + NG * PER_G

    ROWS = [
        [("c", KT), ("norm_mix_g", KT), ("rnn_conv_w", CW * KT), ("rnn_conv_b", KT), ("lru_b_a", KT),
         ("lru_b_x", KT), ("lru_lambda", KT), ("sgu_ln_g", KT), ("sgu_ln_b", KT), ("norm_ffn_g", KT),
         ("norm_final_g", KT)],
        [("b_ada", 6 * KT), ("ffn_conv_b", 2 * FT)],
        [("ffn_conv_w01", 4 * FT)],
        [("ffn_conv_w2", 2 * FT)],
    ]
    col = {}
    for t, rows in enumerate(ROWS):
        at = 0
        for name, n in rows:
            col[name] = t * P + at
            at += n
        assert at <= P
    row_src = {name: a[name].rearrange("a (r p) -> (a r) p", p=P) for name in
               ("c", "norm_mix_g", "rnn_conv_b", "lru_b_a", "lru_b_x", "lru_lambda", "sgu_ln_g",
                "sgu_ln_b", "norm_ffn_g", "b_ada", "ffn_conv_b")}
    row_src["norm_final_g"] = a["norm_final_g"].rearrange("(r p) -> r p", p=P)
    row_src["rnn_conv_w"] = a["rnn_conv_w"].rearrange("a w (r p) -> (a w r) p", p=P)
    fcw = a["ffn_conv_w"].rearrange("a w (r p) -> (a w r) p", p=P)
    row_src["ffn_conv_w01"] = fcw[0:4 * FT, :]
    row_src["ffn_conv_w2"] = fcw[4 * FT:6 * FT, :]

    def tiles_of(name):
        return a[name].rearrange("a (k p) c -> p (a k) c", p=P)

    w_in, w_ada, w_up, w_down = (tiles_of(x) for x in ("w_in", "w_ada", "w_up", "w_down"))
    w_pa, w_pb, w_o = (tiles_of(x) for x in ("w_branch_a", "w_branch_b", "w_out"))
    w_lru = [a[x].rearrange("a h i j -> i (a h) j") for x in ("lru_w_a", "lru_w_x")]
    w_s = a["sgu_w_s"].rearrange("a g t s -> t (a g) s")
    b_s = a["sgu_b_s"].rearrange("a g t -> a (g t)")
    x_tok = a["x"].rearrange("a (i p) d -> p (a i) d", p=P)
    out_tok = out.rearrange("a (i p) d -> p (a i) d", p=P)

    with ExitStack() as ctx:
        def sem(name):
            return ctx.enter_context(nc.semaphore(name))

        BASE = (nc.sbuf_base + 31) // 32 * 32
        KB = 1024
        TILE = 4 * S
        OFF = {}
        at = BASE
        for name, size in (("H", 8 * 2 * TILE), ("Y", 8 * 2 * TILE), ("X", 8 * TILE),
                           ("WRAW", 2 * TILE), ("WSP", 4 * TILE), ("T", 4 * TILE), ("BD", 3 * KB),
                           ("C", 4 * KB + 512)):
            OFF[name] = at
            at += size
        assert at <= nc.sbuf_usable_end, at

        def place(name, shape, dt, region, offset=0):
            return nc.alloc_sbuf_tensor_at(name, [P] + shape, dt, offset=OFF[region] + offset)

        h_split = place("h_split", [KT, 2, S], F32R, "H")
        merged_split = place("merged_split", [KT, 2, S], F32R, "H")
        hid_split = place("hid_split", [KT, 2, S], F32R, "H")
        ada_w = place("ada_w", [2 * KT, D], F32, "H")
        ya_split = place("ya_split", [KT, 2, S], F32R, "Y")
        zuv = place("zuv", [KT, 2, S], F32, "Y")
        yb_split = place("yb_split", [KT, 2, S], F32R, "Y")
        h2_split = place("h2_split", [KT, 2, S], F32R, "Y")
        xtok = place("xtok", [NB, D], F32, "Y")
        fin = place("fin", [KT, S], F32, "Y")
        otok = place("otok", [NB, D], F32, "Y", 8 * TILE)
        xT = place("xT", [KT, S], F32, "X")
        xc_split = place("xc_split", [2, S], F32R, "X")
        xc, gg, tr, ti, la_a, m2 = (place(n, [S], F32, "X", (2 + i) * TILE)
                                    for i, n in enumerate(("xc", "gg", "tr", "ti", "la_a", "m2")))
        th = place("th", [S], F32, "T")
        bd_raw = place("bd_raw", [2, P], F32, "BD")
        bd_split = place("bd_split", [2, 2, P], F32R, "BD", 2 * P * 4)
        wraw = [place(f"wraw{s}", [KT, P], F32, "WRAW", s * TILE) for s in range(2)]
        wsplit = [place(f"wsplit{s}", [2, KT, P], F32R, "WSP", 2 * s * TILE) for s in range(2)]
        q = place("q", [S], F32, "T", 3 * TILE)
        sq = place("sq", [S], F32, "T", 0)
        nt = [place(f"nt{s}", [S], F32, "T", (1 + s) * TILE) for s in range(2)]
        diag = place("diag", [NB, P], F32, "T", 0)
        prow = place("prow", [4, P], F32, "T", 1 * TILE)
        ada_acc = place("ada_acc", [D], F32, "T", 2 * TILE)
        ada_ring = [place(f"ada_ring{s}", [D], F32, "T", s * TILE) for s in range(2)]
        tg = place("tg", [S], F32, "T", 3 * TILE)
        ws_raw = place("ws_raw", [G, P], F32, "T", 1 * TILE)
        vstage = place("vstage", [G, P], F32, "T", 0)
        vhat = place("vhat", [G, P], F32, "T", 1 * TILE)
        wsT = place("wsT", [G, P], F32, "T", 2 * TILE)
        sbias = place("sbias", [G, P], F32, "T", 3 * TILE)
        ybt = [place(f"ybt{s}", [S], F32, "T", s * TILE) for s in range(2)]
        mt = place("mt", [S], F32, "T", 2 * TILE)
        ca, cb, gt = (place(n, [S], F32, "T", i * TILE) for i, n in enumerate(("ca", "cb", "gt")))

        coff = [0]

        def const(name, shape, dt=F32):
            n = 4
            for d in shape:
                n *= d
            t = place(name, shape, dt, "C", coff[0])
            coff[0] += (n + 31) // 32 * 32
            return t

        pc = const("pc", [4 * P])
        ident = const("ident", [P])
        ones = const("ones", [P])
        mod = const("mod", [6 * KT])
        s1 = const("s1", [KT])
        s2 = const("s2", [KT])
        g1h = const("g1h", [KT])
        cact = const("cact", [KT])
        hba = const("hba", [KT])
        hbx = const("hbx", [KT])
        la4 = const("la4", [KT])
        la4n = const("la4n", [KT])
        lt = const("lt", [6, KT])
        rs = const("rs", [KT])
        stats = const("stats", [2, 6])
        mv = const("mv", [2])
        sd = const("sd", [1])
        eps_t = const("eps_t", [1])
        rsd = const("rsd", [1])
        assert coff[0] <= 4 * KB + 512, coff[0]

        def C(name, i=0, n=1):
            c0 = col[name] + i
            return pc[:, c0:c0 + n] if isinstance(c0, int) else pc[:, bass.ds(c0, n)]

        ps = [ctx.enter_context(nc.psum_tensor(f"ps{i}", [P, 2, HALF], F32)) for i in range(4)]

        def flat(t):
            return t[:, :, :].rearrange("p h t -> p (h t)")

        def blocks(t):
            return t[:, :, :].rearrange("p h (b t) -> p (h b) t", t=P)

        raw_landed = [sem(f"raw_landed{s}") for s in range(2)]
        weights_hi, weights_lo, product_done = sem("weights_hi"), sem("weights_lo"), sem("product_done")
        wait_done = sem("wait_done")
        x_landed = [sem(f"x_landed{i}") for i in range(4)]
        rows_landed = sem("rows_landed")
        ada1_landed = [sem(f"ada1_landed{i}") for i in range(KT)]
        consts_made, param_T, param_col = sem("consts_made"), sem("param_T"), sem("param_col")
        vch, ach = sem("vector_step"), sem("scalar_step")
        silu_t, cact_ready, lam_e, lru_consts = (sem(x) for x in ("silu_t", "cact_ready", "lam_e", "lru_consts"))
        xT_psum, xT_ready, sq_ready, q_added = (sem(x) for x in ("xT_psum", "xT_ready", "sq_ready", "q_added"))
        ss_ready, ss_root, diag_ready, rbc_ready = (sem(x) for x in ("ss_ready", "ss_root", "diag_ready", "rbc_ready"))
        ada_sum, ada_psum, mod_ready = sem("ada_sum"), sem("ada_psum"), sem("mod_ready")
        nt_ready, norm_hi, norm_lo = sem("nt_ready"), sem("norm_hi"), sem("norm_lo")
        spilled = sem("spilled")
        bd_landed, bd_hi, bd_lo, bd_done = (sem(x) for x in ("bd_landed", "bd_hi", "bd_lo", "bd_done"))
        conv_done, xc_hi, xc_lo = sem("conv_done"), sem("xc_hi"), sem("xc_lo")
        gelu_done, gates_read, th_ready, w1_ready = (sem(x) for x in ("gelu_done", "gates_read", "th_ready", "w1_ready"))
        m2_ready, msq_ready, y_ready, ya_hi, ya_lo = (sem(x) for x in ("m2_ready", "msq_ready", "y_ready", "ya_hi", "ya_lo"))
        conv_step, tail_step, ffn_conv_step, ln_step, mb_step, g1h_ready = (
            sem(x) for x in ("conv_step", "tail_step", "ffn_conv_step", "ln_step", "mb_step", "g1h_ready"))
        tga_ready, ma_done = sem("tga_ready"), sem("ma_done")
        ring_landed = [sem(f"ring_landed{s}") for s in range(2)]
        ring_used = sem("ring_used")
        zv_ready, ws_landed, ws_masked, ws_psum, ws_ready = (sem(x) for x in ("zv_ready", "ws_landed", "ws_masked", "ws_psum", "ws_ready"))
        bs_landed, r_psum, sbias_ready = sem("bs_landed"), sem("r_psum"), sem("sbias_ready")
        staged, v_psum, var_ready, sd_ready, vhat_ready, mix_psum, mixed_ready, zu_ready = (
            sem(x) for x in ("staged", "v_psum", "var_ready", "sd_ready", "vhat_ready", "mix_psum", "mixed_ready", "zu_ready"))
        ybt_ready, yb_hi, yb_lo = sem("ybt_ready"), sem("yb_hi"), sem("yb_lo")
        tgb_ready, mb_done, mg_hi, mg_lo = (sem(x) for x in ("tgb_ready", "mb_done", "mg_hi", "mg_lo"))
        x_back = [sem(f"x_back{i}") for i in range(2)]
        x2_ready, sq2_ready, q2_added = (sem(x) for x in ("x2_ready", "sq2_ready", "q2_added"))
        ca_ready, cb_ready, ga_ready, g_ready, hid_hi, hid_lo = (
            sem(x) for x in ("ca_ready", "cb_ready", "ga_ready", "g_ready", "hid_hi", "hid_lo"))
        down_used, fin_ready, sq3_ready, q3_added = (sem(x) for x in ("down_used", "fin_ready", "sq3_ready", "q3_added"))
        o_psum, o_act, o_dve, stored = (sem(x) for x in ("o_psum", "o_act", "o_dve", "stored"))

        x_keep = nc.dram_tensor("x_keep", (P, KT, S), F32, kind="Internal").ap()

        def settled(eng):
            eng.sem_inc(wait_done, 1)

        block = ctx.enter_context(nc.Block())

        @block.sync
        def _(sp):
            def load_tile(pair, s, src):
                if not (isinstance(pair, int) and pair == 0):
                    sp.wait_ge(weights_lo, 2 * pair + s - 1)
                    settled(sp)
                sp.dma_start(wraw[s][:, :, :], src).then_inc(raw_landed[s], 16)

            def cols(w, c):
                return w[:, :, c:c + P] if isinstance(c, int) else w[:, :, bass.ds(c, P)]

            for t, rows in enumerate(ROWS):
                for name, n in rows:
                    c0 = col[name] - t * P
                    sp.dma_start(prow[c0:c0 + n, t, :], row_src[name]).then_inc(rows_landed, 16)
            for i in range(4):
                sp.dma_start(xtok[:, 2 * i:2 * i + 2, :], x_tok[:, 2 * i:2 * i + 2, :]).then_inc(x_landed[i], 16)
            for j, part in enumerate((1, 0)):
                for k in range(0, KT, 2):
                    sp.dma_start(ada_w[:, j * KT + k:j * KT + k + 2, :], w_ada[:, k:k + 2, part * D:(part + 1) * D])\
                      .then_inc(ada1_landed[j * KT // 2 + k // 2], 16)
            load_tile(0, 0, cols(w_in, 0))
            load_tile(0, 1, cols(w_in, D))
            sp.dma_start(bd_raw[:, 0, :], w_lru[0][:, 0, :]).then_inc(bd_landed, 16)
            sp.dma_start(bd_raw[:, 1, :], w_lru[1][:, 0, :]).then_inc(bd_landed, 16)
            sp.wait_ge(xT_ready, KT)
            sp.dma_start(x_keep[:, :, :], xT[:, :, :]).then_inc(spilled, 16)
            with sp.Fori(1, KT) as m:
                load_tile(m, 0, cols(w_in, m * P))
                load_tile(m, 1, cols(w_in, m * P + D))
                sp.wait_ge(bd_lo, m)
                for j in range(2):
                    sp.dma_start(bd_raw[:, j, :], w_lru[j][:, bass.ds(m, 1), :]).then_inc(bd_landed, 16)
            def merge_tile(m, s):
                load_tile(N_MA // 2 + m, s, cols(w_pa, m * P) if s else cols(w_in, m * P + 4 * D))

            def merge_part(part, last=False):
                for e in range(2):
                    if last and e == 1:
                        load_tile(N_ZV // 2, 0, cols(w_in, 3 * D))
                    else:
                        merge_tile(2 * part + e + 1, 0)
                    for k in range(4):
                        s = k % 2
                        sp.wait_ge(ring_used, 8 * part + 4 * e + k + 1)
                        sp.dma_start(ada_ring[s][:, :], w_ada[:, 4 * e + k, bass.ds((part + 2) * D, D)])\
                          .then_inc(ring_landed[s], 16)
                    if last and e == 1:
                        load_tile(N_ZV // 2, 1, cols(w_in, 3 * D + P))
                    else:
                        merge_tile(2 * part + e + 1, 1)

            merge_tile(0, 0)
            merge_tile(0, 1)
            sp.wait_ge(ya_lo, KT)
            with sp.Fori(0, KT // 2 - 1) as part:
                merge_part(part)
            merge_part(KT // 2 - 1, True)
            sp.wait_ge(mod_ready, 6)
            sp.dma_start(ws_raw[:, :, :], w_s).then_inc(ws_landed, 16)
            sp.wait_ge(ma_done, KT + 1)
            sp.dma_start(sbias[:, :, :].rearrange("p g t -> p (g t)"), b_s.to_broadcast([P, G * P]))\
              .then_inc(bs_landed, 16)
            with sp.Fori(1, KT // 2) as i:
                for s in range(2):
                    load_tile(N_ZV // 2 + i, s, cols(w_in, (2 * i + s) * P + 3 * D))
            with sp.Fori(0, KT // 2) as i:
                for s in range(2):
                    load_tile(N_ZU // 2 + i, s, cols(w_in, (2 * i + s) * P + 2 * D))
            with sp.Fori(0, KT) as m:
                load_tile(N_MB // 2 + m, 0, cols(w_in, m * P + 5 * D))
                load_tile(N_MB // 2 + m, 1, cols(w_pb, m * P))
            load_tile(N_OUT // 2, 0, cols(w_o, 0))
            load_tile(N_OUT // 2, 1, cols(w_o, P))
            sp.wait_ge(spilled, 16)
            for i in range(2):
                sp.wait_ge(mg_lo, (i + 1) * KT // 2)
                sp.dma_start(xT[:, i * KT // 2:(i + 1) * KT // 2, :], x_keep[:, i * KT // 2:(i + 1) * KT // 2, :])\
                  .then_inc(x_back[i], 16)
            with sp.Fori(1, KT // 2) as i:
                for s in range(2):
                    load_tile(N_OUT // 2 + i, s, cols(w_o, (2 * i + s) * P))
            with sp.Fori(0, NG) as g:
                with sp.Fori(0, KT) as j:
                    for s in range(2):
                        load_tile(N_FFN // 2 + PER_G // 2 * g + j, s, cols(w_up, g * KT * P + j * P + s * FT * P))
                with sp.Fori(0, KT // 2) as i:
                    for s in range(2):
                        load_tile(N_FFN // 2 + PER_G // 2 * g + KT + i, s,
                                  w_down[:, bass.ds(KT * g, KT), bass.ds((2 * i + s) * P, P)])
            for i in range(NB):
                if i % 2 == 0:
                    sp.wait_ge(o_act, i // 2 + 1)
                else:
                    sp.wait_ge(o_dve, i // 2 + 1)
                sp.dma_start(out_tok[:, i, :], otok[:, i, :]).then_inc(stored, 16)
            sp.wait_ge(stored, 16 * NB)

        @block.gpsimd
        def _(pool):
            nc.gpsimd.memset(ident[:, :], 0.0).then_inc(consts_made, 1)
            pool.wait_ge(consts_made, 1)
            nc.gpsimd.affine_select(out=ident[:, :], in_=ident[:, :], compare_op=ALU.not_equal, fill=1.0, base=0,
                                    pattern=[[-1, P]], channel_multiplier=1).then_inc(consts_made, 1)
            nc.gpsimd.memset(ones[:, :], 1.0).then_inc(consts_made, 1)
            pool.wait_ge(ws_landed, 16)
            nc.gpsimd.affine_select(out=ws_raw[:, :, :], in_=ws_raw[:, :, :], compare_op=ALU.is_ge, fill=0.0, base=0,
                                    pattern=[[0, G], [-1, P]], channel_multiplier=1).then_inc(ws_masked, 1)

        @block.tensor
        def _(pe):
            def product(pair, s, psum, acts, k_sem=None, k_base=0):
                pe.wait_ge(weights_lo, 2 * pair + s + 1)
                for k in range(KT):
                    if k_sem is not None:
                        pe.wait_ge(k_sem, k_base + k + 1)
                    for w, x in ((0, 0), (0, 1), (1, 0)):
                        for h in range(2):
                            last = nc.tensor.matmul(
                                psum[:, h, :], wsplit[s][:, w, k, :], acts[:, k, x, h * HALF:(h + 1) * HALF],
                                start=(k == 0 and w == 0 and x == 0), stop=(k == KT - 1 and w == 1))
                last.then_inc(product_done, 1)

            def column_sums(src, n, psum):
                for j in range(n):
                    last = nc.tensor.matmul(psum[:, 0, j:j + 1], src[:, j * P:(j + 1) * P], ones[:, 0:1],
                                            start=True, stop=True)
                return last

            def norm_scale(count, counter_sem, counter):
                pe.wait_ge(counter_sem, counter)
                column_sums(q, NB, ps[2]).then_inc(ss_ready, 1)
                pe.wait_ge(diag_ready, count)
                for h in range(2):
                    last = nc.tensor.matmul(ps[3][:, h, :], ones[:, :],
                                            diag[:, 4 * h:4 * h + 4, :].rearrange("p b t -> p (b t)"),
                                            start=True, stop=True)
                last.then_inc(rbc_ready, 1)

            pe.wait_ge(consts_made, 3)
            pe.wait_ge(rows_landed, 16 * sum(len(r) for r in ROWS))
            for t in range(4):
                n = sum(n for _, n in ROWS[t])
                last = nc.tensor.transpose(ps[3][:, 0, t * P:t * P + n], prow[0:n, t, :], ident[0:n, 0:n])
            last.then_inc(param_T, 1)
            for m in range(KT):
                if m >= 2:
                    pe.wait_ge(xT_ready, m - 1)
                    pe.wait_ge(sq_ready, m - 1)
                for i in range(NB):
                    if m == 0:
                        pe.wait_ge(x_landed[i // 2], 16)
                    last = nc.tensor.transpose(blocks(ps[m % 2])[:, i, :], xtok[:, i, m * P:(m + 1) * P], ident[:, :])
                last.then_inc(xT_psum, 1)
            pe.wait_ge(param_col, 4)
            norm_scale(1, q_added, KT)
            for j in range(2):
                pe.wait_ge(ada_sum, j + 1)
                if j:
                    pe.wait_ge(mod_ready, j)
                else:
                    pe.wait_ge(ss_root, 1)
                column_sums(ada_acc, KT, ps[2]).then_inc(ada_psum, 1)

            def rnn(m, first=False):
                if not first:
                    pe.wait_ge(conv_done, m)
                product(m, 0, ps[0], h_split, norm_lo if first else None)
                if not first:
                    pe.wait_ge(gelu_done, m)
                product(m, 1, ps[1], h_split)
                pe.wait_ge(xc_lo, m + 1)
                pe.wait_ge(bd_lo, m + 1)
                if first:
                    pe.wait_ge(mod_ready, 2)
                    pe.wait_ge(norm_lo, KT)
                else:
                    pe.wait_ge(gates_read, 2 * m)
                for j in range(2):
                    for w, x in ((0, 0), (0, 1), (1, 0)):
                        for h in range(2):
                            last = nc.tensor.matmul(ps[2 + j][:, h, :], bd_split[:, w, j, :],
                                                    xc_split[:, x, h * HALF:(h + 1) * HALF],
                                                    start=(w == 0 and x == 0), stop=(w == 1))
                    last.then_inc(bd_done, 1)

            rnn(0, True)
            with pe.Fori(1, KT) as m:
                rnn(m)
            with pe.Fori(0, KT // 2) as part:
                for e in range(2):
                    pair = N_MA // 2 + 2 * part + e
                    pe.wait_ge(conv_done, KT)
                    pe.wait_ge(tga_ready, 2 * part + e + 1)
                    product(pair, 0, ps[0], h_split)
                    pe.wait_ge(gelu_done, KT)
                    pe.wait_ge(ma_done, 2 * part + e + 1)
                    product(pair, 1, ps[1], ya_split, ya_lo)
                pe.wait_ge(gates_read, 2 * KT)
                pe.wait_ge(mod_ready, part + 2)
                pe.wait_ge(ada_sum, part + 3)
                column_sums(ada_acc, KT, ps[2]).then_inc(ada_psum, 1)

            def zv(i):
                for s in range(2):
                    pe.wait_ge(zv_ready, 2 * i + s - 1)
                    product(N_ZV // 2 + i, s, ps[s], h_split)

            pe.wait_ge(tga_ready, KT + 1)
            product(N_ZV // 2, 0, ps[0], h_split)
            pe.wait_ge(ma_done, KT + 1)
            product(N_ZV // 2, 1, ps[1], h_split)
            pe.wait_ge(mod_ready, 6)
            pe.wait_ge(ws_masked, 1)
            for g in range(G):
                last = nc.tensor.transpose(blocks(ps[2])[:, g, :], ws_raw[:, g, :], ident[:, :])
            last.then_inc(ws_psum, 1)
            zv(1)
            pe.wait_ge(ws_ready, 1)
            for h in range(2):
                last = nc.tensor.matmul(ps[3][:, h, :], ones[:, :],
                                        wsT[:, 4 * h:4 * h + 4, :].rearrange("p g t -> p (g t)"), start=True, stop=True)
            last.then_inc(r_psum, 1)
            with pe.Fori(2, KT // 2) as i:
                zv(i)

            def zu(i, first=False):
                for s in range(2):
                    b = 2 * i + s
                    pe.wait_ge(staged, b + 1)
                    if not (first and s == 0):
                        pe.wait_ge(vhat_ready, b)
                    for g in range(G):
                        last = nc.tensor.transpose(blocks(ps[2])[:, g, :], vstage[:, g, :], ident[:, :])
                    last.then_inc(v_psum, 1)
                    if first:
                        pe.wait_ge(zv_ready, KT - 1 + s)
                    else:
                        pe.wait_ge(zu_ready, b - 1)
                    product(N_ZU // 2 + i, s, ps[s], h_split)
                    pe.wait_ge(vhat_ready, b + 1)
                    if first and s == 0:
                        pe.wait_ge(sbias_ready, 1)
                    else:
                        pe.wait_ge(mixed_ready, b)
                    for g in range(G):
                        last = nc.tensor.matmul(blocks(ps[3])[:, g, :], vhat[:, g, :], wsT[:, g, :],
                                                start=True, stop=True)
                    last.then_inc(mix_psum, 1)

            zu(0, True)
            with pe.Fori(1, KT // 2) as i:
                zu(i)

            pe.wait_ge(zu_ready, KT)
            with pe.Fori(0, KT) as m:
                pe.wait_ge(tgb_ready, m + 1)
                product(N_MB // 2 + m, 0, ps[0], h_split)
                pe.wait_ge(mb_done, m + 1)
                product(N_MB // 2 + m, 1, ps[1], yb_split, yb_lo)

            def proj(i, first=False):
                for s in range(2):
                    if first:
                        pe.wait_ge(tgb_ready if s == 0 else mb_done, KT + 1)
                    else:
                        pe.wait_ge(x2_ready, 2 * i + s - 1)
                    product(N_OUT // 2 + i, s, ps[s], merged_split, mg_lo)

            proj(0, True)
            with pe.Fori(1, KT // 2) as i:
                proj(i)
            pe.wait_ge(mixed_ready, KT)
            norm_scale(2, q2_added, KT)

            def ups(g, first=False):
                def pair(j, head):
                    f = KT * g + j
                    n2 = N_FFN // 2 + PER_G // 2 * g + j
                    if head and first:
                        pe.wait_ge(x2_ready, KT)
                    else:
                        pe.wait_ge(ca_ready, f)
                    product(n2, 0, ps[0], h2_split, norm_lo if head and first else None, KT)
                    if not (head and first):
                        pe.wait_ge(cb_ready, f)
                    product(n2, 1, ps[1], h2_split)

                pair(0, True)
                with pe.Fori(1, KT) as j:
                    pair(j, False)

            def downs(g):
                with pe.Fori(0, KT // 2) as i:
                    for s in range(2):
                        pe.wait_ge(down_used, KT * g + 2 * i + s + 1)
                        product(N_FFN // 2 + PER_G // 2 * g + KT + i, s, ps[2 + s], hid_split, hid_lo, KT * g)

            ups(0, True)
            pe.wait_ge(norm_lo, 2 * KT)
            downs(0)
            with pe.Fori(1, NG) as g:
                ups(g)
                downs(g)

            pe.wait_ge(down_used, KT * NG + 2)
            pe.wait_ge(q3_added, KT)
            column_sums(q, NB, ps[2]).then_inc(ss_ready, 1)
            pe.wait_ge(ca_ready, FT)
            pe.wait_ge(cb_ready, FT)
            pe.wait_ge(fin_ready, KT)
            for i in range(NB):
                if i >= 3:
                    before = i - 3
                    pe.wait_ge(o_act if before % 2 == 0 else o_dve, before // 2 + 1)
                for m in range(KT):
                    last = nc.tensor.transpose(blocks(ps[(3, 0, 1)[i % 3]])[:, m, :], fin[:, m, i * P:(i + 1) * P],
                                               ident[:, :])
                last.then_inc(o_psum, 1)

        @block.scalar
        def _(act):
            def split_hi(pair, s):
                act.wait_ge(raw_landed[s], 16 * pair + 16)
                if not (isinstance(pair, int) and pair == 0):
                    act.wait_ge(product_done, 2 * pair + s - 1)
                nc.scalar.activation(wsplit[s][:, 0, :, :], wraw[s][:, :, :], ACT.Copy).then_inc(weights_hi, 1)

            def norm_part(count, shift):
                act.wait_ge(ss_ready, count)
                nc.scalar.activation(rs[:, :], ps[2][:, 0, 0:NB], ACT.Sqrt, bias=epsc, scale=1.0 / D).then_inc(ss_root, 1)
                if count == 1:
                    split_hi(0, 0)
                    split_hi(0, 1)
                    act.wait_ge(bd_landed, 32)
                    nc.scalar.activation(bd_split[:, 0, :, :], bd_raw[:, :, :], ACT.Copy).then_inc(bd_hi, 1)
                    act.wait_ge(mod_ready, 2)
                for k in range(KT):
                    act.wait_ge(nt_ready, KT * (count - 1) + k + 1)
                    nc.scalar.activation((h_split if count == 1 else h2_split)[:, k, 0, :], nt[k % 2][:, :], ACT.Identity,
                                         bias=mod[:, shift * KT + k:shift * KT + k + 1]).then_inc(norm_hi, 1)

            epsc = eps_t[:, 0:1]
            act.wait_ge(param_T, 1)
            for t in range(4):
                n = sum(n for _, n in ROWS[t])
                nc.scalar.activation(pc[:, t * P:t * P + n], ps[3][:, 0, t * P:t * P + n], ACT.Copy)\
                    .then_inc(param_col, 1)
            act.wait_ge(param_col, 4)
            nc.scalar.activation(cact[:, :], C("c", 0, KT), ACT.Tanh, scale=0.5).then_inc(silu_t, 1)
            act.wait_ge(lam_e, 1)
            nc.scalar.activation(lt[:, 1, :], lt[:, 0, :], ACT.Exp, scale=-1.0).then_inc(lam_e, 1)
            for m in range(KT):
                act.wait_ge(xT_psum, m + 1)
                nc.scalar.activation(xT[:, m, :], flat(ps[m % 2]), ACT.Copy).then_inc(xT_ready, 1)
                if m >= 1:
                    act.wait_ge(q_added, m)
                nc.scalar.activation(sq[:, :], flat(ps[m % 2]), ACT.Square).then_inc(sq_ready, 1)
            norm_part(1, 0)
            act.wait_ge(lru_consts, 4)
            act.wait_ge(spilled, 16)

            def gates(m, first):
                act.wait_ge(bd_done, 2 * m + 1)
                nc.scalar.activation(tr[:, :], flat(ps[2]), ACT.Tanh, bias=hba[:, bass.ds(m, 1)], scale=0.5)\
                    .then_inc(gates_read, 1)
                act.wait_ge(bd_done, 2 * m + 2)
                if not first:
                    act.wait_ge(ya_lo, m)
                nc.scalar.activation(ti[:, :], flat(ps[3]), ACT.Tanh, bias=hbx[:, bass.ds(m, 1)], scale=0.5)\
                    .then_inc(gates_read, 1)
                act.wait_ge(gates_read, 2 * m + 1)
                nc.scalar.activation(th[:, :], tr[:, :], ACT.Tanh, bias=la4n[:, bass.ds(m, 1)],
                                     scale=la4n[:, bass.ds(m, 1)]).then_inc(ach, 1)
                nc.scalar.activation(la_a[:, :], tr[:, :], ACT.Exp, bias=la4[:, bass.ds(m, 1)],
                                     scale=la4[:, bass.ds(m, 1)]).then_inc(ach, 1)
                act.wait_ge(ach, 2 * m + 2)
                nc.scalar.activation(m2[:, :], la_a[:, :], ACT.Square).then_inc(th_ready, 1)
                act.wait_ge(m2_ready, m + 1)
                nc.scalar.activation(m2[:, :], m2[:, :], ACT.Sqrt, scale=0.25).then_inc(msq_ready, 1)

            def store_ya_hi(m):
                act.wait_ge(y_ready, m + 1)
                nc.scalar.activation(ya_split[:, bass.ds(m, 1), 0, :], ti[:, :], ACT.Copy).then_inc(ya_hi, 1)

            def rnn(m, first=False):
                split_hi(m + 1, 0)
                act.wait_ge(conv_done, m + 1)
                nc.scalar.activation(xc_split[:, 0, :], xc[:, :], ACT.Copy).then_inc(xc_hi, 1)
                if not first:
                    store_ya_hi(m - 1)
                split_hi(m + 1, 1)
                if not first:
                    act.wait_ge(y_ready, m)
                nc.scalar.activation(gg[:, :], flat(ps[1]), ACT.Gelu_apprx_tanh).then_inc(gelu_done, 1)
                gates(m, first)

            rnn(0, True)

            def bd_next(m):
                act.wait_ge(bd_landed, 32 * m + 32)
                act.wait_ge(bd_done, 2 * m)
                nc.scalar.activation(bd_split[:, 0, :, :], bd_raw[:, :, :], ACT.Copy).then_inc(bd_hi, 1)

            with act.Fori(1, KT) as m:
                bd_next(m)
                rnn(m)
            store_ya_hi(KT - 1)

            act.wait_ge(ya_lo, KT)
            act.sem_inc(tga_ready, 1)
            with act.Fori(0, KT) as m:
                n2 = N_MA // 2 + m
                split_hi(n2 + 1, 0)
                act.wait_ge(ma_done, m + 1)
                nc.scalar.activation(tg[:, :], flat(ps[0]), ACT.Tanh, scale=0.5).then_inc(tga_ready, 1)
                split_hi(n2 + 1, 1)

            def zv(i):
                for s in range(2):
                    split_hi(N_ZV // 2 + i + 1, s)
                    nc.scalar.activation(zuv[:, bass.ds(2 * i + s, 1), 1, :], flat(ps[s]), ACT.Gelu_apprx_tanh)\
                        .then_inc(zv_ready, 1)

            zv(0)
            act.wait_ge(ws_psum, 1)
            nc.scalar.activation(wsT[:, :, :], blocks(ps[2]), ACT.Copy).then_inc(ws_ready, 1)
            with act.Fori(1, KT // 2) as i:
                zv(i)
            act.wait_ge(zv_ready, KT)

            def stage(b):
                nc.scalar.activation(vstage[:, :, :], zuv[:, :, 1, bass.ds(b * P, P)], ACT.Copy).then_inc(staged, 1)

            stage(0)

            def zu(i, last=False):
                for s in range(2):
                    b = 2 * i + s
                    act.wait_ge(var_ready, b + 1)
                    nc.scalar.activation(sd[:, :], mv[:, 1:2], ACT.Sqrt, bias=epsc).then_inc(sd_ready, 1)
                    if not (last and s == 1):
                        act.wait_ge(v_psum, b + 1)
                        stage(b + 1)
                    split_hi(N_ZU // 2 + i + 1, s)
                    nc.scalar.activation(zuv[:, bass.ds(b, 1), 0, :], flat(ps[s]), ACT.Gelu_apprx_tanh)\
                        .then_inc(zu_ready, 1)

            with act.Fori(0, KT // 2 - 1) as i:
                zu(i)
            zu(KT // 2 - 1, True)

            def yb_part(m):
                act.wait_ge(ybt_ready, m + 1)
                nc.scalar.activation(yb_split[:, m, 0, :], ybt[m % 2][:, :], ACT.Copy).then_inc(yb_hi, 1)

            act.sem_inc(tgb_ready, 1)
            for m in range(4):
                yb_part(m)
            split_hi(N_MB // 2 + 1, 0)
            for m in range(4, KT):
                yb_part(m)

            def merge_b(m, first=False):
                n2 = N_MB // 2 + m
                if not first:
                    split_hi(n2 + 1, 0)
                    act.wait_ge(mb_done, m + 1)
                nc.scalar.activation(tg[:, :], flat(ps[0]), ACT.Tanh, scale=0.5).then_inc(tgb_ready, 1)
                split_hi(n2 + 1, 1)

            merge_b(0, True)
            with act.Fori(1, KT - 1) as m:
                merge_b(m)

            def merged_hi(m):
                nc.scalar.activation(merged_split[:, m, 0, :], xT[:, m, :], ACT.Copy).then_inc(mg_hi, 1)

            m = KT - 1
            split_hi(N_MB // 2 + m + 1, 0)
            act.wait_ge(mb_done, m + 1)
            nc.scalar.activation(tg[:, :], flat(ps[0]), ACT.Tanh, scale=0.5).then_inc(tgb_ready, 1)
            for k in range(KT - 1):
                merged_hi(k)
            split_hi(N_MB // 2 + m + 1, 1)
            act.wait_ge(mb_done, KT + 1)
            merged_hi(KT - 1)

            def proj(i, first=False):
                for s in range(2):
                    split_hi(N_OUT // 2 + i + 1, s)
                    m = 2 * i + s
                    act.wait_ge(x2_ready, m + 1)
                    if not (first and s == 0):
                        act.wait_ge(q2_added, m)
                    nc.scalar.activation(sq[:, :], xT[:, bass.ds(m, 1), :], ACT.Square).then_inc(sq2_ready, 1)

            proj(0, True)
            with act.Fori(1, KT // 2) as i:
                proj(i)
            norm_part(2, 3)

            def ups(g):
                with act.Fori(0, KT) as j:
                    f = KT * g + j
                    n2 = N_FFN // 2 + PER_G // 2 * g + j
                    split_hi(n2 + 1, 0)
                    act.wait_ge(ca_ready, f + 1)
                    nc.scalar.activation(ca[:, :], ca[:, :], ACT.Gelu_apprx_tanh).then_inc(ga_ready, 1)
                    split_hi(n2 + 1, 1)
                    act.wait_ge(g_ready, f + 1)
                    nc.scalar.activation(hid_split[:, bass.ds(j, 1), 0, :], gt[:, :], ACT.Copy).then_inc(hid_hi, 1)

            def downs(g):
                with act.Fori(0, KT // 2) as i:
                    for s in range(2):
                        split_hi(N_FFN // 2 + PER_G // 2 * g + KT + i + 1, s)

            with act.Fori(0, NG - 1) as g:
                ups(g)
                downs(g)
            ups(NG - 1)

            def last_down(i, split, first=False):
                for s in range(2):
                    m = 2 * i + s
                    if split:
                        split_hi(N_TILES // 2 - KT // 2 + i + 1, s)
                    act.wait_ge(down_used, KT * (NG - 1) + m + 3)
                    nc.scalar.activation(fin[:, bass.ds(m, 1), :], xT[:, bass.ds(m, 1), :], ACT.Identity,
                                         scale=C("norm_final_g", m)).then_inc(fin_ready, 1)
                    if not (first and s == 0):
                        act.wait_ge(q3_added, m)
                        settled(act)
                    nc.scalar.activation(sq[:, :], xT[:, bass.ds(m, 1), :], ACT.Square).then_inc(sq3_ready, 1)

            last_down(0, True, True)
            with act.Fori(1, KT // 2 - 1) as i:
                last_down(i, True)
            last_down(KT // 2 - 1, False)
            act.wait_ge(ss_ready, 3)
            nc.scalar.activation(rs[:, :], ps[2][:, 0, 0:NB], ACT.Sqrt, bias=epsc, scale=1.0 / D).then_inc(ss_root, 1)
            act.wait_ge(diag_ready, 3)
            for i in range(0, NB, 2):
                act.wait_ge(o_psum, i + 1)
                nc.scalar.activation(otok[:, i, :], flat(ps[(3, 0, 1)[i % 3]]), ACT.Identity,
                                     scale=rs[:, i:i + 1]).then_inc(o_act, 1)

        @block.vector
        def _(dve):
            V = nc.vector
            steps = [0]

            def step(ins):
                steps[0] += 1
                ins.then_inc(vch, 1)
                dve.wait_ge(vch, steps[0])

            def split_lo(pair, s):
                dve.wait_ge(weights_hi, 2 * pair + s + 1)
                V.tensor_tensor(wsplit[s][:, 1, :, :], wraw[s][:, :, :], wsplit[s][:, 0, :, :].bitcast(F32),
                                ALU.subtract).then_inc(weights_lo, 1)

            def bd_next(m):
                dve.wait_ge(bd_hi, m + 1)
                V.tensor_tensor(bd_split[:, 1, :, :], bd_raw[:, :, :], bd_split[:, 0, :, :].bitcast(F32),
                                ALU.subtract).then_inc(bd_lo, 1)

            def ada_piece(w, k, first):
                if first:
                    return V.tensor_scalar(ada_acc[:, :], w, cact[:, k:k + 1], None, ALU.mult)
                return V.scalar_tensor_tensor(ada_acc[:, :], w, cact[:, k:k + 1], ada_acc[:, :], ALU.mult, ALU.add)

            def mod_part(part, count):
                dve.wait_ge(ada_psum, count)
                dst = mod[:, part * KT:(part + 1) * KT] if isinstance(part, int) else mod[:, bass.ds(part * KT, KT)]
                V.tensor_tensor(dst, ps[2][:, 0, 0:KT], C("b_ada", part * KT, KT), ALU.add).then_inc(mod_ready, 1)

            def root_to_diag(count):
                dve.wait_ge(ss_root, count)
                step(V.reciprocal(rs[:, :], rs[:, :]))

            def norm_part(count, src, dst, scale, shift):
                root_to_diag(count)
                for i in range(NB):
                    last = V.tensor_scalar(diag[:, i, :], ident[:, :], rs[:, i:i + 1], None, ALU.mult)
                last.then_inc(diag_ready, 1)
                dve.wait_ge(rbc_ready, count)
                if count == 1:
                    for j in range(2):
                        for k in range(KT):
                            dve.wait_ge(ada1_landed[j * KT // 2 + k // 2], 16)
                            if k == 0 and j == 1:
                                dve.wait_ge(ada_psum, 1)
                            ins = ada_piece(ada_w[:, j * KT + k, :], k, k == 0)
                            if k < KT - 1:
                                step(ins)
                        ins.then_inc(ada_sum, 1)
                        mod_part(1 - j, j + 1)
                    dve.wait_ge(mod_ready, 2)
                    bd_next(0)
                    split_lo(0, 0)
                    split_lo(0, 1)
                part = 1 if count == 1 else 4
                g = C("norm_mix_g" if count == 1 else "norm_ffn_g", 0, KT)
                step(V.scalar_tensor_tensor(scale[:, :], mod[:, part * KT:(part + 1) * KT], 1.0, g, ALU.add, ALU.mult))
                for k in range(KT + 1):
                    if k < KT:
                        if k >= 2:
                            dve.wait_ge(norm_lo, KT * (count - 1) + k - 1)
                        V.scalar_tensor_tensor(nt[k % 2][:, :], src[:, k, :], scale[:, k:k + 1], flat(ps[3]),
                                               ALU.mult, ALU.mult).then_inc(nt_ready, 1)
                    if k:
                        dve.wait_ge(norm_hi, KT * (count - 1) + k)
                        V.scalar_tensor_tensor(dst[:, k - 1, 1, :], nt[(k - 1) % 2][:, :],
                                               mod[:, shift * KT + k - 1:shift * KT + k], dst[:, k - 1, 0, :].bitcast(F32),
                                               ALU.add, ALU.subtract).then_inc(norm_lo, 1)

            V.memset(eps_t[:, :], EPS).then_inc(vch, 1)
            steps[0] += 1
            dve.wait_ge(silu_t, 1)
            step(V.tensor_scalar(cact[:, :], cact[:, :], 1.0, 0.5, ALU.add, ALU.mult))
            step(V.tensor_tensor(cact[:, :], cact[:, :], C("c", 0, KT), ALU.mult))
            lam = C("lru_lambda", 0, KT)
            step(V.tensor_scalar(lt[:, 2, :], lam, -1.0, None, ALU.mult))
            V.tensor_tensor(lt[:, 0, :], lt[:, 2, :], lam, ALU.max).then_inc(lam_e, 1)
            dve.wait_ge(lam_e, 2)
            step(V.tensor_scalar(lt[:, 2, :], lt[:, 1, :], 2.0, None, ALU.add))
            step(V.reciprocal(lt[:, 2, :], lt[:, 2, :]))
            step(V.tensor_tensor(lt[:, 1, :], lt[:, 1, :], lt[:, 2, :], ALU.mult))
            step(V.tensor_tensor(lt[:, 2, :], lt[:, 1, :], lt[:, 1, :], ALU.mult))
            TERMS = 9
            step(V.tensor_scalar(lt[:, 3, :], lt[:, 2, :], 1.0 / (2 * TERMS + 1), 1.0 / (2 * TERMS - 1), ALU.mult, ALU.add))
            for j in range(TERMS - 2, -1, -1):
                step(V.tensor_tensor(lt[:, 3, :], lt[:, 3, :], lt[:, 2, :], ALU.mult))
                step(V.tensor_scalar(lt[:, 3, :], lt[:, 3, :], 1.0 / (2 * j + 1), None, ALU.add))
            step(V.tensor_tensor(lt[:, 3, :], lt[:, 3, :], lt[:, 1, :], ALU.mult))
            step(V.tensor_scalar(lt[:, 4, :], lam, 0.0, None, ALU.min))
            step(V.scalar_tensor_tensor(lt[:, 4, :], lt[:, 3, :], -2.0, lt[:, 4, :], ALU.mult, ALU.add))
            V.tensor_scalar(la4[:, :], lt[:, 4, :], LRU_C / 2, None, ALU.mult).then_inc(lru_consts, 1)
            V.tensor_scalar(la4n[:, :], lt[:, 4, :], -LRU_C / 2, None, ALU.mult).then_inc(lru_consts, 1)
            V.tensor_scalar(hba[:, :], C("lru_b_a", 0, KT), 0.5, None, ALU.mult).then_inc(lru_consts, 1)
            V.tensor_scalar(hbx[:, :], C("lru_b_x", 0, KT), 0.5, None, ALU.mult).then_inc(lru_consts, 1)

            def add_square(sem_ready, sem_added, m, first):
                dve.wait_ge(sem_ready, m + 1)
                if first:
                    V.tensor_copy(q[:, :], sq[:, :]).then_inc(sem_added, 1)
                else:
                    dve.wait_ge(sem_added, m)
                    V.tensor_tensor(q[:, :], q[:, :], sq[:, :], ALU.add).then_inc(sem_added, 1)

            for m in range(KT):
                add_square(sq_ready, q_added, m, m == 0)
            norm_part(1, xT, h_split, s1, 0)
            dve.wait_ge(spilled, 16)

            def conv(dst, src, width, taps, bias, step_sem, before, done):
                ins = V.tensor_scalar(dst[:, :], flat(src), taps(width - 1), bias, ALU.mult, ALU.add)
                for d in range(1, width):
                    ins.then_inc(step_sem, 1)
                    dve.wait_ge(step_sem, before + d)
                    ins = V.scalar_tensor_tensor(dst[:, d:S], flat(src)[:, 0:S - d], taps(width - 1 - d), dst[:, d:S],
                                                 ALU.mult, ALU.add)
                ins.then_inc(done, 1)

            def rnn_tail(m):
                dve.wait_ge(w1_ready, m + 1)
                dve.wait_ge(msq_ready, m + 1)
                V.tensor_tensor(ti[:, :], ti[:, :], m2[:, :], ALU.mult).then_inc(tail_step, 1)
                dve.wait_ge(tail_step, 2 * m + 1)
                V.tensor_tensor_scan(ti[:, :], la_a[:, :], ti[:, :], 0.0, ALU.mult, ALU.add).then_inc(tail_step, 1)
                dve.wait_ge(tail_step, 2 * m + 2)
                V.tensor_tensor(ti[:, :], ti[:, :], gg[:, :], ALU.mult).then_inc(y_ready, 1)

            def ya_part(m):
                dve.wait_ge(ya_hi, m + 1)
                V.tensor_tensor(ya_split[:, bass.ds(m, 1), 1, :], ti[:, :], ya_split[:, bass.ds(m, 1), 0, :].bitcast(F32),
                                ALU.subtract).then_inc(ya_lo, 1)

            def rnn(m, first=False):
                split_lo(m + 1, 0)
                dve.wait_ge(product_done, 2 * m + 1)
                if not first:
                    dve.wait_ge(w1_ready, m)
                conv(xc, ps[0], CW, lambda k: C("rnn_conv_w", k * KT + m), C("rnn_conv_b", m),
                     conv_step, (CW - 1) * m, conv_done)
                dve.wait_ge(xc_hi, m + 1)
                V.tensor_tensor(xc_split[:, 1, :], xc[:, :], xc_split[:, 0, :].bitcast(F32), ALU.subtract)\
                 .then_inc(xc_lo, 1)
                if not first:
                    rnn_tail(m - 1)
                    ya_part(m - 1)
                split_lo(m + 1, 1)
                dve.wait_ge(th_ready, m + 1)
                V.scalar_tensor_tensor(m2[:, :], m2[:, :], 1.0, th[:, :], ALU.add, ALU.mult).then_inc(m2_ready, 1)
                dve.wait_ge(gates_read, 2 * m + 2)
                V.scalar_tensor_tensor(ti[:, :], ti[:, :], 1.0, xc[:, :], ALU.add, ALU.mult).then_inc(w1_ready, 1)

            rnn(0, True)
            with dve.Fori(1, KT) as m:
                bd_next(m)
                rnn(m)
            rnn_tail(KT - 1)
            ya_part(KT - 1)

            dve.sem_inc(ma_done, 1)
            dve.sem_inc(ring_used, 2)
            with dve.Fori(0, KT // 2) as part:
                for e in range(2):
                    m = 2 * part + e
                    n2 = N_MA // 2 + m
                    split_lo(n2 + 1, 0)
                    for k in range(4):
                        kk = 4 * e + k
                        dve.wait_ge(ring_landed[k % 2], 64 * part + 32 * e + 16 * (k // 2) + 16)
                        if kk == 0:
                            dve.wait_ge(ada_psum, part + 2)
                        else:
                            dve.wait_ge(ring_used, 8 * part + kk + 2)
                        ins = ada_piece(ada_ring[k % 2][:, :], kk, kk == 0)
                        ins.then_inc(ring_used, 1)
                    if e == 1:
                        dve.wait_ge(ring_used, 8 * part + 10)
                        dve.sem_inc(ada_sum, 1)
                    split_lo(n2 + 1, 1)
                    dve.wait_ge(tga_ready, m + 2)
                    V.scalar_tensor_tensor(xT[:, bass.ds(m, 1), :], tg[:, :], 1.0, flat(ps[1]), ALU.add, ALU.mult)\
                     .then_inc(ma_done, 1)
                mod_part(part + 2, part + 3)
            dve.wait_ge(mod_ready, 6)
            V.tensor_scalar(g1h[:, :], mod[:, 2 * KT:3 * KT], 0.5, None, ALU.mult).then_inc(g1h_ready, 1)

            for s in range(2):
                split_lo(N_ZV // 2 + 1, s)
            for s in range(2):
                split_lo(N_ZV // 2 + 2, s)
            dve.wait_ge(r_psum, 1)
            dve.wait_ge(bs_landed, 16)
            for g in range(G):
                last = V.scalar_tensor_tensor(sbias[:, g, :], blocks(ps[3])[:, g, :], C("sgu_ln_b", g), sbias[:, g, :],
                                              ALU.mult, ALU.add)
            last.then_inc(sbias_ready, 1)
            with dve.Fori(2, KT // 2) as i:
                for s in range(2):
                    split_lo(N_ZV // 2 + i + 1, s)

            def zu(i):
                for s in range(2):
                    b = 2 * i + s
                    dve.wait_ge(v_psum, b + 1)
                    for h in range(2):
                        V.bn_stats(stats[:, h, :], ps[2][:, h, :]).then_inc(ln_step, 1)
                    dve.wait_ge(ln_step, 4 * b + 2)
                    settled(dve)
                    V.bn_aggr(mv[:, :], stats[:, :, :].rearrange("p a b -> p (a b)")).then_inc(var_ready, 1)
                    dve.wait_ge(sd_ready, b + 1)
                    V.reciprocal(rsd[:, :], sd[:, :]).then_inc(ln_step, 1)
                    dve.wait_ge(ln_step, 4 * b + 3)
                    V.tensor_scalar(vhat[:, :, :], blocks(ps[2]), mv[:, 0:1], rsd[:, 0:1], ALU.subtract, ALU.mult)\
                     .then_inc(vhat_ready, 1)
                    split_lo(N_ZU // 2 + i + 1, s)
                    dve.wait_ge(mix_psum, b + 1)
                    V.tensor_tensor(blocks(ps[3]), blocks(ps[3]),
                                    pc[:, col["sgu_ln_g"]:col["sgu_ln_g"] + G].unsqueeze(2).to_broadcast([P, G, P]),
                                    ALU.mult).then_inc(ln_step, 1)
                    dve.wait_ge(ln_step, 4 * b + 4)
                    V.tensor_tensor(zuv[:, :, 1, bass.ds(b * P, P)], blocks(ps[3]), sbias[:, :, :], ALU.add)\
                     .then_inc(mixed_ready, 1)

            with dve.Fori(0, KT // 2) as i:
                zu(i)

            dve.sem_inc(mb_done, 1)
            dve.wait_ge(zu_ready, KT)
            dve.wait_ge(mixed_ready, KT)
            dve.wait_ge(ma_done, KT + 1)

            def yb_mul(m):
                if m >= 2:
                    dve.wait_ge(yb_lo, m - 1)
                V.tensor_tensor(ybt[m % 2][:, :], zuv[:, m, 0, :], zuv[:, m, 1, :], ALU.mult).then_inc(ybt_ready, 1)

            def yb_sub(m):
                dve.wait_ge(yb_hi, m + 1)
                V.tensor_tensor(yb_split[:, m, 1, :], ybt[m % 2][:, :], yb_split[:, m, 0, :].bitcast(F32), ALU.subtract)\
                 .then_inc(yb_lo, 1)

            yb_mul(0)
            for m in range(KT):
                if m + 1 < KT:
                    yb_mul(m + 1)
                yb_sub(m)
                if m == 3:
                    split_lo(N_MB // 2 + 1, 0)

            def merge_b(m):
                dve.wait_ge(tgb_ready, m + 2)
                dve.wait_ge(mb_done, m + 1)
                V.scalar_tensor_tensor(mt[:, :], tg[:, :], 1.0, flat(ps[1]), ALU.add, ALU.mult).then_inc(mb_step, 1)
                dve.wait_ge(mb_step, m + 1)
                V.tensor_tensor(xT[:, bass.ds(m, 1), :], xT[:, bass.ds(m, 1), :], mt[:, :], ALU.add).then_inc(mb_done, 1)

            split_lo(N_MB // 2 + 1, 1)
            merge_b(0)
            with dve.Fori(1, KT - 1) as m:
                split_lo(N_MB // 2 + m + 1, 0)
                split_lo(N_MB // 2 + m + 1, 1)
                merge_b(m)

            def merged_lo(m):
                dve.wait_ge(mg_hi, m + 1)
                V.tensor_tensor(merged_split[:, m, 1, :], xT[:, m, :], merged_split[:, m, 0, :].bitcast(F32),
                                ALU.subtract).then_inc(mg_lo, 1)

            m = KT - 1
            split_lo(N_MB // 2 + m + 1, 0)
            for k in range(KT - 1):
                merged_lo(k)
            split_lo(N_MB // 2 + m + 1, 1)
            merge_b(m)
            merged_lo(KT - 1)

            def proj(i, first=False):
                for s in range(2):
                    m = 2 * i + s
                    split_lo(N_OUT // 2 + i + 1, s)
                    V.scalar_tensor_tensor(xT[:, bass.ds(m, 1), :], flat(ps[s]), g1h[:, bass.ds(m, 1)],
                                           xT[:, bass.ds(m, 1), :], ALU.mult, ALU.add).then_inc(x2_ready, 1)
                    add_square(sq2_ready, q2_added, m, first and s == 0)

            dve.wait_ge(g1h_ready, 1)
            dve.wait_ge(x_back[0], 16)
            proj(0, True)
            proj(1)
            dve.wait_ge(x_back[1], 16)
            with dve.Fori(2, KT // 2) as i:
                proj(i)
            norm_part(2, xT, h2_split, s2, 3)

            dve.sem_inc(down_used, 2)

            dve.wait_ge(x2_ready, KT)

            def ups(g):
                with dve.Fori(0, KT) as j:
                    f = KT * g + j
                    n2 = N_FFN // 2 + PER_G // 2 * g + j

                    def taps(o):
                        def tap(k):
                            return C("ffn_conv_w01" if k < 2 else "ffn_conv_w2", (k % 2) * 2 * FT + o + f)
                        return tap

                    split_lo(n2 + 1, 0)
                    conv(ca, ps[0], FW, taps(0), C("ffn_conv_b", f), ffn_conv_step, 2 * (FW - 1) * f, ca_ready)
                    split_lo(n2 + 1, 1)
                    conv(cb, ps[1], FW, taps(FT), C("ffn_conv_b", f + FT), ffn_conv_step,
                         2 * (FW - 1) * f + FW - 1, cb_ready)
                    dve.wait_ge(cb_ready, f + 1)
                    dve.wait_ge(ga_ready, f + 1)
                    V.tensor_tensor(gt[:, :], ca[:, :], cb[:, :], ALU.mult).then_inc(g_ready, 1)
                    dve.wait_ge(hid_hi, f + 1)
                    V.tensor_tensor(hid_split[:, bass.ds(j, 1), 1, :], gt[:, :],
                                    hid_split[:, bass.ds(j, 1), 0, :].bitcast(F32), ALU.subtract).then_inc(hid_lo, 1)

            def down(m, s):
                V.scalar_tensor_tensor(xT[:, bass.ds(m, 1), :], flat(ps[2 + s]), mod[:, bass.ds(5 * KT + m, 1)],
                                       xT[:, bass.ds(m, 1), :], ALU.mult, ALU.add).then_inc(down_used, 1)

            with dve.Fori(0, NG - 1) as g:
                ups(g)
                dve.wait_ge(down_used, KT * g + 2)
                settled(dve)
                with dve.Fori(0, KT // 2) as i:
                    for s in range(2):
                        split_lo(N_FFN // 2 + PER_G // 2 * g + KT + i + 1, s)
                        down(2 * i + s, s)
            ups(NG - 1)
            dve.wait_ge(down_used, KT * (NG - 1) + 2)

            def last_down(i, split, first=False):
                for s in range(2):
                    m = 2 * i + s
                    n2 = N_TILES // 2 - KT // 2 + i
                    if split:
                        split_lo(n2 + 1, s)
                    else:
                        dve.wait_ge(product_done, 2 * n2 + s + 1)
                    down(m, s)
                    add_square(sq3_ready, q3_added, m, first and s == 0)

            last_down(0, True, True)
            with dve.Fori(1, KT // 2 - 1) as i:
                last_down(i, True)
            last_down(KT // 2 - 1, False)
            dve.wait_ge(ss_root, 3)
            V.reciprocal(rs[:, :], rs[:, :]).then_inc(diag_ready, 1)
            dve.wait_ge(diag_ready, 3)
            for i in range(1, NB, 2):
                dve.wait_ge(o_psum, i + 1)
                V.tensor_scalar(otok[:, i, :], flat(ps[(3, 0, 1)[i % 3]]), rs[:, i:i + 1], None, ALU.mult)\
                 .then_inc(o_dve, 1)


def kernel(**inputs):
    import numpy as np
    import concourse.bacc as bacc
    from concourse.bass_utils import run_bass_kernel_spmd

    nc = bacc.Bacc("TRN2", target_bir_lowering=False, num_devices=1)
    arrays, aps = {}, {}
    for name, value in inputs.items():
        value = np.ascontiguousarray(value)
        arrays[f"in_{name}"] = value
        aps[name] = nc.dram_tensor(f"in_{name}", value.shape, mybir.dt.from_np(value.dtype), kind="ExternalInput").ap()
    out = nc.dram_tensor("out_x", inputs["x"].shape, F32, kind="ExternalOutput").ap()
    build(nc, aps, out)
    result = run_bass_kernel_spmd(nc, [arrays], core_ids=[0])
    return result.results[0]["out_x"]
```

```python
from contextlib import ExitStack

import concourse.bass as bass
from concourse import mybir

F32 = mybir.dt.float32
F32R = mybir.dt.float32r
ALU = mybir.AluOpType
ACT = mybir.ActivationFunctionType

P = 128
HALF = 512
EPS = 1e-6
LRU_C = 8.0


def build(nc, a, out):
    _, S, D = a["x"].shape
    KT = D // P
    NB = S // P
    G = a["sgu_w_s"].shape[1]
    FT = a["w_down"].shape[1] // P
    NG = FT // KT
    assert S == 2 * HALF and KT == 8 and G == KT and FT % KT == 0 and a["lru_w_a"].shape[2] == P
    CW = a["rnn_conv_w"].shape[1]
    FW = a["ffn_conv_w"].shape[1]

    N_RNN = 0
    N_MA = N_RNN + 2 * KT
    N_ZV = N_MA + 2 * KT
    N_ZU = N_ZV + KT
    N_MB = N_ZU + KT
    N_OUT = N_MB + 2 * KT
    N_FFN = N_OUT + KT
    PER_G = 3 * KT
    N_TILES = N_FFN + NG * PER_G

    ROWS = [
        [("c", KT), ("norm_mix_g", KT), ("rnn_conv_w", CW * KT), ("rnn_conv_b", KT), ("lru_b_a", KT),
         ("lru_b_x", KT), ("lru_lambda", KT), ("sgu_ln_g", KT), ("sgu_ln_b", KT), ("norm_ffn_g", KT),
         ("norm_final_g", KT)],
        [("b_ada", 6 * KT), ("ffn_conv_b", 2 * FT)],
        [("ffn_conv_w01", 4 * FT)],
        [("ffn_conv_w2", 2 * FT)],
    ]
    col = {}
    for t, rows in enumerate(ROWS):
        at = 0
        for name, n in rows:
            col[name] = t * P + at
            at += n
        assert at <= P
    row_src = {name: a[name].rearrange("a (r p) -> (a r) p", p=P) for name in
               ("c", "norm_mix_g", "rnn_conv_b", "lru_b_a", "lru_b_x", "lru_lambda", "sgu_ln_g",
                "sgu_ln_b", "norm_ffn_g", "b_ada", "ffn_conv_b")}
    row_src["norm_final_g"] = a["norm_final_g"].rearrange("(r p) -> r p", p=P)
    row_src["rnn_conv_w"] = a["rnn_conv_w"].rearrange("a w (r p) -> (a w r) p", p=P)
    fcw = a["ffn_conv_w"].rearrange("a w (r p) -> (a w r) p", p=P)
    row_src["ffn_conv_w01"] = fcw[0:4 * FT, :]
    row_src["ffn_conv_w2"] = fcw[4 * FT:6 * FT, :]

    def tiles_of(name):
        return a[name].rearrange("a (k p) c -> p (a k) c", p=P)

    w_in, w_ada, w_up, w_down = (tiles_of(x) for x in ("w_in", "w_ada", "w_up", "w_down"))
    w_pa, w_pb, w_o = (tiles_of(x) for x in ("w_branch_a", "w_branch_b", "w_out"))
    w_lru = [a[x].rearrange("a h i j -> i (a h) j") for x in ("lru_w_a", "lru_w_x")]
    w_s = a["sgu_w_s"].rearrange("a g t s -> t (a g) s")
    b_s = a["sgu_b_s"].rearrange("a g t -> a (g t)")
    x_tok = a["x"].rearrange("a (i p) d -> p (a i) d", p=P)
    out_tok = out.rearrange("a (i p) d -> p (a i) d", p=P)

    with ExitStack() as ctx:
        def sem(name):
            return ctx.enter_context(nc.semaphore(name))

        BASE = (nc.sbuf_base + 31) // 32 * 32
        KB = 1024
        TILE = 4 * S
        OFF = {}
        at = BASE
        for name, size in (("H", 8 * 2 * TILE), ("Y", 8 * 2 * TILE), ("X", 8 * TILE),
                           ("WRAW", 2 * TILE), ("WSP", 4 * TILE), ("T", 4 * TILE), ("BD", 3 * KB),
                           ("C", 4 * KB + 512)):
            OFF[name] = at
            at += size
        assert at <= nc.sbuf_usable_end, at

        def place(name, shape, dt, region, offset=0):
            return nc.alloc_sbuf_tensor_at(name, [P] + shape, dt, offset=OFF[region] + offset)

        h_split = place("h_split", [KT, 2, S], F32R, "H")
        merged_split = place("merged_split", [KT, 2, S], F32R, "H")
        hid_split = place("hid_split", [KT, 2, S], F32R, "H")
        ada_w = place("ada_w", [2 * KT, D], F32, "H")
        ya_split = place("ya_split", [KT, 2, S], F32R, "Y")
        zuv = place("zuv", [KT, 2, S], F32, "Y")
        yb_split = place("yb_split", [KT, 2, S], F32R, "Y")
        h2_split = place("h2_split", [KT, 2, S], F32R, "Y")
        xtok = place("xtok", [NB, D], F32, "Y")
        tn = place("tn", [KT, S], F32, "Y", 8 * TILE)
        fin = place("fin", [KT, S], F32, "Y")
        otok = place("otok", [NB, D], F32, "Y", 8 * TILE)
        xT = place("xT", [KT, S], F32, "X")
        xc_split = place("xc_split", [2, S], F32R, "X")
        xc, gg, tr, ti, la_a, m2 = (place(n, [S], F32, "X", (2 + i) * TILE)
                                    for i, n in enumerate(("xc", "gg", "tr", "ti", "la_a", "m2")))
        th = place("th", [S], F32, "T")
        bd_raw = place("bd_raw", [2, P], F32, "BD")
        bd_split = place("bd_split", [2, 2, P], F32R, "BD", 2 * P * 4)
        wraw = [place(f"wraw{s}", [KT, P], F32, "WRAW", s * TILE) for s in range(2)]
        wsplit = [place(f"wsplit{s}", [2, KT, P], F32R, "WSP", 2 * s * TILE) for s in range(2)]
        q = place("q", [S], F32, "T", 3 * TILE)
        sq = place("sq", [S], F32, "T", 0)
        nt = [place(f"nt{s}", [S], F32, "T", (1 + s) * TILE) for s in range(2)]
        diag = place("diag", [NB, P], F32, "T", 0)
        prow = place("prow", [4, P], F32, "T", 1 * TILE)
        ada_acc = place("ada_acc", [D], F32, "T", 2 * TILE)
        ada_ring = [place(f"ada_ring{s}", [D], F32, "T", s * TILE) for s in range(2)]
        tg = place("tg", [S], F32, "T", 3 * TILE)
        ws_raw = place("ws_raw", [G, P], F32, "T", 1 * TILE)
        vstage = place("vstage", [G, P], F32, "T", 0)
        vhat = place("vhat", [G, P], F32, "T", 1 * TILE)
        wsT = place("wsT", [G, P], F32, "T", 2 * TILE)
        sbias = place("sbias", [G, P], F32, "T", 3 * TILE)
        ybt = [place(f"ybt{s}", [S], F32, "T", s * TILE) for s in range(2)]
        mt = place("mt", [S], F32, "T", 2 * TILE)
        ca, cb, gt = (place(n, [S], F32, "T", i * TILE) for i, n in enumerate(("ca", "cb", "gt")))

        coff = [0]

        def const(name, shape, dt=F32):
            n = 4
            for d in shape:
                n *= d
            t = place(name, shape, dt, "C", coff[0])
            coff[0] += (n + 31) // 32 * 32
            return t

        pc = const("pc", [4 * P])
        ident = const("ident", [P])
        ones = const("ones", [P])
        mod = const("mod", [6 * KT])
        s1 = const("s1", [KT])
        s2 = const("s2", [KT])
        g1h = const("g1h", [KT])
        cact = const("cact", [KT])
        hba = const("hba", [KT])
        hbx = const("hbx", [KT])
        la4 = const("la4", [KT])
        la4n = const("la4n", [KT])
        lt = const("lt", [6, KT])
        rs = const("rs", [KT])
        stats = const("stats", [2, 6])
        mv = const("mv", [2])
        sd = const("sd", [1])
        ss = const("ss", [KT])
        eps_t = const("eps_t", [1])
        rsd = const("rsd", [1])
        assert coff[0] <= 4 * KB + 512, coff[0]

        def C(name, i=0, n=1):
            c0 = col[name] + i
            return pc[:, c0:c0 + n] if isinstance(c0, int) else pc[:, bass.ds(c0, n)]

        ps = [ctx.enter_context(nc.psum_tensor(f"ps{i}", [P, 2, HALF], F32)) for i in range(4)]

        def flat(t):
            return t[:, :, :].rearrange("p h t -> p (h t)")

        def blocks(t):
            return t[:, :, :].rearrange("p h (b t) -> p (h b) t", t=P)

        raw_landed = [sem(f"raw_landed{s}") for s in range(2)]
        weights_hi, weights_lo, product_done = sem("weights_hi"), sem("weights_lo"), sem("product_done")
        wait_done = sem("wait_done")
        x_landed = [sem(f"x_landed{i}") for i in range(4)]
        rows_landed = sem("rows_landed")
        ada1_landed = [sem(f"ada1_landed{i}") for i in range(KT)]
        consts_made, param_T, param_col = sem("consts_made"), sem("param_T"), sem("param_col")
        vch, ach = sem("vector_step"), sem("scalar_step")
        silu_t, cact_ready, lam_e, lru_consts = (sem(x) for x in ("silu_t", "cact_ready", "lam_e", "lru_consts"))
        xT_psum, xT_ready, sq_ready, q_added = (sem(x) for x in ("xT_psum", "xT_ready", "sq_ready", "q_added"))
        ss_ready, ss_root, diag_ready, rbc_ready = (sem(x) for x in ("ss_ready", "ss_root", "diag_ready", "rbc_ready"))
        ada_sum, ada_psum, mod_ready = sem("ada_sum"), sem("ada_psum"), sem("mod_ready")
        ada_step, s2_ready = sem("ada_step"), sem("s2_ready")
        s1_ready, eps_made = sem("s1_ready"), sem("eps_made")
        tap0, tap0a, tap0b = sem("tap0"), sem("tap0a"), sem("tap0b")
        tn_ready, x_squared = sem("tn_ready"), sem("x_squared")
        nt_ready, norm_hi, norm_lo = sem("nt_ready"), sem("norm_hi"), sem("norm_lo")
        spilled = sem("spilled")
        bd_landed, bd_hi, bd_lo, bd_done = (sem(x) for x in ("bd_landed", "bd_hi", "bd_lo", "bd_done"))
        conv_done, xc_hi, xc_lo = sem("conv_done"), sem("xc_hi"), sem("xc_lo")
        gelu_done, gates_read, th_ready, w1_ready = (sem(x) for x in ("gelu_done", "gates_read", "th_ready", "w1_ready"))
        m2_ready, msq_ready, y_ready, ya_hi, ya_lo = (sem(x) for x in ("m2_ready", "msq_ready", "y_ready", "ya_hi", "ya_lo"))
        conv_step, tail_step, ffn_conv_step, ln_step, mb_step, g1h_ready = (
            sem(x) for x in ("conv_step", "tail_step", "ffn_conv_step", "ln_step", "mb_step", "g1h_ready"))
        tga_ready, ma_done = sem("tga_ready"), sem("ma_done")
        ring_landed = [sem(f"ring_landed{s}") for s in range(2)]
        ring_used = sem("ring_used")
        zv_ready, ws_landed, ws_masked, ws_psum, ws_ready = (sem(x) for x in ("zv_ready", "ws_landed", "ws_masked", "ws_psum", "ws_ready"))
        bs_landed, r_psum, sbias_ready = sem("bs_landed"), sem("r_psum"), sem("sbias_ready")
        staged, v_psum, var_ready, sd_ready, vhat_ready, mix_psum, mixed_ready, zu_ready = (
            sem(x) for x in ("staged", "v_psum", "var_ready", "sd_ready", "vhat_ready", "mix_psum", "mixed_ready", "zu_ready"))
        ybt_ready, yb_hi, yb_lo = sem("ybt_ready"), sem("yb_hi"), sem("yb_lo")
        tgb_ready, mb_done, mg_hi, mg_lo = (sem(x) for x in ("tgb_ready", "mb_done", "mg_hi", "mg_lo"))
        x_back = [sem(f"x_back{i}") for i in range(2)]
        x2_ready, sq2_ready, q2_added = (sem(x) for x in ("x2_ready", "sq2_ready", "q2_added"))
        ca_ready, cb_ready, ga_ready, g_ready, hid_hi, hid_lo = (
            sem(x) for x in ("ca_ready", "cb_ready", "ga_ready", "g_ready", "hid_hi", "hid_lo"))
        down_used, fin_ready, sq3_ready, q3_added = (sem(x) for x in ("down_used", "fin_ready", "sq3_ready", "q3_added"))
        o_psum, o_act, o_dve, stored = (sem(x) for x in ("o_psum", "o_act", "o_dve", "stored"))

        x_keep = nc.dram_tensor("x_keep", (P, KT, S), F32, kind="Internal").ap()

        def settled(eng):
            eng.sem_inc(wait_done, 1)

        block = ctx.enter_context(nc.Block())

        @block.sync
        def _(sp):
            def load_tile(pair, s, src):
                if not (isinstance(pair, int) and pair == 0):
                    sp.wait_ge(weights_lo, 2 * pair + s - 1)
                    settled(sp)
                sp.dma_start(wraw[s][:, :, :], src).then_inc(raw_landed[s], 16)

            def cols(w, c):
                return w[:, :, c:c + P] if isinstance(c, int) else w[:, :, bass.ds(c, P)]

            for t, rows in enumerate(ROWS):
                for name, n in rows:
                    c0 = col[name] - t * P
                    sp.dma_start(prow[c0:c0 + n, t, :], row_src[name]).then_inc(rows_landed, 16)
            for i in range(4):
                sp.dma_start(xtok[:, 2 * i:2 * i + 2, :], x_tok[:, 2 * i:2 * i + 2, :]).then_inc(x_landed[i], 16)
            for j, part in enumerate((1, 0)):
                for k in range(0, KT, 2):
                    if j == 1 and k == KT - 2:
                        load_tile(0, 0, cols(w_in, 0))
                    sp.dma_start(ada_w[:, j * KT + k:j * KT + k + 2, :], w_ada[:, k:k + 2, part * D:(part + 1) * D])\
                      .then_inc(ada1_landed[j * KT // 2 + k // 2], 16)
            load_tile(0, 1, cols(w_in, D))
            sp.dma_start(bd_raw[:, 0, :], w_lru[0][:, 0, :]).then_inc(bd_landed, 16)
            sp.dma_start(bd_raw[:, 1, :], w_lru[1][:, 0, :]).then_inc(bd_landed, 16)
            sp.wait_ge(xT_ready, KT)
            sp.dma_start(x_keep[:, :, :], xT[:, :, :]).then_inc(spilled, 16)
            with sp.Fori(1, KT) as m:
                load_tile(m, 0, cols(w_in, m * P))
                load_tile(m, 1, cols(w_in, m * P + D))
                sp.wait_ge(bd_lo, m)
                for j in range(2):
                    sp.dma_start(bd_raw[:, j, :], w_lru[j][:, bass.ds(m, 1), :]).then_inc(bd_landed, 16)
            def merge_tile(m, s):
                load_tile(N_MA // 2 + m, s, cols(w_pa, m * P) if s else cols(w_in, m * P + 4 * D))

            def merge_part(part, last=False):
                for e in range(2):
                    if last and e == 1:
                        load_tile(N_ZV // 2, 0, cols(w_in, 3 * D))
                    else:
                        merge_tile(2 * part + e + 1, 0)
                    for k in range(4):
                        s = k % 2
                        sp.wait_ge(ring_used, 8 * part + 4 * e + k + 1)
                        sp.dma_start(ada_ring[s][:, :], w_ada[:, 4 * e + k, bass.ds((part + 2) * D, D)])\
                          .then_inc(ring_landed[s], 16)
                    if last and e == 1:
                        load_tile(N_ZV // 2, 1, cols(w_in, 3 * D + P))
                    else:
                        merge_tile(2 * part + e + 1, 1)

            merge_tile(0, 0)
            merge_tile(0, 1)
            sp.wait_ge(ya_lo, KT)
            with sp.Fori(0, KT // 2 - 1) as part:
                merge_part(part)
            merge_part(KT // 2 - 1, True)
            sp.wait_ge(mod_ready, 6)
            sp.dma_start(ws_raw[:, :, :], w_s).then_inc(ws_landed, 16)
            sp.wait_ge(ma_done, KT + 1)
            sp.dma_start(sbias[:, :, :].rearrange("p g t -> p (g t)"), b_s.to_broadcast([P, G * P]))\
              .then_inc(bs_landed, 16)
            with sp.Fori(1, KT // 2) as i:
                for s in range(2):
                    load_tile(N_ZV // 2 + i, s, cols(w_in, (2 * i + s) * P + 3 * D))
            with sp.Fori(0, KT // 2) as i:
                for s in range(2):
                    load_tile(N_ZU // 2 + i, s, cols(w_in, (2 * i + s) * P + 2 * D))
            with sp.Fori(0, KT) as m:
                load_tile(N_MB // 2 + m, 0, cols(w_in, m * P + 5 * D))
                load_tile(N_MB // 2 + m, 1, cols(w_pb, m * P))
            load_tile(N_OUT // 2, 0, cols(w_o, 0))
            load_tile(N_OUT // 2, 1, cols(w_o, P))
            sp.wait_ge(spilled, 16)
            for i in range(2):
                sp.wait_ge(mg_lo, (i + 1) * KT // 2)
                sp.dma_start(xT[:, i * KT // 2:(i + 1) * KT // 2, :], x_keep[:, i * KT // 2:(i + 1) * KT // 2, :])\
                  .then_inc(x_back[i], 16)
            with sp.Fori(1, KT // 2) as i:
                for s in range(2):
                    load_tile(N_OUT // 2 + i, s, cols(w_o, (2 * i + s) * P))
            with sp.Fori(0, NG) as g:
                with sp.Fori(0, KT) as j:
                    for s in range(2):
                        load_tile(N_FFN // 2 + PER_G // 2 * g + j, s, cols(w_up, g * KT * P + j * P + s * FT * P))
                with sp.Fori(0, KT // 2) as i:
                    for s in range(2):
                        load_tile(N_FFN // 2 + PER_G // 2 * g + KT + i, s,
                                  w_down[:, bass.ds(KT * g, KT), bass.ds((2 * i + s) * P, P)])
            for i in range(NB):
                if i % 2 == 0:
                    sp.wait_ge(o_act, i // 2 + 1)
                else:
                    sp.wait_ge(o_dve, i // 2 + 1)
                sp.dma_start(out_tok[:, i, :], otok[:, i, :]).then_inc(stored, 16)
            sp.wait_ge(stored, 16 * NB)

        @block.gpsimd
        def _(pool):
            nc.gpsimd.memset(ident[:, :], 0.0).then_inc(consts_made, 1)
            pool.wait_ge(consts_made, 1)
            nc.gpsimd.affine_select(out=ident[:, :], in_=ident[:, :], compare_op=ALU.not_equal, fill=1.0, base=0,
                                    pattern=[[-1, P]], channel_multiplier=1).then_inc(consts_made, 1)
            nc.gpsimd.memset(ones[:, :], 1.0).then_inc(consts_made, 1)
            pool.wait_ge(ws_landed, 16)
            nc.gpsimd.affine_select(out=ws_raw[:, :, :], in_=ws_raw[:, :, :], compare_op=ALU.is_ge, fill=0.0, base=0,
                                    pattern=[[0, G], [-1, P]], channel_multiplier=1).then_inc(ws_masked, 1)

        @block.tensor
        def _(pe):
            def product_step(s, psum, acts, k):
                for w, x in ((0, 0), (0, 1), (1, 0)):
                    for h in range(2):
                        last = nc.tensor.matmul(
                            psum[:, h, :], wsplit[s][:, w, k, :], acts[:, k, x, h * HALF:(h + 1) * HALF],
                            start=(k == 0 and w == 0 and x == 0), stop=(k == KT - 1 and w == 1))
                return last

            def product(pair, s, psum, acts, k_sem=None, k_base=0):
                pe.wait_ge(weights_lo, 2 * pair + s + 1)
                for k in range(KT):
                    if k_sem is not None:
                        pe.wait_ge(k_sem, k_base + k + 1)
                    last = product_step(s, psum, acts, k)
                last.then_inc(product_done, 1)

            def column_sums(src, n, psum):
                for j in range(n):
                    last = nc.tensor.matmul(psum[:, 0, j:j + 1], src[:, j * P:(j + 1) * P], ones[:, 0:1],
                                            start=True, stop=True)
                return last

            def norm_scale(count):
                pe.wait_ge(diag_ready, count)
                for h in range(2):
                    last = nc.tensor.matmul(ps[3][:, h, :], ones[:, :],
                                            diag[:, 4 * h:4 * h + 4, :].rearrange("p b t -> p (b t)"),
                                            start=True, stop=True)
                last.then_inc(rbc_ready, 1)

            pe.wait_ge(consts_made, 3)
            pe.wait_ge(rows_landed, 16 * sum(len(r) for r in ROWS))
            for t in range(4):
                n = sum(n for _, n in ROWS[t])
                last = nc.tensor.transpose(ps[3][:, 0, t * P:t * P + n], prow[0:n, t, :], ident[0:n, 0:n])
            last.then_inc(param_T, 1)
            pe.wait_ge(param_col, 4)
            norm_scale(1)
            for m in range(KT):
                if m >= 2:
                    pe.wait_ge(xT_ready, m - 1)
                for i in range(NB):
                    if m == 0:
                        pe.wait_ge(x_landed[i // 2], 16)
                    last = nc.tensor.transpose(blocks(ps[m % 2])[:, i, :], xtok[:, i, m * P:(m + 1) * P], ident[:, :])
                last.then_inc(xT_psum, 1)
            for j in range(2):
                pe.wait_ge(ada_sum, j + 1)
                if j:
                    pe.wait_ge(mod_ready, j)
                column_sums(ada_acc, KT, ps[2]).then_inc(ada_psum, 1)

            def rnn(m, first=False):
                if not first:
                    pe.wait_ge(conv_done, m)
                product(m, 0, ps[0], h_split, norm_lo if first else None)
                if not first:
                    pe.wait_ge(gelu_done, m)
                product(m, 1, ps[1], h_split)
                pe.wait_ge(xc_lo, m + 1)
                pe.wait_ge(bd_lo, m + 1)
                if first:
                    pe.wait_ge(mod_ready, 2)
                    pe.wait_ge(tn_ready, KT)
                else:
                    pe.wait_ge(gates_read, 2 * m)
                for j in range(2):
                    for w, x in ((0, 0), (0, 1), (1, 0)):
                        for h in range(2):
                            last = nc.tensor.matmul(ps[2 + j][:, h, :], bd_split[:, w, j, :],
                                                    xc_split[:, x, h * HALF:(h + 1) * HALF],
                                                    start=(w == 0 and x == 0), stop=(w == 1))
                    last.then_inc(bd_done, 1)

            rnn(0, True)
            with pe.Fori(1, KT) as m:
                rnn(m)
            with pe.Fori(0, KT // 2) as part:
                for e in range(2):
                    pair = N_MA // 2 + 2 * part + e
                    pe.wait_ge(conv_done, KT)
                    pe.wait_ge(tga_ready, 2 * part + e + 1)
                    product(pair, 0, ps[0], h_split)
                    pe.wait_ge(gelu_done, KT)
                    pe.wait_ge(ma_done, 2 * part + e + 1)
                    product(pair, 1, ps[1], ya_split, ya_lo)
                pe.wait_ge(gates_read, 2 * KT)
                pe.wait_ge(mod_ready, part + 2)
                pe.wait_ge(ada_sum, part + 3)
                column_sums(ada_acc, KT, ps[2]).then_inc(ada_psum, 1)

            def zv(i):
                for s in range(2):
                    pe.wait_ge(zv_ready, 2 * i + s - 1)
                    product(N_ZV // 2 + i, s, ps[s], h_split)

            pe.wait_ge(tga_ready, KT + 1)
            product(N_ZV // 2, 0, ps[0], h_split)
            pe.wait_ge(ma_done, KT + 1)
            product(N_ZV // 2, 1, ps[1], h_split)
            pe.wait_ge(mod_ready, 6)
            pe.wait_ge(ws_masked, 1)
            for g in range(G):
                last = nc.tensor.transpose(blocks(ps[2])[:, g, :], ws_raw[:, g, :], ident[:, :])
            last.then_inc(ws_psum, 1)
            zv(1)
            pe.wait_ge(ws_ready, 1)
            for h in range(2):
                last = nc.tensor.matmul(ps[3][:, h, :], ones[:, :],
                                        wsT[:, 4 * h:4 * h + 4, :].rearrange("p g t -> p (g t)"), start=True, stop=True)
            last.then_inc(r_psum, 1)
            with pe.Fori(2, KT // 2) as i:
                zv(i)

            def zu(i, first=False):
                for s in range(2):
                    b = 2 * i + s
                    pe.wait_ge(staged, b + 1)
                    if not (first and s == 0):
                        pe.wait_ge(vhat_ready, b)
                    for g in range(G):
                        last = nc.tensor.transpose(blocks(ps[2])[:, g, :], vstage[:, g, :], ident[:, :])
                    last.then_inc(v_psum, 1)
                    if first:
                        pe.wait_ge(zv_ready, KT - 1 + s)
                    else:
                        pe.wait_ge(zu_ready, b - 1)
                    product(N_ZU // 2 + i, s, ps[s], h_split)
                    pe.wait_ge(vhat_ready, b + 1)
                    if first and s == 0:
                        pe.wait_ge(sbias_ready, 1)
                    else:
                        pe.wait_ge(mixed_ready, b)
                    for g in range(G):
                        last = nc.tensor.matmul(blocks(ps[3])[:, g, :], vhat[:, g, :], wsT[:, g, :],
                                                start=True, stop=True)
                    last.then_inc(mix_psum, 1)

            zu(0, True)
            with pe.Fori(1, KT // 2) as i:
                zu(i)

            pe.wait_ge(zu_ready, KT)
            with pe.Fori(0, KT) as m:
                pe.wait_ge(tgb_ready, m + 1)
                product(N_MB // 2 + m, 0, ps[0], h_split)
                pe.wait_ge(mb_done, m + 1)
                product(N_MB // 2 + m, 1, ps[1], yb_split, yb_lo)

            def proj(i, first=False):
                for s in range(2):
                    if first:
                        pe.wait_ge(tgb_ready if s == 0 else mb_done, KT + 1)
                    else:
                        pe.wait_ge(x2_ready, 2 * i + s - 1)
                    product(N_OUT // 2 + i, s, ps[s], merged_split, mg_lo)

            proj(0, True)
            with pe.Fori(1, KT // 2) as i:
                proj(i)
            pe.wait_ge(mixed_ready, KT)
            pe.wait_ge(q2_added, KT)
            column_sums(q, NB, ps[2]).then_inc(ss_ready, 1)
            norm_scale(2)

            def ups(g, first=False):
                def pair(j, free=False):
                    f = KT * g + j
                    n2 = N_FFN // 2 + PER_G // 2 * g + j
                    if not free:
                        pe.wait_ge(ca_ready, f)
                    product(n2, 0, ps[0], h2_split)
                    pe.wait_ge(cb_ready, f)
                    product(n2, 1, ps[1], h2_split)

                if first:
                    pe.wait_ge(x2_ready, KT)
                    pe.wait_ge(weights_lo, N_FFN + 2)
                    for k in range(KT):
                        pe.wait_ge(norm_lo, KT + k + 1)
                        for s in range(2):
                            last = product_step(s, ps[2 - s], h2_split, k)
                            if k == KT - 1:
                                last.then_inc(product_done, 1)
                    pair(1, True)
                    with pe.Fori(2, KT) as j:
                        pair(j)
                else:
                    with pe.Fori(0, KT) as j:
                        pair(j)

            def downs(g):
                with pe.Fori(0, KT // 2) as i:
                    for s in range(2):
                        pe.wait_ge(down_used, KT * g + 2 * i + s + 1)
                        product(N_FFN // 2 + PER_G // 2 * g + KT + i, s, ps[2 + s], hid_split, hid_lo, KT * g)

            ups(0, True)
            pe.wait_ge(norm_lo, 2 * KT)
            downs(0)
            with pe.Fori(1, NG) as g:
                ups(g)
                downs(g)

            pe.wait_ge(down_used, KT * NG + 2)
            pe.wait_ge(q3_added, KT)
            column_sums(q, NB, ps[2]).then_inc(ss_ready, 1)
            pe.wait_ge(ca_ready, FT)
            pe.wait_ge(cb_ready, FT)
            pe.wait_ge(fin_ready, KT)
            for i in range(NB):
                if i >= 3:
                    before = i - 3
                    pe.wait_ge(o_act if before % 2 == 0 else o_dve, before // 2 + 1)
                for m in range(KT):
                    last = nc.tensor.transpose(blocks(ps[(3, 0, 1)[i % 3]])[:, m, :], fin[:, m, i * P:(i + 1) * P],
                                               ident[:, :])
                last.then_inc(o_psum, 1)

        @block.scalar
        def _(act):
            def split_hi(pair, s):
                act.wait_ge(raw_landed[s], 16 * pair + 16)
                if not (isinstance(pair, int) and pair == 0):
                    act.wait_ge(product_done, 2 * pair + s - 1)
                nc.scalar.activation(wsplit[s][:, 0, :, :], wraw[s][:, :, :], ACT.Copy).then_inc(weights_hi, 1)


            epsc = eps_t[:, 0:1]
            act.sem_inc(tga_ready, 1)
            act.sem_inc(tgb_ready, 1)
            act.wait_ge(param_T, 1)
            for t in range(4):
                n = sum(n for _, n in ROWS[t])
                nc.scalar.activation(pc[:, t * P:t * P + n], ps[3][:, 0, t * P:t * P + n], ACT.Copy)\
                    .then_inc(param_col, 1)
            act.wait_ge(param_col, 4)
            nc.scalar.activation(cact[:, :], C("c", 0, KT), ACT.Tanh, scale=0.5).then_inc(silu_t, 1)
            act.wait_ge(lam_e, 1)
            nc.scalar.activation(lt[:, 1, :], lt[:, 0, :], ACT.Exp, scale=-1.0).then_inc(lam_e, 1)
            for i in range(NB):
                act.wait_ge(x_landed[i // 2], 16)
                if i:
                    act.wait_ge(x_squared, i)
                nc.scalar.activation(sq[:, :], xtok[:, i, :], ACT.Square, accum_out=ss[:, i:i + 1]).then_inc(x_squared, 1)
            act.wait_ge(x_squared, NB)
            act.wait_ge(eps_made, 1)
            nc.scalar.activation(rs[:, :], ss[:, :], ACT.Sqrt, bias=epsc, scale=1.0 / D).then_inc(ss_root, 1)
            for m in range(KT):
                act.wait_ge(xT_psum, m + 1)
                nc.scalar.activation(xT[:, m, :], flat(ps[m % 2]), ACT.Copy).then_inc(xT_ready, 1)
            split_hi(0, 0)
            act.wait_ge(s1_ready, 1)
            act.wait_ge(mod_ready, 2)
            for k in range(KT):
                act.wait_ge(tn_ready, k + 1)
                nc.scalar.activation(h_split[:, k, 0, :], tn[:, k, :], ACT.Identity, bias=mod[:, k:k + 1],
                                     scale=s1[:, k:k + 1]).then_inc(norm_hi, 1)
            split_hi(0, 1)
            act.wait_ge(bd_landed, 32)
            nc.scalar.activation(bd_split[:, 0, :, :], bd_raw[:, :, :], ACT.Copy).then_inc(bd_hi, 1)
            act.wait_ge(lru_consts, 4)
            act.wait_ge(spilled, 16)

            def gates(m, first):
                act.wait_ge(bd_done, 2 * m + 1)
                nc.scalar.activation(tr[:, :], flat(ps[2]), ACT.Tanh, bias=hba[:, bass.ds(m, 1)], scale=0.5)\
                    .then_inc(gates_read, 1)
                act.wait_ge(bd_done, 2 * m + 2)
                if not first:
                    act.wait_ge(ya_lo, m)
                nc.scalar.activation(ti[:, :], flat(ps[3]), ACT.Tanh, bias=hbx[:, bass.ds(m, 1)], scale=0.5)\
                    .then_inc(gates_read, 1)
                act.wait_ge(gates_read, 2 * m + 1)
                nc.scalar.activation(th[:, :], tr[:, :], ACT.Tanh, bias=la4n[:, bass.ds(m, 1)],
                                     scale=la4n[:, bass.ds(m, 1)]).then_inc(ach, 1)
                nc.scalar.activation(la_a[:, :], tr[:, :], ACT.Exp, bias=la4[:, bass.ds(m, 1)],
                                     scale=la4[:, bass.ds(m, 1)]).then_inc(ach, 1)
                act.wait_ge(ach, 2 * m + 2)
                nc.scalar.activation(m2[:, :], la_a[:, :], ACT.Square).then_inc(th_ready, 1)
                split_hi(m + 1, 1)
                act.wait_ge(m2_ready, m + 1)
                nc.scalar.activation(m2[:, :], m2[:, :], ACT.Sqrt, scale=0.25).then_inc(msq_ready, 1)

            def store_ya_hi(m):
                act.wait_ge(y_ready, m + 1)
                nc.scalar.activation(ya_split[:, bass.ds(m, 1), 0, :], ti[:, :], ACT.Copy).then_inc(ya_hi, 1)

            def rnn(m, first=False):
                act.wait_ge(product_done, 2 * m + 1)
                if not first:
                    act.wait_ge(w1_ready, m)
                nc.scalar.activation(xc[:, :], flat(ps[0]), ACT.Identity, bias=C("rnn_conv_b", m),
                                     scale=C("rnn_conv_w", (CW - 1) * KT + m)).then_inc(tap0, 1)
                split_hi(m + 1, 0)
                if not first:
                    store_ya_hi(m - 1)
                act.wait_ge(conv_done, m + 1)
                nc.scalar.activation(xc_split[:, 0, :], xc[:, :], ACT.Copy).then_inc(xc_hi, 1)
                act.wait_ge(product_done, 2 * m + 2)
                nc.scalar.activation(gg[:, :], flat(ps[1]), ACT.Gelu_apprx_tanh).then_inc(gelu_done, 1)
                gates(m, first)

            rnn(0, True)

            def bd_next(m):
                act.wait_ge(bd_landed, 32 * m + 32)
                act.wait_ge(bd_done, 2 * m)
                nc.scalar.activation(bd_split[:, 0, :, :], bd_raw[:, :, :], ACT.Copy).then_inc(bd_hi, 1)

            with act.Fori(1, KT) as m:
                bd_next(m)
                rnn(m)
            store_ya_hi(KT - 1)

            with act.Fori(0, KT) as m:
                n2 = N_MA // 2 + m
                split_hi(n2 + 1, 0)
                act.wait_ge(ma_done, m + 1)
                nc.scalar.activation(tg[:, :], flat(ps[0]), ACT.Tanh, scale=0.5).then_inc(tga_ready, 1)
                split_hi(n2 + 1, 1)

            def zv(i):
                for s in range(2):
                    split_hi(N_ZV // 2 + i + 1, s)
                    nc.scalar.activation(zuv[:, bass.ds(2 * i + s, 1), 1, :], flat(ps[s]), ACT.Gelu_apprx_tanh)\
                        .then_inc(zv_ready, 1)

            zv(0)
            act.wait_ge(ws_psum, 1)
            nc.scalar.activation(wsT[:, :, :], blocks(ps[2]), ACT.Copy).then_inc(ws_ready, 1)
            with act.Fori(1, KT // 2) as i:
                zv(i)
            act.wait_ge(zv_ready, KT)

            def stage(b):
                nc.scalar.activation(vstage[:, :, :], zuv[:, :, 1, bass.ds(b * P, P)], ACT.Copy).then_inc(staged, 1)

            stage(0)

            def zu(i, last=False):
                for s in range(2):
                    b = 2 * i + s
                    act.wait_ge(var_ready, b + 1)
                    nc.scalar.activation(sd[:, :], mv[:, 1:2], ACT.Sqrt, bias=epsc).then_inc(sd_ready, 1)
                    if not (last and s == 1):
                        act.wait_ge(v_psum, b + 1)
                        stage(b + 1)
                    split_hi(N_ZU // 2 + i + 1, s)
                    nc.scalar.activation(zuv[:, bass.ds(b, 1), 0, :], flat(ps[s]), ACT.Gelu_apprx_tanh)\
                        .then_inc(zu_ready, 1)

            with act.Fori(0, KT // 2 - 1) as i:
                zu(i)
            zu(KT // 2 - 1, True)

            def yb_part(m):
                act.wait_ge(ybt_ready, m + 1)
                nc.scalar.activation(yb_split[:, m, 0, :], ybt[m % 2][:, :], ACT.Copy).then_inc(yb_hi, 1)

            for m in range(4):
                yb_part(m)
            split_hi(N_MB // 2 + 1, 0)
            for m in range(4, KT):
                yb_part(m)

            def merge_b(m, first=False):
                n2 = N_MB // 2 + m
                if not first:
                    split_hi(n2 + 1, 0)
                    act.wait_ge(mb_done, m + 1)
                nc.scalar.activation(tg[:, :], flat(ps[0]), ACT.Tanh, scale=0.5).then_inc(tgb_ready, 1)
                split_hi(n2 + 1, 1)

            merge_b(0, True)
            with act.Fori(1, KT - 1) as m:
                merge_b(m)

            def merged_hi(m):
                nc.scalar.activation(merged_split[:, m, 0, :], xT[:, m, :], ACT.Copy).then_inc(mg_hi, 1)

            m = KT - 1
            split_hi(N_MB // 2 + m + 1, 0)
            act.wait_ge(mb_done, m + 1)
            nc.scalar.activation(tg[:, :], flat(ps[0]), ACT.Tanh, scale=0.5).then_inc(tgb_ready, 1)
            for k in range(KT - 1):
                merged_hi(k)
            split_hi(N_MB // 2 + m + 1, 1)
            act.wait_ge(mb_done, KT + 1)
            merged_hi(KT - 1)

            def proj(i, first=False):
                for s in range(2):
                    m = 2 * i + s
                    act.wait_ge(x2_ready, m + 1)
                    if not (first and s == 0):
                        act.wait_ge(q2_added, m)
                    nc.scalar.activation(sq[:, :], xT[:, bass.ds(m, 1), :], ACT.Square).then_inc(sq2_ready, 1)
                    split_hi(N_OUT // 2 + i + 1, s)

            proj(0, True)
            with act.Fori(1, KT // 2) as i:
                proj(i)
            act.wait_ge(ss_ready, 1)
            nc.scalar.activation(rs[:, :], ps[2][:, 0, 0:NB], ACT.Sqrt, bias=epsc, scale=1.0 / D).then_inc(ss_root, 1)
            for k in range(KT):
                act.wait_ge(nt_ready, KT + k + 1)
                nc.scalar.activation(h2_split[:, k, 0, :], nt[k % 2][:, :], ACT.Identity,
                                     bias=mod[:, 3 * KT + k:3 * KT + k + 1]).then_inc(norm_hi, 1)

            def up(g, j, first=False):
                f = KT * g + j
                n2 = N_FFN // 2 + PER_G // 2 * g + j
                for dst, s, o, done in ((ca, 0, 0, tap0a), (cb, 1, FT, tap0b)):
                    act.wait_ge(product_done, 2 * n2 + s + 1)
                    if not first:
                        act.wait_ge(g_ready, f)
                    nc.scalar.activation(dst[:, :], flat(ps[2] if first and s == 0 else ps[s]), ACT.Identity,
                                         bias=C("ffn_conv_b", o + f), scale=C("ffn_conv_w2", o + f)).then_inc(done, 1)
                    split_hi(n2 + 1, s)
                    if s == 0:
                        act.wait_ge(ca_ready, f + 1)
                        nc.scalar.activation(ca[:, :], ca[:, :], ACT.Gelu_apprx_tanh).then_inc(ga_ready, 1)
                act.wait_ge(g_ready, f + 1)
                nc.scalar.activation(hid_split[:, bass.ds(j, 1), 0, :], gt[:, :], ACT.Copy).then_inc(hid_hi, 1)

            def ups(g, first=False):
                if first:
                    up(0, 0, True)
                with act.Fori(1 if first else 0, KT) as j:
                    up(g, j)

            def downs(g):
                with act.Fori(0, KT // 2) as i:
                    for s in range(2):
                        split_hi(N_FFN // 2 + PER_G // 2 * g + KT + i + 1, s)

            ups(0, True)
            downs(0)
            with act.Fori(1, NG - 1) as g:
                ups(g)
                downs(g)
            ups(NG - 1)

            def last_down(i, split, first=False):
                for s in range(2):
                    m = 2 * i + s
                    if split:
                        split_hi(N_TILES // 2 - KT // 2 + i + 1, s)
                    act.wait_ge(down_used, KT * (NG - 1) + m + 3)
                    nc.scalar.activation(fin[:, bass.ds(m, 1), :], xT[:, bass.ds(m, 1), :], ACT.Identity,
                                         scale=C("norm_final_g", m)).then_inc(fin_ready, 1)
                    if not (first and s == 0):
                        act.wait_ge(q3_added, m)
                        settled(act)
                    nc.scalar.activation(sq[:, :], xT[:, bass.ds(m, 1), :], ACT.Square).then_inc(sq3_ready, 1)

            last_down(0, True, True)
            with act.Fori(1, KT // 2 - 1) as i:
                last_down(i, True)
            last_down(KT // 2 - 1, False)
            act.wait_ge(ss_ready, 2)
            nc.scalar.activation(rs[:, :], ps[2][:, 0, 0:NB], ACT.Sqrt, bias=epsc, scale=1.0 / D).then_inc(ss_root, 1)
            act.wait_ge(diag_ready, 3)
            for i in range(0, NB, 2):
                act.wait_ge(o_psum, i + 1)
                nc.scalar.activation(otok[:, i, :], flat(ps[(3, 0, 1)[i % 3]]), ACT.Identity,
                                     scale=rs[:, i:i + 1]).then_inc(o_act, 1)

        @block.vector
        def _(dve):
            V = nc.vector
            steps = [0]

            def step(ins):
                steps[0] += 1
                ins.then_inc(vch, 1)
                dve.wait_ge(vch, steps[0])

            def split_lo(pair, s):
                dve.wait_ge(weights_hi, 2 * pair + s + 1)
                V.tensor_tensor(wsplit[s][:, 1, :, :], wraw[s][:, :, :], wsplit[s][:, 0, :, :].bitcast(F32),
                                ALU.subtract).then_inc(weights_lo, 1)

            def bd_next(m):
                dve.wait_ge(bd_hi, m + 1)
                V.tensor_tensor(bd_split[:, 1, :, :], bd_raw[:, :, :], bd_split[:, 0, :, :].bitcast(F32),
                                ALU.subtract).then_inc(bd_lo, 1)

            def ada_piece(w, k, first):
                if first:
                    return V.tensor_scalar(ada_acc[:, :], w, cact[:, k:k + 1], None, ALU.mult)
                return V.scalar_tensor_tensor(ada_acc[:, :], w, cact[:, k:k + 1], ada_acc[:, :], ALU.mult, ALU.add)

            def mod_part(part, count):
                dve.wait_ge(ada_psum, count)
                dst = mod[:, part * KT:(part + 1) * KT] if isinstance(part, int) else mod[:, bass.ds(part * KT, KT)]
                V.tensor_tensor(dst, ps[2][:, 0, 0:KT], C("b_ada", part * KT, KT), ALU.add).then_inc(mod_ready, 1)

            def rms_diag(count):
                dve.wait_ge(ss_root, count)
                step(V.reciprocal(rs[:, :], rs[:, :]))
                V.tensor_tensor(diag[:, :, :], ident[:, :].unsqueeze(1).to_broadcast([P, NB, P]),
                                rs[:, :].unsqueeze(2).to_broadcast([P, NB, P]), ALU.mult).then_inc(diag_ready, 1)

            def modulation(dst, part, g):
                return V.scalar_tensor_tensor(dst[:, :], mod[:, part * KT:(part + 1) * KT], 1.0, C(g, 0, KT),
                                              ALU.add, ALU.mult)

            dve.sem_inc(ma_done, 1)
            dve.sem_inc(mb_done, 1)
            dve.sem_inc(ring_used, 2)
            dve.sem_inc(down_used, 2)
            V.memset(eps_t[:, :], EPS).then_inc(eps_made, 1)
            dve.wait_ge(silu_t, 1)
            step(V.tensor_scalar(cact[:, :], cact[:, :], 1.0, 0.5, ALU.add, ALU.mult))
            step(V.tensor_tensor(cact[:, :], cact[:, :], C("c", 0, KT), ALU.mult))
            lam = C("lru_lambda", 0, KT)
            step(V.tensor_scalar(lt[:, 2, :], lam, -1.0, None, ALU.mult))
            V.tensor_tensor(lt[:, 0, :], lt[:, 2, :], lam, ALU.max).then_inc(lam_e, 1)
            dve.wait_ge(lam_e, 2)
            step(V.tensor_scalar(lt[:, 2, :], lt[:, 1, :], 2.0, None, ALU.add))
            step(V.reciprocal(lt[:, 2, :], lt[:, 2, :]))
            step(V.tensor_tensor(lt[:, 1, :], lt[:, 1, :], lt[:, 2, :], ALU.mult))
            step(V.tensor_tensor(lt[:, 2, :], lt[:, 1, :], lt[:, 1, :], ALU.mult))
            TERMS = 9
            step(V.tensor_scalar(lt[:, 3, :], lt[:, 2, :], 1.0 / (2 * TERMS + 1), 1.0 / (2 * TERMS - 1), ALU.mult, ALU.add))
            for j in range(TERMS - 2, -1, -1):
                step(V.tensor_tensor(lt[:, 3, :], lt[:, 3, :], lt[:, 2, :], ALU.mult))
                step(V.tensor_scalar(lt[:, 3, :], lt[:, 3, :], 1.0 / (2 * j + 1), None, ALU.add))
            step(V.tensor_tensor(lt[:, 3, :], lt[:, 3, :], lt[:, 1, :], ALU.mult))
            step(V.tensor_scalar(lt[:, 4, :], lam, 0.0, None, ALU.min))
            step(V.scalar_tensor_tensor(lt[:, 4, :], lt[:, 3, :], -2.0, lt[:, 4, :], ALU.mult, ALU.add))
            V.tensor_scalar(la4[:, :], lt[:, 4, :], LRU_C / 2, None, ALU.mult).then_inc(lru_consts, 1)
            V.tensor_scalar(la4n[:, :], lt[:, 4, :], -LRU_C / 2, None, ALU.mult).then_inc(lru_consts, 1)
            V.tensor_scalar(hba[:, :], C("lru_b_a", 0, KT), 0.5, None, ALU.mult).then_inc(lru_consts, 1)
            V.tensor_scalar(hbx[:, :], C("lru_b_x", 0, KT), 0.5, None, ALU.mult).then_inc(lru_consts, 1)

            def add_square(sem_ready, sem_added, m, first):
                dve.wait_ge(sem_ready, m + 1)
                if first:
                    V.tensor_copy(q[:, :], sq[:, :]).then_inc(sem_added, 1)
                else:
                    dve.wait_ge(sem_added, m)
                    V.tensor_tensor(q[:, :], q[:, :], sq[:, :], ALU.add).then_inc(sem_added, 1)

            rms_diag(1)
            for j in range(2):
                for k in range(KT):
                    dve.wait_ge(ada1_landed[j * KT // 2 + k // 2], 16)
                    if k == 0 and j == 1:
                        dve.wait_ge(ada_psum, 1)
                        mod_part(1, 1)
                        dve.wait_ge(mod_ready, 1)
                        modulation(s1, 1, "norm_mix_g").then_inc(s1_ready, 1)
                    if k:
                        dve.wait_ge(ada_step, j * KT + k)
                    ada_piece(ada_w[:, j * KT + k, :], k, k == 0).then_inc(ada_step, 1)
                    if j == 0:
                        if k == 0:
                            dve.wait_ge(rbc_ready, 1)
                        dve.wait_ge(xT_ready, k + 1)
                        V.tensor_tensor(tn[:, k, :], xT[:, k, :], flat(ps[3]), ALU.mult).then_inc(tn_ready, 1)
                    if j == 1 and k == KT - 2:
                        split_lo(0, 0)
                dve.wait_ge(ada_step, (j + 1) * KT)
                dve.sem_inc(ada_sum, 1)
            mod_part(0, 2)
            dve.wait_ge(s1_ready, 1)
            dve.wait_ge(mod_ready, 2)
            for k in range(KT + 1):
                if k < KT:
                    if k >= 2:
                        dve.wait_ge(norm_lo, k - 1)
                    V.tensor_scalar(nt[k % 2][:, :], tn[:, k, :], s1[:, k:k + 1], mod[:, k:k + 1], ALU.mult, ALU.add)\
                     .then_inc(nt_ready, 1)
                if k:
                    dve.wait_ge(nt_ready, k)
                    dve.wait_ge(norm_hi, k)
                    V.tensor_tensor(h_split[:, k - 1, 1, :], nt[(k - 1) % 2][:, :], h_split[:, k - 1, 0, :].bitcast(F32),
                                    ALU.subtract).then_inc(norm_lo, 1)
            split_lo(0, 1)
            bd_next(0)
            dve.wait_ge(spilled, 16)

            def conv(dst, src, width, taps, step_sem, before, done):
                for d in range(1, width):
                    if d > 1:
                        ins.then_inc(step_sem, 1)
                        dve.wait_ge(step_sem, before + d - 1)
                    ins = V.scalar_tensor_tensor(dst[:, d:S], flat(src)[:, 0:S - d], taps(width - 1 - d), dst[:, d:S],
                                                 ALU.mult, ALU.add)
                ins.then_inc(done, 1)

            def rnn_tail(m):
                dve.wait_ge(w1_ready, m + 1)
                dve.wait_ge(msq_ready, m + 1)
                V.tensor_tensor(ti[:, :], ti[:, :], m2[:, :], ALU.mult).then_inc(tail_step, 1)
                dve.wait_ge(tail_step, 2 * m + 1)
                V.tensor_tensor_scan(ti[:, :], la_a[:, :], ti[:, :], 0.0, ALU.mult, ALU.add).then_inc(tail_step, 1)
                dve.wait_ge(tail_step, 2 * m + 2)
                V.tensor_tensor(ti[:, :], ti[:, :], gg[:, :], ALU.mult).then_inc(y_ready, 1)

            def ya_part(m):
                dve.wait_ge(ya_hi, m + 1)
                V.tensor_tensor(ya_split[:, bass.ds(m, 1), 1, :], ti[:, :], ya_split[:, bass.ds(m, 1), 0, :].bitcast(F32),
                                ALU.subtract).then_inc(ya_lo, 1)

            def rnn(m, first=False):
                split_lo(m + 1, 0)
                dve.wait_ge(tap0, m + 1)
                conv(xc, ps[0], CW, lambda k: C("rnn_conv_w", k * KT + m), conv_step, (CW - 2) * m, conv_done)
                dve.wait_ge(xc_hi, m + 1)
                V.tensor_tensor(xc_split[:, 1, :], xc[:, :], xc_split[:, 0, :].bitcast(F32), ALU.subtract)\
                 .then_inc(xc_lo, 1)
                if not first:
                    ya_part(m - 1)
                dve.wait_ge(gates_read, 2 * m + 2)
                V.scalar_tensor_tensor(ti[:, :], ti[:, :], 1.0, xc[:, :], ALU.add, ALU.mult).then_inc(w1_ready, 1)
                dve.wait_ge(th_ready, m + 1)
                V.scalar_tensor_tensor(m2[:, :], m2[:, :], 1.0, th[:, :], ALU.add, ALU.mult).then_inc(m2_ready, 1)
                split_lo(m + 1, 1)
                rnn_tail(m)

            rnn(0, True)
            with dve.Fori(1, KT) as m:
                bd_next(m)
                rnn(m)
            ya_part(KT - 1)

            with dve.Fori(0, KT // 2) as part:
                for e in range(2):
                    m = 2 * part + e
                    n2 = N_MA // 2 + m
                    split_lo(n2 + 1, 0)
                    for k in range(4):
                        kk = 4 * e + k
                        dve.wait_ge(ring_landed[k % 2], 64 * part + 32 * e + 16 * (k // 2) + 16)
                        if kk == 0:
                            dve.wait_ge(ada_psum, part + 2)
                        else:
                            dve.wait_ge(ring_used, 8 * part + kk + 2)
                        ins = ada_piece(ada_ring[k % 2][:, :], kk, kk == 0)
                        ins.then_inc(ring_used, 1)
                    if e == 1:
                        dve.wait_ge(ring_used, 8 * part + 10)
                        dve.sem_inc(ada_sum, 1)
                    split_lo(n2 + 1, 1)
                    dve.wait_ge(tga_ready, m + 2)
                    V.scalar_tensor_tensor(xT[:, bass.ds(m, 1), :], tg[:, :], 1.0, flat(ps[1]), ALU.add, ALU.mult)\
                     .then_inc(ma_done, 1)
                mod_part(part + 2, part + 3)
            dve.wait_ge(mod_ready, 6)
            V.tensor_scalar(g1h[:, :], mod[:, 2 * KT:3 * KT], 0.5, None, ALU.mult).then_inc(g1h_ready, 1)

            for s in range(2):
                split_lo(N_ZV // 2 + 1, s)
            for s in range(2):
                split_lo(N_ZV // 2 + 2, s)
            dve.wait_ge(r_psum, 1)
            dve.wait_ge(bs_landed, 16)
            for g in range(G):
                last = V.scalar_tensor_tensor(sbias[:, g, :], blocks(ps[3])[:, g, :], C("sgu_ln_b", g), sbias[:, g, :],
                                              ALU.mult, ALU.add)
            last.then_inc(sbias_ready, 1)
            with dve.Fori(2, KT // 2) as i:
                for s in range(2):
                    split_lo(N_ZV // 2 + i + 1, s)

            def zu(i):
                for s in range(2):
                    b = 2 * i + s
                    dve.wait_ge(v_psum, b + 1)
                    for h in range(2):
                        V.bn_stats(stats[:, h, :], ps[2][:, h, :]).then_inc(ln_step, 1)
                    dve.wait_ge(ln_step, 4 * b + 2)
                    settled(dve)
                    V.bn_aggr(mv[:, :], stats[:, :, :].rearrange("p a b -> p (a b)")).then_inc(var_ready, 1)
                    dve.wait_ge(sd_ready, b + 1)
                    V.reciprocal(rsd[:, :], sd[:, :]).then_inc(ln_step, 1)
                    dve.wait_ge(ln_step, 4 * b + 3)
                    V.tensor_scalar(vhat[:, :, :], blocks(ps[2]), mv[:, 0:1], rsd[:, 0:1], ALU.subtract, ALU.mult)\
                     .then_inc(vhat_ready, 1)
                    split_lo(N_ZU // 2 + i + 1, s)
                    dve.wait_ge(mix_psum, b + 1)
                    V.tensor_tensor(blocks(ps[3]), blocks(ps[3]),
                                    pc[:, col["sgu_ln_g"]:col["sgu_ln_g"] + G].unsqueeze(2).to_broadcast([P, G, P]),
                                    ALU.mult).then_inc(ln_step, 1)
                    dve.wait_ge(ln_step, 4 * b + 4)
                    V.tensor_tensor(zuv[:, :, 1, bass.ds(b * P, P)], blocks(ps[3]), sbias[:, :, :], ALU.add)\
                     .then_inc(mixed_ready, 1)

            with dve.Fori(0, KT // 2) as i:
                zu(i)

            dve.wait_ge(zu_ready, KT)
            dve.wait_ge(mixed_ready, KT)
            dve.wait_ge(ma_done, KT + 1)

            def yb_mul(m):
                if m >= 2:
                    dve.wait_ge(yb_lo, m - 1)
                V.tensor_tensor(ybt[m % 2][:, :], zuv[:, m, 0, :], zuv[:, m, 1, :], ALU.mult).then_inc(ybt_ready, 1)

            def yb_sub(m):
                dve.wait_ge(yb_hi, m + 1)
                V.tensor_tensor(yb_split[:, m, 1, :], ybt[m % 2][:, :], yb_split[:, m, 0, :].bitcast(F32), ALU.subtract)\
                 .then_inc(yb_lo, 1)

            yb_mul(0)
            for m in range(KT):
                if m + 1 < KT:
                    yb_mul(m + 1)
                yb_sub(m)
                if m == 3:
                    split_lo(N_MB // 2 + 1, 0)

            def merge_b(m):
                dve.wait_ge(tgb_ready, m + 2)
                dve.wait_ge(mb_done, m + 1)
                V.scalar_tensor_tensor(mt[:, :], tg[:, :], 1.0, flat(ps[1]), ALU.add, ALU.mult).then_inc(mb_step, 1)
                dve.wait_ge(mb_step, m + 1)
                V.tensor_tensor(xT[:, bass.ds(m, 1), :], xT[:, bass.ds(m, 1), :], mt[:, :], ALU.add).then_inc(mb_done, 1)

            split_lo(N_MB // 2 + 1, 1)
            merge_b(0)
            with dve.Fori(1, KT - 1) as m:
                split_lo(N_MB // 2 + m + 1, 0)
                split_lo(N_MB // 2 + m + 1, 1)
                merge_b(m)

            def merged_lo(m):
                dve.wait_ge(mg_hi, m + 1)
                V.tensor_tensor(merged_split[:, m, 1, :], xT[:, m, :], merged_split[:, m, 0, :].bitcast(F32),
                                ALU.subtract).then_inc(mg_lo, 1)

            m = KT - 1
            split_lo(N_MB // 2 + m + 1, 0)
            for k in range(KT - 1):
                merged_lo(k)
            split_lo(N_MB // 2 + m + 1, 1)
            merge_b(m)
            merged_lo(KT - 1)

            def proj(i, first=False):
                for s in range(2):
                    m = 2 * i + s
                    dve.wait_ge(product_done, N_OUT + m + 1)
                    V.scalar_tensor_tensor(xT[:, bass.ds(m, 1), :], flat(ps[s]), g1h[:, bass.ds(m, 1)],
                                           xT[:, bass.ds(m, 1), :], ALU.mult, ALU.add).then_inc(x2_ready, 1)
                    add_square(sq2_ready, q2_added, m, first and s == 0)
                    split_lo(N_OUT // 2 + i + 1, s)

            dve.wait_ge(g1h_ready, 1)
            dve.wait_ge(x_back[0], 16)
            proj(0, True)
            proj(1)
            dve.wait_ge(x_back[1], 16)
            with dve.Fori(2, KT // 2) as i:
                proj(i)
            modulation(s2, 4, "norm_ffn_g").then_inc(s2_ready, 1)
            rms_diag(2)
            dve.wait_ge(s2_ready, 1)
            dve.wait_ge(rbc_ready, 2)
            for k in range(KT + 1):
                if k < KT:
                    if k >= 2:
                        dve.wait_ge(norm_lo, KT + k - 1)
                    V.scalar_tensor_tensor(nt[k % 2][:, :], xT[:, k, :], s2[:, k:k + 1], flat(ps[3]),
                                           ALU.mult, ALU.mult).then_inc(nt_ready, 1)
                if k:
                    dve.wait_ge(norm_hi, KT + k)
                    V.scalar_tensor_tensor(h2_split[:, k - 1, 1, :], nt[(k - 1) % 2][:, :],
                                           mod[:, 3 * KT + k - 1:3 * KT + k], h2_split[:, k - 1, 0, :].bitcast(F32),
                                           ALU.add, ALU.subtract).then_inc(norm_lo, 1)

            dve.wait_ge(x2_ready, KT)

            def up(g, j, first=False):
                f = KT * g + j
                n2 = N_FFN // 2 + PER_G // 2 * g + j

                def taps(o):
                    def tap(k):
                        return C("ffn_conv_w01" if k < 2 else "ffn_conv_w2", (k % 2) * 2 * FT + o + f)
                    return tap

                dve.wait_ge(tap0a, f + 1)
                conv(ca, ps[2] if first else ps[0], FW, taps(0), ffn_conv_step, 2 * (FW - 2) * f, ca_ready)
                split_lo(n2 + 1, 0)
                dve.wait_ge(tap0b, f + 1)
                conv(cb, ps[1], FW, taps(FT), ffn_conv_step, 2 * (FW - 2) * f + FW - 2, cb_ready)
                dve.wait_ge(cb_ready, f + 1)
                dve.wait_ge(ga_ready, f + 1)
                V.tensor_tensor(gt[:, :], ca[:, :], cb[:, :], ALU.mult).then_inc(g_ready, 1)
                split_lo(n2 + 1, 1)
                dve.wait_ge(hid_hi, f + 1)
                V.tensor_tensor(hid_split[:, bass.ds(j, 1), 1, :], gt[:, :],
                                hid_split[:, bass.ds(j, 1), 0, :].bitcast(F32), ALU.subtract).then_inc(hid_lo, 1)

            def ups(g, first=False):
                if first:
                    up(0, 0, True)
                with dve.Fori(1 if first else 0, KT) as j:
                    up(g, j)

            def down(m, s):
                V.scalar_tensor_tensor(xT[:, bass.ds(m, 1), :], flat(ps[2 + s]), mod[:, bass.ds(5 * KT + m, 1)],
                                       xT[:, bass.ds(m, 1), :], ALU.mult, ALU.add).then_inc(down_used, 1)

            def downs(g):
                with dve.Fori(0, KT // 2) as i:
                    for s in range(2):
                        split_lo(N_FFN // 2 + PER_G // 2 * g + KT + i + 1, s)
                        down(2 * i + s, s)

            ups(0, True)
            downs(0)
            with dve.Fori(1, NG - 1) as g:
                ups(g)
                dve.wait_ge(down_used, KT * g + 2)
                settled(dve)
                downs(g)
            ups(NG - 1)
            dve.wait_ge(down_used, KT * (NG - 1) + 2)

            def last_down(i, split, first=False):
                for s in range(2):
                    m = 2 * i + s
                    n2 = N_TILES // 2 - KT // 2 + i
                    if split:
                        split_lo(n2 + 1, s)
                    else:
                        dve.wait_ge(product_done, 2 * n2 + s + 1)
                    down(m, s)
                    add_square(sq3_ready, q3_added, m, first and s == 0)

            last_down(0, True, True)
            with dve.Fori(1, KT // 2 - 1) as i:
                last_down(i, True)
            last_down(KT // 2 - 1, False)
            dve.wait_ge(ss_root, 3)
            V.reciprocal(rs[:, :], rs[:, :]).then_inc(diag_ready, 1)
            dve.wait_ge(diag_ready, 3)
            for i in range(1, NB, 2):
                dve.wait_ge(o_psum, i + 1)
                V.tensor_scalar(otok[:, i, :], flat(ps[(3, 0, 1)[i % 3]]), rs[:, i:i + 1], None, ALU.mult)\
                 .then_inc(o_dve, 1)


def kernel(**inputs):
    import numpy as np
    import concourse.bacc as bacc
    from concourse.bass_utils import run_bass_kernel_spmd

    nc = bacc.Bacc("TRN2", target_bir_lowering=False, num_devices=1)
    arrays, aps = {}, {}
    for name, value in inputs.items():
        value = np.ascontiguousarray(value)
        arrays[f"in_{name}"] = value
        aps[name] = nc.dram_tensor(f"in_{name}", value.shape, mybir.dt.from_np(value.dtype), kind="ExternalInput").ap()
    out = nc.dram_tensor("out_x", inputs["x"].shape, F32, kind="ExternalOutput").ap()
    build(nc, aps, out)
    result = run_bass_kernel_spmd(nc, [arrays], core_ids=[0])
    return result.results[0]["out_x"]
```

```python
from contextlib import ExitStack

import concourse.bass as bass
from concourse import mybir

F32 = mybir.dt.float32
F32R = mybir.dt.float32r
ALU = mybir.AluOpType
ACT = mybir.ActivationFunctionType

P = 128
HALF = 512
EPS = 1e-6
LRU_C = 8.0


def build(nc, a, out):
    _, S, D = a["x"].shape
    KT = D // P
    NB = S // P
    G = a["sgu_w_s"].shape[1]
    FT = a["w_down"].shape[1] // P
    NG = FT // KT
    assert S == 2 * HALF and KT == 8 and G == KT and FT % KT == 0 and a["lru_w_a"].shape[2] == P
    CW = a["rnn_conv_w"].shape[1]
    FW = a["ffn_conv_w"].shape[1]

    N_RNN = 0
    N_MA = N_RNN + 2 * KT
    N_ZV = N_MA + 2 * KT
    N_ZU = N_ZV + KT
    N_MB = N_ZU + KT
    N_OUT = N_MB + 2 * KT
    N_FFN = N_OUT + KT
    PER_G = 3 * KT
    N_TILES = N_FFN + NG * PER_G

    ROWS = [
        [("c", KT), ("norm_mix_g", KT), ("rnn_conv_w", CW * KT), ("rnn_conv_b", KT), ("lru_b_a", KT),
         ("lru_b_x", KT), ("lru_lambda", KT), ("sgu_ln_g", KT), ("sgu_ln_b", KT), ("norm_ffn_g", KT),
         ("norm_final_g", KT)],
        [("b_ada", 6 * KT), ("ffn_conv_b", 2 * FT)],
        [("ffn_conv_w01", 4 * FT)],
        [("ffn_conv_w2", 2 * FT)],
    ]
    col = {}
    for t, rows in enumerate(ROWS):
        at = 0
        for name, n in rows:
            col[name] = t * P + at
            at += n
        assert at <= P
    row_src = {name: a[name].rearrange("a (r p) -> (a r) p", p=P) for name in
               ("c", "norm_mix_g", "rnn_conv_b", "lru_b_a", "lru_b_x", "lru_lambda", "sgu_ln_g",
                "sgu_ln_b", "norm_ffn_g", "b_ada", "ffn_conv_b")}
    row_src["norm_final_g"] = a["norm_final_g"].rearrange("(r p) -> r p", p=P)
    row_src["rnn_conv_w"] = a["rnn_conv_w"].rearrange("a w (r p) -> (a w r) p", p=P)
    fcw = a["ffn_conv_w"].rearrange("a w (r p) -> (a w r) p", p=P)
    row_src["ffn_conv_w01"] = fcw[0:4 * FT, :]
    row_src["ffn_conv_w2"] = fcw[4 * FT:6 * FT, :]

    def tiles_of(name):
        return a[name].rearrange("a (k p) c -> p (a k) c", p=P)

    w_in, w_ada, w_up, w_down = (tiles_of(x) for x in ("w_in", "w_ada", "w_up", "w_down"))
    w_pa, w_pb, w_o = (tiles_of(x) for x in ("w_branch_a", "w_branch_b", "w_out"))
    w_lru = [a[x].rearrange("a h i j -> i (a h) j") for x in ("lru_w_a", "lru_w_x")]
    w_s = a["sgu_w_s"].rearrange("a g t s -> t (a g) s")
    b_s = a["sgu_b_s"].rearrange("a g t -> a (g t)")
    x_tok = a["x"].rearrange("a (i p) d -> p (a i) d", p=P)
    out_tok = out.rearrange("a (i p) d -> p (a i) d", p=P)

    with ExitStack() as ctx:
        def sem(name):
            return ctx.enter_context(nc.semaphore(name))

        BASE = (nc.sbuf_base + 31) // 32 * 32
        KB = 1024
        TILE = 4 * S
        OFF = {}
        at = BASE
        for name, size in (("H", 8 * 2 * TILE), ("Y", 8 * 2 * TILE), ("X", 8 * TILE),
                           ("WRAW", 2 * TILE), ("WSP", 4 * TILE), ("T", 4 * TILE), ("BD", 3 * KB),
                           ("C", 4 * KB + 512)):
            OFF[name] = at
            at += size
        assert at <= nc.sbuf_usable_end, at

        def place(name, shape, dt, region, offset=0):
            return nc.alloc_sbuf_tensor_at(name, [P] + shape, dt, offset=OFF[region] + offset)

        h_split = place("h_split", [KT, 2, S], F32R, "H")
        merged_split = place("merged_split", [KT, 2, S], F32R, "H")
        hid_split = place("hid_split", [KT, 2, S], F32R, "H")
        ada_w = place("ada_w", [2 * KT, D], F32, "H")
        ya_split = place("ya_split", [KT, 2, S], F32R, "Y")
        zuv = place("zuv", [KT, 2, S], F32, "Y")
        yb_split = place("yb_split", [KT, 2, S], F32R, "Y")
        h2_split = place("h2_split", [KT, 2, S], F32R, "Y")
        xtok = place("xtok", [NB, D], F32, "Y")
        tn = place("tn", [KT, S], F32, "Y", 8 * TILE)
        fin = place("fin", [KT, S], F32, "Y")
        otok = place("otok", [NB, D], F32, "Y", 8 * TILE)
        xT = place("xT", [KT, S], F32, "X")
        xc_split = place("xc_split", [2, S], F32R, "X")
        xc, gg, tr, ti, la_a, m2 = (place(n, [S], F32, "X", (2 + i) * TILE)
                                    for i, n in enumerate(("xc", "gg", "tr", "ti", "la_a", "m2")))
        th = place("th", [S], F32, "T")
        bd_raw = place("bd_raw", [2, P], F32, "BD")
        bd_split = place("bd_split", [2, 2, P], F32R, "BD", 2 * P * 4)
        wraw = [place(f"wraw{s}", [KT, P], F32, "WRAW", s * TILE) for s in range(2)]
        wsplit = [place(f"wsplit{s}", [2, KT, P], F32R, "WSP", 2 * s * TILE) for s in range(2)]
        q = place("q", [S], F32, "T", 3 * TILE)
        sq = place("sq", [S], F32, "T", 0)
        nt = [place(f"nt{s}", [S], F32, "T", (1 + s) * TILE) for s in range(2)]
        nt_half = [nt[n // 2][:, n % 2 * HALF:(n % 2 + 1) * HALF] for n in range(4)]
        diag = place("diag", [NB, P], F32, "T", 0)
        prow = place("prow", [4, P], F32, "T", 1 * TILE)
        ada_acc = place("ada_acc", [D], F32, "T", 2 * TILE)
        shift_acc = place("shift_acc", [HALF], F32, "T", 3 * TILE)
        shift_row = place("shift_row", [HALF], F32, "T", 3 * TILE + 4 * HALF)
        ada_ring = [place(f"ada_ring{s}", [D], F32, "T", s * TILE) for s in range(2)]
        tg = place("tg", [S], F32, "T", 3 * TILE)
        ws_raw = place("ws_raw", [G, P], F32, "T", 1 * TILE)
        vstage = place("vstage", [G, P], F32, "T", 0)
        vhat = place("vhat", [G, P], F32, "T", 1 * TILE)
        wsT = place("wsT", [G, P], F32, "T", 2 * TILE)
        sbias = place("sbias", [G, P], F32, "T", 3 * TILE)
        ybt = [place(f"ybt{s}", [S], F32, "T", s * TILE) for s in range(3)]
        YBT = [0, 1, 0, 2] * (KT // 4)
        mt = place("mt", [S], F32, "T", 2 * TILE)
        ca, cb, gt = (place(n, [S], F32, "T", i * TILE) for i, n in enumerate(("ca", "cb", "gt")))

        coff = [0]

        def const(name, shape, dt=F32):
            n = 4
            for d in shape:
                n *= d
            t = place(name, shape, dt, "C", coff[0])
            coff[0] += (n + 31) // 32 * 32
            return t

        pc = const("pc", [4 * P])
        ident = const("ident", [P])
        ones = const("ones", [P])
        mod = const("mod", [6 * KT])
        s1 = const("s1", [KT])
        s2 = const("s2", [KT])
        g1h = const("g1h", [KT])
        cact = const("cact", [KT])
        hba = const("hba", [KT])
        hbx = const("hbx", [KT])
        la4 = const("la4", [KT])
        la4n = const("la4n", [KT])
        lt = const("lt", [6, KT])
        rs = const("rs", [KT])
        stats = const("stats", [2, 6])
        mv = const("mv", [2])
        sd = const("sd", [1])
        ss = const("ss", [KT])
        eps_t = const("eps_t", [1])
        rsd = const("rsd", [1])
        assert coff[0] <= 4 * KB + 512, coff[0]

        def C(name, i=0, n=1):
            c0 = col[name] + i
            return pc[:, c0:c0 + n] if isinstance(c0, int) else pc[:, bass.ds(c0, n)]

        N2_LAST, N2_ROOT = 2, 6
        SLOTS = (0, 1, 3)
        COPIER = (0, 1, 1, 1, 0, 1, 0, 0)
        ps = [ctx.enter_context(nc.psum_tensor(f"ps{i}", [P, 2, HALF], F32)) for i in range(4)]

        def flat(t):
            return t[:, :, :].rearrange("p h t -> p (h t)")

        def blocks(t):
            return t[:, :, :].rearrange("p h (b t) -> p (h b) t", t=P)

        raw_landed = [sem(f"raw_landed{s}") for s in range(2)]
        weights_hi, weights_lo, product_done = sem("weights_hi"), sem("weights_lo"), sem("product_done")
        wait_done = sem("wait_done")
        x_landed = [sem(f"x_landed{i}") for i in range(4)]
        rows_landed = [sem(f"rows_landed{i}") for i in range(2)]
        scale_landed = [sem(f"scale_landed{i}") for i in range(KT // 2)]
        shift_landed = [[sem(f"shift_landed{h}_{i}") for i in range(KT // 2)] for h in range(2)]
        x_normed = sem("x_normed")
        xT_copied = [sem("xT_copied_act"), sem("xT_copied_dve")]
        shift_row_psum, shift_row_ready, shift_ready = sem("shift_row_psum"), sem("shift_row_ready"), sem("shift_ready")
        consts_made, param_T, param_col = sem("consts_made"), sem("param_T"), sem("param_col")
        vch, ach = sem("vector_step"), sem("scalar_step")
        silu_t, cact_ready, lam_e, lru_consts = (sem(x) for x in ("silu_t", "cact_ready", "lam_e", "lru_consts"))
        xT_psum, tn_psum = sem("xT_psum"), sem("tn_psum")
        ss_ready, ss_root, diag_ready, rbc_ready = (sem(x) for x in ("ss_ready", "ss_root", "diag_ready", "rbc_ready"))
        ada_sum, ada_psum, mod_ready = sem("ada_sum"), sem("ada_psum"), sem("mod_ready")
        ada_step, s2_ready = sem("ada_step"), sem("s2_ready")
        s1_ready, eps_made = sem("s1_ready"), sem("eps_made")
        tap0, tap0a, tap0b = sem("tap0"), sem("tap0a"), sem("tap0b")
        tn_ready, x_squared = sem("tn_ready"), sem("x_squared")
        nt_ready, norm_hi, norm_lo = sem("nt_ready"), sem("norm_hi"), sem("norm_lo")
        spilled = sem("spilled")
        bd_landed, bd_hi, bd_lo, bd_done = (sem(x) for x in ("bd_landed", "bd_hi", "bd_lo", "bd_done"))
        conv_done, xc_hi, xc_lo = sem("conv_done"), sem("xc_hi"), sem("xc_lo")
        gelu_done, gates_read, th_ready, w1_ready = (sem(x) for x in ("gelu_done", "gates_read", "th_ready", "w1_ready"))
        m2_ready, msq_ready, y_ready, ya_hi, ya_lo = (sem(x) for x in ("m2_ready", "msq_ready", "y_ready", "ya_hi", "ya_lo"))
        conv_step, tail_step, ffn_conv_step, ln_step, mb_step, g1h_ready = (
            sem(x) for x in ("conv_step", "tail_step", "ffn_conv_step", "ln_step", "mb_step", "g1h_ready"))
        tga_ready, ma_done = sem("tga_ready"), sem("ma_done")
        ring_landed = [sem(f"ring_landed{s}") for s in range(2)]
        ring_used = sem("ring_used")
        zv_ready, ws_landed, ws_masked, ws_psum, ws_ready = (sem(x) for x in ("zv_ready", "ws_landed", "ws_masked", "ws_psum", "ws_ready"))
        bs_landed, r_psum, sbias_ready = sem("bs_landed"), sem("r_psum"), sem("sbias_ready")
        staged, v_psum, var_ready, sd_ready, vhat_ready, mix_psum, mixed_ready, zu_ready = (
            sem(x) for x in ("staged", "v_psum", "var_ready", "sd_ready", "vhat_ready", "mix_psum", "mixed_ready", "zu_ready"))
        ybt_odd = sem("ybt_odd")
        ybt_ready, yb_hi, yb_lo = sem("ybt_ready"), sem("yb_hi"), sem("yb_lo")
        tgb_ready, mb_done, mg_hi, mg_lo = (sem(x) for x in ("tgb_ready", "mb_done", "mg_hi", "mg_lo"))
        x_back = [sem(f"x_back{i}") for i in range(2)]
        x2_ready, sq2_ready, q2_added = (sem(x) for x in ("x2_ready", "sq2_ready", "q2_added"))
        ca_ready, cb_ready, ga_ready, g_ready, hid_hi, hid_lo = (
            sem(x) for x in ("ca_ready", "cb_ready", "ga_ready", "g_ready", "hid_hi", "hid_lo"))
        down_used, fin_ready, sq3_ready, q3_added = (sem(x) for x in ("down_used", "fin_ready", "sq3_ready", "q3_added"))
        half_done, fin_half = sem("half_done"), sem("fin_half")
        x2_half, sq2_half, q2_half = sem("x2_half"), sem("sq2_half"), sem("q2_half")
        x3_half, sq3_half, q3_half = sem("x3_half"), sem("sq3_half"), sem("q3_half")
        o_psum, o_act, o_dve, stored = (sem(x) for x in ("o_psum", "o_act", "o_dve", "stored"))

        H = [slice(h * HALF, (h + 1) * HALF) for h in range(2)]
        HB = NB // 2
        LAST_IN = N_OUT // 2 + KT // 2 - 1
        LAST = N_TILES // 2 - 1

        x_keep = nc.dram_tensor("x_keep", (P, KT, S), F32, kind="Internal").ap()

        def settled(eng):
            eng.sem_inc(wait_done, 1)

        block = ctx.enter_context(nc.Block())

        @block.sync
        def _(sp):
            def load_tile(pair, s, src):
                if not (isinstance(pair, int) and pair == 0):
                    sp.wait_ge(weights_lo, 2 * pair + s - 1)
                    settled(sp)
                sp.dma_start(wraw[s][:, :, :], src).then_inc(raw_landed[s], 16)

            def cols(w, c):
                return w[:, :, c:c + P] if isinstance(c, int) else w[:, :, bass.ds(c, P)]

            def load_rows(t):
                for name, n in ROWS[t]:
                    c0 = col[name] - t * P
                    sp.dma_start(prow[c0:c0 + n, t, :], row_src[name]).then_inc(rows_landed[min(t, 1)], 16)

            def load_scale(i):
                sp.dma_start(ada_w[:, 2 * i:2 * i + 2, :], w_ada[:, 2 * i:2 * i + 2, D:2 * D])\
                  .then_inc(scale_landed[i], 16)

            load_scale(0)
            load_scale(1)
            load_rows(0)
            load_scale(2)
            load_scale(3)
            for t in range(1, len(ROWS)):
                load_rows(t)
            for i in range(4):
                sp.dma_start(xtok[:, 2 * i:2 * i + 2, :], x_tok[:, 2 * i:2 * i + 2, :]).then_inc(x_landed[i], 16)
            load_tile(0, 0, cols(w_in, 0))
            for h in range(2):
                for i in range(KT // 2):
                    sp.dma_start(ada_w[:, KT + 2 * i:KT + 2 * i + 2, h * HALF:(h + 1) * HALF],
                                 w_ada[:, 2 * i:2 * i + 2, h * HALF:(h + 1) * HALF]).then_inc(shift_landed[h][i], 16)
            load_tile(0, 1, cols(w_in, D))
            sp.dma_start(bd_raw[:, 0, :], w_lru[0][:, 0, :]).then_inc(bd_landed, 16)
            sp.dma_start(bd_raw[:, 1, :], w_lru[1][:, 0, :]).then_inc(bd_landed, 16)
            for e in range(2):
                sp.wait_ge(xT_copied[e], COPIER.count(e))
            sp.dma_start(x_keep[:, :, :], xT[:, :, :]).then_inc(spilled, 16)
            with sp.Fori(1, KT) as m:
                load_tile(m, 0, cols(w_in, m * P))
                load_tile(m, 1, cols(w_in, m * P + D))
                sp.wait_ge(bd_lo, m)
                for j in range(2):
                    sp.dma_start(bd_raw[:, j, :], w_lru[j][:, bass.ds(m, 1), :]).then_inc(bd_landed, 16)
            def merge_tile(m, s):
                load_tile(N_MA // 2 + m, s, cols(w_pa, m * P) if s else cols(w_in, m * P + 4 * D))

            def merge_part(part, last=False):
                for e in range(2):
                    if last and e == 1:
                        load_tile(N_ZV // 2, 0, cols(w_in, 3 * D))
                    else:
                        merge_tile(2 * part + e + 1, 0)
                    sp.wait_ge(ya_lo, KT)
                    for k in range(4):
                        s = k % 2
                        sp.wait_ge(ring_used, 8 * part + 4 * e + k + 1)
                        sp.dma_start(ada_ring[s][:, :], w_ada[:, 4 * e + k, bass.ds((part + 2) * D, D)])\
                          .then_inc(ring_landed[s], 16)
                    if last and e == 1:
                        load_tile(N_ZV // 2, 1, cols(w_in, 3 * D + P))
                    else:
                        merge_tile(2 * part + e + 1, 1)

            merge_tile(0, 0)
            merge_tile(0, 1)
            with sp.Fori(0, KT // 2 - 1) as part:
                merge_part(part)
            merge_part(KT // 2 - 1, True)
            sp.wait_ge(mod_ready, 6)
            sp.dma_start(ws_raw[:, :, :], w_s).then_inc(ws_landed, 16)
            sp.wait_ge(ma_done, KT + 1)
            sp.dma_start(sbias[:, :, :].rearrange("p g t -> p (g t)"), b_s.to_broadcast([P, G * P]))\
              .then_inc(bs_landed, 16)
            with sp.Fori(1, KT // 2) as i:
                for s in range(2):
                    load_tile(N_ZV // 2 + i, s, cols(w_in, (2 * i + s) * P + 3 * D))
            with sp.Fori(0, KT // 2) as i:
                for s in range(2):
                    load_tile(N_ZU // 2 + i, s, cols(w_in, (2 * i + s) * P + 2 * D))
            with sp.Fori(0, KT) as m:
                load_tile(N_MB // 2 + m, 0, cols(w_in, m * P + 5 * D))
                load_tile(N_MB // 2 + m, 1, cols(w_pb, m * P))
            load_tile(N_OUT // 2, 0, cols(w_o, 0))
            load_tile(N_OUT // 2, 1, cols(w_o, P))
            sp.wait_ge(spilled, 16)
            for i in range(2):
                sp.wait_ge(mg_lo, (i + 1) * KT // 2)
                sp.dma_start(xT[:, i * KT // 2:(i + 1) * KT // 2, :], x_keep[:, i * KT // 2:(i + 1) * KT // 2, :])\
                  .then_inc(x_back[i], 16)
            with sp.Fori(1, KT // 2) as i:
                for s in range(2):
                    load_tile(N_OUT // 2 + i, s, cols(w_o, (2 * i + s) * P))
            with sp.Fori(0, NG) as g:
                with sp.Fori(0, KT) as j:
                    for s in range(2):
                        load_tile(N_FFN // 2 + PER_G // 2 * g + j, s, cols(w_up, g * KT * P + j * P + s * FT * P))
                with sp.Fori(0, KT // 2) as i:
                    for s in range(2):
                        load_tile(N_FFN // 2 + PER_G // 2 * g + KT + i, s,
                                  w_down[:, bass.ds(KT * g, KT), bass.ds((2 * i + s) * P, P)])
            for i in range(NB):
                sp.wait_ge(o_act, i + 1)
                sp.wait_ge(o_dve, i + 1)
                sp.dma_start(out_tok[:, i, :], otok[:, i, :]).then_inc(stored, 16)
            sp.wait_ge(stored, 16 * NB)

        @block.gpsimd
        def _(pool):
            nc.gpsimd.memset(ident[:, :], 0.0).then_inc(consts_made, 1)
            pool.wait_ge(consts_made, 1)
            nc.gpsimd.affine_select(out=ident[:, :], in_=ident[:, :], compare_op=ALU.not_equal, fill=1.0, base=0,
                                    pattern=[[-1, P]], channel_multiplier=1).then_inc(consts_made, 1)
            nc.gpsimd.memset(ones[:, :], 1.0).then_inc(consts_made, 1)
            pool.wait_ge(ws_landed, 16)
            nc.gpsimd.affine_select(out=ws_raw[:, :, :], in_=ws_raw[:, :, :], compare_op=ALU.is_ge, fill=0.0, base=0,
                                    pattern=[[0, G], [-1, P]], channel_multiplier=1).then_inc(ws_masked, 1)
            pool.wait_ge(zu_ready, KT)
            pool.wait_ge(mixed_ready, KT)
            for m in range(1, KT, 2):
                if m >= 4:
                    pool.wait_ge(yb_lo, m - 3)
                nc.gpsimd.tensor_tensor(ybt[YBT[m]][:, :], zuv[:, m, 0, :], zuv[:, m, 1, :], ALU.mult)\
                    .then_inc(ybt_odd, 1)

        @block.tensor
        def _(pe):
            def product_step(s, psum, acts, k):
                for w, x in ((0, 0), (0, 1), (1, 0)):
                    for h in range(2):
                        last = nc.tensor.matmul(
                            psum[:, h, :], wsplit[s][:, w, k, :], acts[:, k, x, h * HALF:(h + 1) * HALF],
                            start=(k == 0 and w == 0 and x == 0), stop=(k == KT - 1 and w == 1))
                return last

            def product(pair, s, psum, acts, k_sem=None, k_base=0, middle=None):
                pe.wait_ge(weights_lo, 2 * pair + s + 1)
                for k in range(KT):
                    if k == KT // 2 and middle is not None:
                        middle()
                    if k_sem is not None:
                        pe.wait_ge(k_sem, k_base + k + 1)
                    last = product_step(s, psum, acts, k)
                last.then_inc(product_done, 1)

            def product_half(pair, s, psum, acts, h, middle=None):
                pe.wait_ge(weights_lo, 2 * pair + s + 1)
                for k in range(KT):
                    if k == KT // 2 and middle is not None:
                        middle()
                    last = half_step(s, psum, acts, k, h)
                last.then_inc(product_done if h else half_done, 1)

            def half_step(s, psum, acts, k, h):
                for w, x in ((0, 0), (0, 1), (1, 0)):
                    last = nc.tensor.matmul(psum[:, h, :], wsplit[s][:, w, k, :], acts[:, k, x, H[h]],
                                            start=(k == 0 and w == 0 and x == 0), stop=(k == KT - 1 and w == 1))
                return last

            def token_sums(psum, h):
                for j in range(HB):
                    last = nc.tensor.matmul(psum[:, j:j + 1], q[:, h * HALF + j * P:h * HALF + (j + 1) * P],
                                            ones[:, 0:1], start=True, stop=True)
                last.then_inc(ss_ready, 1)

            def column_sums(src, n, psum, at=0):
                for j in range(n):
                    last = nc.tensor.matmul(psum[:, 0, at + j:at + j + 1], src[:, j * P:(j + 1) * P], ones[:, 0:1],
                                            start=True, stop=True)
                return last

            def norm_scale(h):
                pe.wait_ge(diag_ready, h + 1)
                nc.tensor.matmul(ps[3][:, h, :], ones[:, :],
                                 diag[:, HB * h:HB * h + HB, :].rearrange("p b t -> p (b t)"),
                                 start=True, stop=True).then_inc(rbc_ready, 1)

            pe.wait_ge(consts_made, 3)
            def param_columns(t):
                n = sum(n for _, n in ROWS[t])
                return nc.tensor.transpose(ps[3][:, min(t, 1), t * P:t * P + n], prow[0:n, t, :], ident[0:n, 0:n])

            pe.wait_ge(rows_landed[0], 16 * len(ROWS[0]))
            param_columns(0).then_inc(param_T, 1)
            pe.wait_ge(rows_landed[1], 16 * sum(len(r) for r in ROWS[1:]))
            for t in range(1, len(ROWS)):
                last = param_columns(t)
            last.then_inc(param_T, 1)
            for i in range(NB):
                pe.wait_ge(x_landed[i // 2], 16)
                if i == 2:
                    pe.wait_ge(param_col, len(ROWS))
                if i >= 3:
                    e = COPIER[i - 3]
                    pe.wait_ge(xT_copied[e], COPIER[:i - 2].count(e))
                for m in range(KT):
                    last = nc.tensor.transpose(blocks(ps[SLOTS[i % 3]])[:, m, :], xtok[:, i, m * P:(m + 1) * P],
                                               ident[:, :])
                last.then_inc(xT_psum, 1)
                if i == 3:
                    pe.wait_ge(ada_sum, 1)
                    column_sums(ada_acc, KT, ps[2]).then_inc(ada_psum, 1)
            for e in range(2):
                pe.wait_ge(xT_copied[e], COPIER.count(e))
            for m in range(KT):
                if m >= 3:
                    pe.wait_ge(tn_ready, m - 2)
                for i in range(NB):
                    if m == 0:
                        pe.wait_ge(x_normed, i + 1)
                    last = nc.tensor.transpose(blocks(ps[SLOTS[m % 3]])[:, i, :], xtok[:, i, m * P:(m + 1) * P],
                                               ident[:, :])
                last.then_inc(tn_psum, 1)
            pe.wait_ge(ada_sum, 2)
            column_sums(shift_acc, KT // 2, ps[2], KT).then_inc(ada_psum, 1)
            pe.wait_ge(cact_ready, 1)
            for k in range(KT):
                pe.wait_ge(shift_landed[1][k // 2], 16)
                last = nc.tensor.matmul(ps[2][0:1, 1, :], cact[:, k:k + 1], ada_w[:, KT + k, HALF:2 * HALF],
                                        start=(k == 0), stop=(k == KT - 1))
            last.then_inc(shift_row_psum, 1)

            def shift_row_to_columns():
                pe.wait_ge(shift_row_ready, 1)
                for j in range(KT // 2):
                    last = nc.tensor.matmul(ps[2][:, 0, KT + KT // 2 + j:KT + KT // 2 + j + 1],
                                            shift_row[0:1, j * P:(j + 1) * P], ones[0:1, 0:1], start=True, stop=True)
                last.then_inc(ada_psum, 1)

            def rnn(m, first=False):
                if not first:
                    pe.wait_ge(conv_done, m)
                if first:
                    pe.wait_ge(tn_ready, KT)
                    pe.wait_ge(weights_lo, 1)
                    for k in range(KT):
                        if k == 2:
                            shift_row_to_columns()
                        pe.wait_ge(norm_lo, k + 1)
                        last = product_step(0, ps[0], h_split, k)
                    last.then_inc(product_done, 1)
                else:
                    product(m, 0, ps[0], h_split)
                    pe.wait_ge(gelu_done, m)
                product(m, 1, ps[1], h_split)
                pe.wait_ge(xc_lo, m + 1)
                pe.wait_ge(bd_lo, m + 1)
                if first:
                    pe.wait_ge(mod_ready, 2)
                else:
                    pe.wait_ge(gates_read, 2 * m)
                for j in range(2):
                    for w, x in ((0, 0), (0, 1), (1, 0)):
                        for h in range(2):
                            last = nc.tensor.matmul(ps[2 + j][:, h, :], bd_split[:, w, j, :],
                                                    xc_split[:, x, h * HALF:(h + 1) * HALF],
                                                    start=(w == 0 and x == 0), stop=(w == 1))
                    last.then_inc(bd_done, 1)

            rnn(0, True)
            with pe.Fori(1, KT) as m:
                rnn(m)
            with pe.Fori(0, KT // 2) as part:
                for e in range(2):
                    pair = N_MA // 2 + 2 * part + e
                    pe.wait_ge(conv_done, KT)
                    pe.wait_ge(tga_ready, 2 * part + e + 1)
                    product(pair, 0, ps[0], h_split)
                    pe.wait_ge(gelu_done, KT)
                    pe.wait_ge(ma_done, 2 * part + e + 1)
                    product(pair, 1, ps[1], ya_split, ya_lo)
                pe.wait_ge(gates_read, 2 * KT)
                pe.wait_ge(mod_ready, part + 2)
                pe.wait_ge(ada_sum, part + 3)
                column_sums(ada_acc, KT, ps[2]).then_inc(ada_psum, 1)

            def zv(i):
                for s in range(2):
                    pe.wait_ge(zv_ready, 2 * i + s - 1)
                    product(N_ZV // 2 + i, s, ps[s], h_split)

            pe.wait_ge(tga_ready, KT + 1)
            product(N_ZV // 2, 0, ps[0], h_split)
            pe.wait_ge(ma_done, KT + 1)
            product(N_ZV // 2, 1, ps[1], h_split)
            pe.wait_ge(mod_ready, 6)
            pe.wait_ge(ws_masked, 1)
            for g in range(G):
                last = nc.tensor.transpose(blocks(ps[2])[:, g, :], ws_raw[:, g, :], ident[:, :])
            last.then_inc(ws_psum, 1)
            zv(1)
            pe.wait_ge(ws_ready, 1)
            for h in range(2):
                last = nc.tensor.matmul(ps[3][:, h, :], ones[:, :],
                                        wsT[:, 4 * h:4 * h + 4, :].rearrange("p g t -> p (g t)"), start=True, stop=True)
            last.then_inc(r_psum, 1)
            with pe.Fori(2, KT // 2) as i:
                zv(i)

            def zu(i, first=False):
                for s in range(2):
                    b = 2 * i + s

                    def v_block():
                        pe.wait_ge(staged, b + 1)
                        if not (first and s == 0):
                            pe.wait_ge(vhat_ready, b)
                        for g in range(G):
                            last = nc.tensor.transpose(blocks(ps[2])[:, g, :], vstage[:, g, :], ident[:, :])
                        last.then_inc(v_psum, 1)

                    if first and s == 0:
                        pe.wait_ge(zv_ready, KT - 1)
                        product(N_ZU // 2, 0, ps[0], h_split, middle=v_block)
                    else:
                        v_block()
                        if first:
                            pe.wait_ge(zv_ready, KT)
                        else:
                            pe.wait_ge(zu_ready, b - 1)
                        product(N_ZU // 2 + i, s, ps[s], h_split)
                    pe.wait_ge(vhat_ready, b + 1)
                    if first and s == 0:
                        pe.wait_ge(sbias_ready, 1)
                    else:
                        pe.wait_ge(mixed_ready, b)
                    for g in range(G):
                        last = nc.tensor.matmul(blocks(ps[3])[:, g, :], vhat[:, g, :], wsT[:, g, :],
                                                start=True, stop=True)
                    last.then_inc(mix_psum, 1)

            zu(0, True)
            with pe.Fori(1, KT // 2) as i:
                zu(i)

            pe.wait_ge(zu_ready, KT - 1)
            with pe.Fori(0, KT) as m:
                pe.wait_ge(tgb_ready, m + 1)
                product(N_MB // 2 + m, 0, ps[0], h_split)
                pe.wait_ge(zu_ready, KT)
                pe.wait_ge(mb_done, m + 1)
                product(N_MB // 2 + m, 1, ps[1], yb_split, yb_lo)

            def proj(i, first=False):
                for s in range(2):
                    if first:
                        pe.wait_ge(tgb_ready if s == 0 else mb_done, KT + 1)
                    else:
                        pe.wait_ge(x2_ready, 2 * i + s - 1)
                    product(N_OUT // 2 + i, s, ps[s], merged_split, mg_lo)

            proj(0, True)
            with pe.Fori(1, KT // 2 - 1) as i:
                proj(i)
            for s in range(2):
                pe.wait_ge(x2_ready, KT - 3 + s)
                product_half(LAST_IN, s, ps[s], merged_split, 0)

            def first_sums():
                pe.wait_ge(mixed_ready, KT)
                pe.wait_ge(q2_half, 2)
                token_sums(ps[3][:, 1, :], 0)

            def second_sums():
                pe.wait_ge(ss_root, 5)
                pe.wait_ge(q2_added, KT)
                token_sums(ps[3][:, 1, :], 1)

            product_half(LAST_IN, 0, ps[0], merged_split, 1, first_sums)
            norm_scale(0)
            product_half(LAST_IN, 1, ps[1], merged_split, 1)

            def ups(g, first=False):
                def pair(j, free=False):
                    f = KT * g + j
                    n2 = N_FFN // 2 + PER_G // 2 * g + j
                    if not free:
                        pe.wait_ge(ca_ready, f)
                    product(n2, 0, ps[0], h2_split)
                    pe.wait_ge(cb_ready, f)
                    product(n2, 1, ps[1], h2_split)

                if first:
                    n2 = N_FFN // 2
                    pe.wait_ge(weights_lo, 2 * n2 + 1)
                    for k in range(KT):
                        pe.wait_ge(norm_lo, KT + k + 1)
                        if k == KT // 2:
                            second_sums()
                        half_step(0, ps[2], h2_split, k, 0)
                    norm_scale(1)
                    pe.wait_ge(x2_ready, KT)
                    pe.wait_ge(weights_lo, 2 * n2 + 2)
                    for k in range(KT):
                        half_step(1, ps[1], h2_split, k, 0)
                    turns = [(k, s) for k in range(KT // 2) for s in range(2)]
                    turns += [(k, s) for s in range(2) for k in range(KT // 2, KT)]
                    for k, s in turns:
                        if s == 0:
                            pe.wait_ge(norm_lo, 2 * KT + k + 1)
                        last = half_step(s, ps[2 - s], h2_split, k, 1)
                        if k == KT - 1:
                            last.then_inc(product_done, 1)
                    pair(1, True)
                    with pe.Fori(2, KT) as j:
                        pair(j)
                else:
                    with pe.Fori(0, KT) as j:
                        pair(j)

            def downs(g, pairs=KT // 2):
                with pe.Fori(0, pairs) as i:
                    for s in range(2):
                        pe.wait_ge(down_used, KT * g + 2 * i + s + 1)
                        product(N_FFN // 2 + PER_G // 2 * g + KT + i, s, ps[2 + s], hid_split, hid_lo, KT * g)

            ups(0, True)
            pe.wait_ge(norm_lo, 3 * KT)
            downs(0)
            with pe.Fori(1, NG - 1) as g:
                ups(g)
                downs(g)
            ups(NG - 1)
            downs(NG - 1, KT // 2 - 1)
            for s in range(2):
                pe.wait_ge(down_used, KT * NG - 1 + s)
                product_half(LAST, s, ps[2 + s], hid_split, 0)

            def out_block(i, slot):
                for m in range(KT):
                    last = nc.tensor.transpose(blocks(ps[slot])[:, m, :], fin[:, m, i * P:(i + 1) * P], ident[:, :])
                last.then_inc(o_psum, 1)

            def sums_0():
                pe.wait_ge(x3_half, 1)
                pe.wait_ge(q3_half, 2)
                token_sums(ps[2][:, 0, :], 0)

            def blocks_2_3():
                for i in (2, 3):
                    pe.wait_ge(o_act, i - 1)
                    pe.wait_ge(o_dve, i - 1)
                    out_block(i, i - 2)

            product_half(LAST, 0, ps[2], hid_split, 1, sums_0)
            pe.wait_ge(ca_ready, FT)
            pe.wait_ge(cb_ready, FT)
            pe.wait_ge(fin_ready, KT - 2)
            pe.wait_ge(fin_half, 2)
            out_block(0, 0)
            out_block(1, 1)
            product_half(LAST, 1, ps[3], hid_split, 1, blocks_2_3)
            pe.wait_ge(fin_ready, KT)
            for i in (4, 5):
                pe.wait_ge(o_act, i - 1)
                pe.wait_ge(o_dve, i - 1)
                out_block(i, i - 4)
                if i == 4:
                    pe.wait_ge(q3_added, KT)
                    pe.wait_ge(ss_root, 7)
                    token_sums(ps[2][:, 0, :], 1)
            pe.wait_ge(down_used, KT * NG + 2)
            out_block(6, 3)
            pe.wait_ge(ss_root, 8)
            out_block(7, 2)

        @block.scalar
        def _(act):
            def split_hi(pair, s):
                act.wait_ge(raw_landed[s], 16 * pair + 16)
                if not (isinstance(pair, int) and pair == 0):
                    act.wait_ge(product_done, 2 * pair + s - 1)
                nc.scalar.activation(wsplit[s][:, 0, :, :], wraw[s][:, :, :], ACT.Copy).then_inc(weights_hi, 1)

            epsc = eps_t[:, 0:1]
            act.sem_inc(tga_ready, 1)
            act.sem_inc(tgb_ready, 1)
            def param_copy(t):
                n = sum(n for _, n in ROWS[t])
                nc.scalar.activation(pc[:, t * P:t * P + n], ps[3][:, min(t, 1), t * P:t * P + n], ACT.Copy)\
                    .then_inc(param_col, 1)

            act.wait_ge(param_T, 1)
            param_copy(0)
            act.wait_ge(param_col, 1)
            nc.scalar.activation(cact[:, :], C("c", 0, KT), ACT.Tanh, scale=0.5).then_inc(silu_t, 1)
            act.wait_ge(lam_e, 1)
            nc.scalar.activation(lt[:, 1, :], lt[:, 0, :], ACT.Exp, scale=-1.0).then_inc(lam_e, 1)
            act.wait_ge(param_T, 2)
            for t in range(1, len(ROWS)):
                param_copy(t)
            act.wait_ge(eps_made, 1)
            for c in range(4):
                act.wait_ge(x_landed[c], 16)
                for i in (2 * c, 2 * c + 1):
                    if i:
                        act.wait_ge(x_squared, i)
                    nc.scalar.activation(sq[:, :], xtok[:, i, :], ACT.Square, accum_out=ss[:, i:i + 1])\
                        .then_inc(x_squared, 1)
                act.wait_ge(x_squared, 2 * c + 2)
                nc.scalar.activation(rs[:, 2 * c:2 * c + 2], ss[:, 2 * c:2 * c + 2], ACT.Sqrt, bias=epsc,
                                     scale=1.0 / D).then_inc(ss_root, 1)
                for i in (2 * c, 2 * c + 1):
                    if COPIER[i] == 0:
                        act.wait_ge(xT_psum, i + 1)
                        nc.scalar.activation(xT[:, :, i * P:(i + 1) * P], blocks(ps[SLOTS[i % 3]]), ACT.Copy)\
                            .then_inc(xT_copied[0], 1)
            split_hi(0, 0)
            act.wait_ge(s1_ready, 1)
            for k in range(KT):
                act.wait_ge(tn_psum, k + 1)
                nc.scalar.activation(tn[:, k, :], flat(ps[SLOTS[k % 3]]), ACT.Copy, scale=s1[:, k:k + 1])\
                    .then_inc(tn_ready, 1)
            act.wait_ge(shift_ready, 1)
            for k in range(KT):
                if k == KT // 2:
                    act.wait_ge(shift_row_psum, 1)
                    nc.scalar.activation(shift_row[0:1, :], ps[2][0:1, 1, :], ACT.Copy).then_inc(shift_row_ready, 1)
                    act.wait_ge(shift_ready, 2)
                act.wait_ge(tn_ready, k + 1)
                nc.scalar.activation(h_split[:, k, 0, :], tn[:, k, :], ACT.Identity, bias=mod[:, k:k + 1])\
                    .then_inc(norm_hi, 1)
            split_hi(0, 1)
            act.wait_ge(bd_landed, 32)
            nc.scalar.activation(bd_split[:, 0, :, :], bd_raw[:, :, :], ACT.Copy).then_inc(bd_hi, 1)
            act.wait_ge(spilled, 16)

            def gates(m, first):
                if first:
                    act.wait_ge(lru_consts, 4)
                act.wait_ge(bd_done, 2 * m + 1)
                nc.scalar.activation(tr[:, :], flat(ps[2]), ACT.Tanh, bias=hba[:, bass.ds(m, 1)], scale=0.5)\
                    .then_inc(gates_read, 1)
                act.wait_ge(bd_done, 2 * m + 2)
                if not first:
                    act.wait_ge(ya_lo, m)
                nc.scalar.activation(ti[:, :], flat(ps[3]), ACT.Tanh, bias=hbx[:, bass.ds(m, 1)], scale=0.5)\
                    .then_inc(gates_read, 1)
                act.wait_ge(gates_read, 2 * m + 1)
                nc.scalar.activation(th[:, :], tr[:, :], ACT.Tanh, bias=la4n[:, bass.ds(m, 1)],
                                     scale=la4n[:, bass.ds(m, 1)]).then_inc(ach, 1)
                nc.scalar.activation(la_a[:, :], tr[:, :], ACT.Exp, bias=la4[:, bass.ds(m, 1)],
                                     scale=la4[:, bass.ds(m, 1)]).then_inc(ach, 1)
                act.wait_ge(ach, 2 * m + 2)
                nc.scalar.activation(m2[:, :], la_a[:, :], ACT.Square).then_inc(th_ready, 1)
                split_hi(m + 1, 1)
                act.wait_ge(m2_ready, m + 1)
                nc.scalar.activation(m2[:, :], m2[:, :], ACT.Sqrt, scale=0.25).then_inc(msq_ready, 1)

            def store_ya_hi(m):
                act.wait_ge(y_ready, m + 1)
                nc.scalar.activation(ya_split[:, bass.ds(m, 1), 0, :], ti[:, :], ACT.Copy).then_inc(ya_hi, 1)

            def rnn(m, first=False):
                act.wait_ge(product_done, 2 * m + 1)
                if not first:
                    act.wait_ge(w1_ready, m)
                nc.scalar.activation(xc[:, :], flat(ps[0]), ACT.Identity, bias=C("rnn_conv_b", m),
                                     scale=C("rnn_conv_w", (CW - 1) * KT + m)).then_inc(tap0, 1)
                split_hi(m + 1, 0)
                if not first:
                    store_ya_hi(m - 1)
                act.wait_ge(conv_done, m + 1)
                nc.scalar.activation(xc_split[:, 0, :], xc[:, :], ACT.Copy).then_inc(xc_hi, 1)
                act.wait_ge(product_done, 2 * m + 2)
                nc.scalar.activation(gg[:, :], flat(ps[1]), ACT.Gelu_apprx_tanh).then_inc(gelu_done, 1)
                gates(m, first)

            rnn(0, True)

            def bd_next(m):
                act.wait_ge(bd_landed, 32 * m + 32)
                act.wait_ge(bd_done, 2 * m)
                nc.scalar.activation(bd_split[:, 0, :, :], bd_raw[:, :, :], ACT.Copy).then_inc(bd_hi, 1)

            with act.Fori(1, KT) as m:
                bd_next(m)
                rnn(m)
            store_ya_hi(KT - 1)

            with act.Fori(0, KT) as m:
                n2 = N_MA // 2 + m
                split_hi(n2 + 1, 0)
                act.wait_ge(ma_done, m + 1)
                nc.scalar.activation(tg[:, :], flat(ps[0]), ACT.Tanh, scale=0.5).then_inc(tga_ready, 1)
                split_hi(n2 + 1, 1)

            def zv(i):
                for s in range(2):
                    split_hi(N_ZV // 2 + i + 1, s)
                    nc.scalar.activation(zuv[:, bass.ds(2 * i + s, 1), 1, :], flat(ps[s]), ACT.Gelu_apprx_tanh)\
                        .then_inc(zv_ready, 1)

            zv(0)
            act.wait_ge(ws_psum, 1)
            nc.scalar.activation(wsT[:, :, :], blocks(ps[2]), ACT.Copy).then_inc(ws_ready, 1)
            with act.Fori(1, KT // 2) as i:
                zv(i)
            act.wait_ge(zv_ready, KT)

            def stage(b):
                nc.scalar.activation(vstage[:, :, :], zuv[:, :, 1, bass.ds(b * P, P)], ACT.Copy).then_inc(staged, 1)

            stage(0)

            def zu(i, last=False):
                for s in range(2):
                    b = 2 * i + s
                    act.wait_ge(var_ready, b + 1)
                    nc.scalar.activation(sd[:, :], mv[:, 1:2], ACT.Sqrt, bias=epsc).then_inc(sd_ready, 1)
                    if not (last and s == 1):
                        act.wait_ge(v_psum, b + 1)
                        stage(b + 1)
                    split_hi(N_ZU // 2 + i + 1, s)
                    nc.scalar.activation(zuv[:, bass.ds(b, 1), 0, :], flat(ps[s]), ACT.Gelu_apprx_tanh)\
                        .then_inc(zu_ready, 1)

            with act.Fori(0, KT // 2 - 1) as i:
                zu(i)
            zu(KT // 2 - 1, True)

            def yb_part(m):
                act.wait_ge(ybt_odd if m % 2 else ybt_ready, m // 2 + 1)
                nc.scalar.activation(yb_split[:, m, 0, :], ybt[YBT[m]][:, :], ACT.Copy).then_inc(yb_hi, 1)

            for m in range(4):
                yb_part(m)
            split_hi(N_MB // 2 + 1, 0)
            for m in range(4, KT):
                yb_part(m)

            def merge_b(m, first=False):
                n2 = N_MB // 2 + m
                if not first:
                    split_hi(n2 + 1, 0)
                    act.wait_ge(mb_done, m + 1)
                nc.scalar.activation(tg[:, :], flat(ps[0]), ACT.Tanh, scale=0.5).then_inc(tgb_ready, 1)
                split_hi(n2 + 1, 1)

            merge_b(0, True)
            with act.Fori(1, KT - 1) as m:
                merge_b(m)

            def merged_hi(m):
                nc.scalar.activation(merged_split[:, m, 0, :], xT[:, m, :], ACT.Copy).then_inc(mg_hi, 1)

            m = KT - 1
            split_hi(N_MB // 2 + m + 1, 0)
            act.wait_ge(mb_done, m + 1)
            nc.scalar.activation(tg[:, :], flat(ps[0]), ACT.Tanh, scale=0.5).then_inc(tgb_ready, 1)
            for k in range(KT - 1):
                merged_hi(k)
            split_hi(N_MB // 2 + m + 1, 1)
            act.wait_ge(mb_done, KT + 1)
            merged_hi(KT - 1)

            def proj(i, first=False):
                for s in range(2):
                    m = 2 * i + s
                    act.wait_ge(x2_ready, m + 1)
                    if not (first and s == 0):
                        act.wait_ge(q2_added, m)
                    nc.scalar.activation(sq[:, :], xT[:, bass.ds(m, 1), :], ACT.Square).then_inc(sq2_ready, 1)
                    split_hi(N_OUT // 2 + i + 1, s)

            def square(m, h, read, added, done):
                act.wait_ge(read, added)
                nc.scalar.activation(sq[:, H[h]], xT[:, m, H[h]], ACT.Square).then_inc(done, 1)

            def token_root(h, psum, count):
                act.wait_ge(ss_ready, count)
                nc.scalar.activation(rs[:, HB * h:HB * h + HB], psum[:, 0:HB], ACT.Sqrt, bias=epsc, scale=1.0 / D)\
                    .then_inc(ss_root, 1)

            def root_table():
                nc.scalar.activation(sd[:, :], eps_t[:, :], ACT.Sqrt)

            proj(0, True)
            with act.Fori(1, KT // 2 - 1) as i:
                proj(i)
            root_table()
            act.wait_ge(x2_half, 1)
            square(KT - 2, 0, q2_added, KT - 2, sq2_half)
            act.wait_ge(x2_half, 2)
            square(KT - 1, 0, q2_half, 1, sq2_half)
            token_root(0, ps[3][:, 1, :], 1)
            act.wait_ge(x2_ready, KT - 1)
            square(KT - 2, 1, q2_added, KT - 2, sq2_ready)
            split_hi(LAST_IN + 1, 0)
            for n in range(2 * KT):
                h, k = divmod(n, KT)
                act.wait_ge(nt_ready, n + 1)
                nc.scalar.activation(h2_split[:, k, 0, H[h]], nt_half[n % 4], ACT.Identity,
                                     bias=mod[:, 3 * KT + k:3 * KT + k + 1]).then_inc(norm_hi, 1)
                if n == N2_LAST:
                    act.wait_ge(x2_ready, KT)
                    square(KT - 1, 1, q2_added, KT - 1, sq2_ready)
                if n == N2_ROOT:
                    token_root(1, ps[3][:, 1, :], 2)
                    split_hi(LAST_IN + 1, 1)

            def up(g, j, first=False):
                f = KT * g + j
                n2 = N_FFN // 2 + PER_G // 2 * g + j
                for dst, s, o, done in ((ca, 0, 0, tap0a), (cb, 1, FT, tap0b)):
                    act.wait_ge(product_done, 2 * n2 + s + 1)
                    if first and s == 0:
                        split_hi(n2 + 1, 0)
                    if not first:
                        act.wait_ge(g_ready, f)
                    nc.scalar.activation(dst[:, :], flat(ps[2] if first and s == 0 else ps[s]), ACT.Identity,
                                         bias=C("ffn_conv_b", o + f), scale=C("ffn_conv_w2", o + f)).then_inc(done, 1)
                    if not (first and s == 0):
                        split_hi(n2 + 1, s)
                    if s == 0:
                        act.wait_ge(ca_ready, f + 1)
                        nc.scalar.activation(ca[:, :], ca[:, :], ACT.Gelu_apprx_tanh).then_inc(ga_ready, 1)
                act.wait_ge(g_ready, f + 1)
                nc.scalar.activation(hid_split[:, bass.ds(j, 1), 0, :], gt[:, :], ACT.Copy).then_inc(hid_hi, 1)

            def ups(g, first=False):
                if first:
                    up(0, 0, True)
                with act.Fori(1 if first else 0, KT) as j:
                    up(g, j)

            def downs(g):
                with act.Fori(0, KT // 2) as i:
                    for s in range(2):
                        split_hi(N_FFN // 2 + PER_G // 2 * g + KT + i + 1, s)

            ups(0, True)
            downs(0)
            with act.Fori(1, NG - 1) as g:
                ups(g)
                downs(g)
            ups(NG - 1)

            def last_down(i, first=False):
                for s in range(2):
                    m = 2 * i + s
                    split_hi(N_TILES // 2 - KT // 2 + i + 1, s)
                    act.wait_ge(down_used, KT * (NG - 1) + m + 3)
                    nc.scalar.activation(fin[:, bass.ds(m, 1), :], xT[:, bass.ds(m, 1), :], ACT.Identity,
                                         scale=C("norm_final_g", m)).then_inc(fin_ready, 1)
                    if not (first and s == 0):
                        act.wait_ge(q3_added, m)
                        settled(act)
                    nc.scalar.activation(sq[:, :], xT[:, bass.ds(m, 1), :], ACT.Square).then_inc(sq3_ready, 1)

            last_down(0, True)
            with act.Fori(1, KT // 2 - 1) as i:
                last_down(i)
            root_table()

            def fin_part(m, h, done):
                nc.scalar.activation(fin[:, m, H[h]], xT[:, m, H[h]], ACT.Identity, scale=C("norm_final_g", m))\
                    .then_inc(done, 1)

            def out_half(i, slot):
                act.wait_ge(o_psum, i + 1)
                nc.scalar.activation(otok[:, i, H[0]], ps[slot][:, 0, :], ACT.Identity, scale=rs[:, i:i + 1])\
                    .then_inc(o_act, 1)

            act.wait_ge(x3_half, 1)
            square(KT - 2, 0, q3_added, KT - 2, sq3_half)
            fin_part(KT - 2, 0, fin_half)
            act.wait_ge(x3_half, 2)
            square(KT - 1, 0, q3_half, 1, sq3_half)
            fin_part(KT - 1, 0, fin_half)
            token_root(0, ps[2][:, 0, :], 3)
            act.wait_ge(down_used, KT * NG + 1)
            square(KT - 2, 1, q3_added, KT - 2, sq3_ready)
            fin_part(KT - 2, 1, fin_ready)
            act.wait_ge(diag_ready, 3)
            for i in range(HB):
                out_half(i, i % 2)
            act.wait_ge(down_used, KT * NG + 2)
            square(KT - 1, 1, q3_added, KT - 1, sq3_ready)
            fin_part(KT - 1, 1, fin_ready)
            token_root(1, ps[2][:, 0, :], 4)
            act.wait_ge(diag_ready, 4)
            for i in range(HB, NB):
                out_half(i, (0, 1, 3, 2)[i - HB])

        @block.vector
        def _(dve):
            V = nc.vector
            steps = [0]

            def step(ins):
                steps[0] += 1
                ins.then_inc(vch, 1)
                dve.wait_ge(vch, steps[0])

            def split_lo(pair, s):
                dve.wait_ge(weights_hi, 2 * pair + s + 1)
                V.tensor_tensor(wsplit[s][:, 1, :, :], wraw[s][:, :, :], wsplit[s][:, 0, :, :].bitcast(F32),
                                ALU.subtract).then_inc(weights_lo, 1)

            def bd_next(m):
                dve.wait_ge(bd_hi, m + 1)
                V.tensor_tensor(bd_split[:, 1, :, :], bd_raw[:, :, :], bd_split[:, 0, :, :].bitcast(F32),
                                ALU.subtract).then_inc(bd_lo, 1)

            def ada_piece(w, k, first, acc=ada_acc):
                if first:
                    return V.tensor_scalar(acc[:, :], w, cact[:, k:k + 1], None, ALU.mult)
                return V.scalar_tensor_tensor(acc[:, :], w, cact[:, k:k + 1], acc[:, :], ALU.mult, ALU.add)

            def mod_part(part, count):
                dve.wait_ge(ada_psum, count)
                dst = mod[:, part * KT:(part + 1) * KT] if isinstance(part, int) else mod[:, bass.ds(part * KT, KT)]
                V.tensor_tensor(dst, ps[2][:, 0, 0:KT], C("b_ada", part * KT, KT), ALU.add).then_inc(mod_ready, 1)

            def inverse_root(h):
                part = rs[:, HB * h:HB * h + HB]
                return V.reciprocal(part, part)

            def rms_diag(h):
                dve.wait_ge(ss_root, 5 + h)
                step(inverse_root(h))
                V.tensor_tensor(diag[:, HB * h:HB * h + HB, :], ident[:, :].unsqueeze(1).to_broadcast([P, HB, P]),
                                rs[:, HB * h:HB * h + HB].unsqueeze(2).to_broadcast([P, HB, P]), ALU.mult)\
                 .then_inc(diag_ready, 1)

            def add_square_half(h, squared, n_squared, added, n_added, done):
                dve.wait_ge(squared, n_squared)
                dve.wait_ge(added, n_added)
                V.tensor_tensor(q[:, H[h]], q[:, H[h]], sq[:, H[h]], ALU.add).then_inc(done, 1)

            def modulation(dst, part, g):
                return V.scalar_tensor_tensor(dst[:, :], mod[:, part * KT:(part + 1) * KT], 1.0, C(g, 0, KT),
                                              ALU.add, ALU.mult)

            dve.sem_inc(ma_done, 1)
            dve.sem_inc(mb_done, 1)
            dve.sem_inc(ring_used, 2)
            dve.sem_inc(down_used, 2)
            V.memset(eps_t[:, :], EPS).then_inc(eps_made, 1)
            dve.wait_ge(silu_t, 1)
            step(V.tensor_scalar(cact[:, :], cact[:, :], 1.0, 0.5, ALU.add, ALU.mult))
            V.tensor_tensor(cact[:, :], cact[:, :], C("c", 0, KT), ALU.mult).then_inc(cact_ready, 1)
            lam = C("lru_lambda", 0, KT)
            step(V.tensor_scalar(lt[:, 2, :], lam, -1.0, None, ALU.mult))
            V.tensor_tensor(lt[:, 0, :], lt[:, 2, :], lam, ALU.max).then_inc(lam_e, 1)

            TERMS, MIDDLE = 9, 5

            def series_terms(start, stop):
                for j in range(start, stop - 1, -1):
                    step(V.tensor_tensor(lt[:, 3, :], lt[:, 3, :], lt[:, 2, :], ALU.mult))
                    step(V.tensor_scalar(lt[:, 3, :], lt[:, 3, :], 1.0 / (2 * j + 1), None, ALU.add))

            def log_sigmoid_start():
                dve.wait_ge(lam_e, 2)
                step(V.tensor_scalar(lt[:, 2, :], lt[:, 1, :], 2.0, None, ALU.add))
                step(V.reciprocal(lt[:, 2, :], lt[:, 2, :]))
                step(V.tensor_tensor(lt[:, 1, :], lt[:, 1, :], lt[:, 2, :], ALU.mult))
                step(V.tensor_tensor(lt[:, 2, :], lt[:, 1, :], lt[:, 1, :], ALU.mult))
                step(V.tensor_scalar(lt[:, 3, :], lt[:, 2, :], 1.0 / (2 * TERMS + 1), 1.0 / (2 * TERMS - 1),
                                     ALU.mult, ALU.add))
                series_terms(TERMS - 2, MIDDLE)

            def lru_constants():
                series_terms(MIDDLE - 1, 0)
                step(V.tensor_tensor(lt[:, 3, :], lt[:, 3, :], lt[:, 1, :], ALU.mult))
                step(V.tensor_scalar(lt[:, 4, :], lam, 0.0, None, ALU.min))
                step(V.scalar_tensor_tensor(lt[:, 4, :], lt[:, 3, :], -2.0, lt[:, 4, :], ALU.mult, ALU.add))
                V.tensor_scalar(la4[:, :], lt[:, 4, :], LRU_C / 2, None, ALU.mult).then_inc(lru_consts, 1)
                V.tensor_scalar(la4n[:, :], lt[:, 4, :], -LRU_C / 2, None, ALU.mult).then_inc(lru_consts, 1)
                V.tensor_scalar(hba[:, :], C("lru_b_a", 0, KT), 0.5, None, ALU.mult).then_inc(lru_consts, 1)
                V.tensor_scalar(hbx[:, :], C("lru_b_x", 0, KT), 0.5, None, ALU.mult).then_inc(lru_consts, 1)

            def add_square(sem_ready, sem_added, m, first):
                dve.wait_ge(sem_ready, m + 1)
                if first:
                    V.tensor_copy(q[:, :], sq[:, :]).then_inc(sem_added, 1)
                else:
                    dve.wait_ge(sem_added, m)
                    V.tensor_tensor(q[:, :], q[:, :], sq[:, :], ALU.add).then_inc(sem_added, 1)

            dve.wait_ge(cact_ready, 1)
            for k in range(KT):
                dve.wait_ge(scale_landed[k // 2], 16)
                if k:
                    dve.wait_ge(ada_step, k)
                ada_piece(ada_w[:, k, :], k, k == 0).then_inc(ada_step, 1)
            dve.wait_ge(ada_step, KT)
            dve.sem_inc(ada_sum, 1)
            for c in range(4):
                for i in (2 * c, 2 * c + 1):
                    if COPIER[i] == 1:
                        dve.wait_ge(xT_psum, i + 1)
                        V.tensor_copy(xT[:, :, i * P:(i + 1) * P], blocks(ps[SLOTS[i % 3]])).then_inc(xT_copied[1], 1)
                dve.wait_ge(xT_psum, 2 * c + 2)
                dve.wait_ge(ss_root, c + 1)
                step(V.reciprocal(rs[:, 2 * c:2 * c + 2], rs[:, 2 * c:2 * c + 2]))
                for i in (2 * c, 2 * c + 1):
                    V.tensor_scalar(xtok[:, i, :], xtok[:, i, :], rs[:, i:i + 1], None, ALU.mult).then_inc(x_normed, 1)
                if c == 1:
                    mod_part(1, 1)
                    dve.wait_ge(mod_ready, 1)
                    modulation(s1, 1, "norm_mix_g").then_inc(s1_ready, 1)
            for k in range(KT):
                dve.wait_ge(shift_landed[0][k // 2], 16)
                if k:
                    dve.wait_ge(ada_step, KT + k)
                ada_piece(ada_w[:, KT + k, 0:HALF], k, k == 0, shift_acc).then_inc(ada_step, 1)
            dve.wait_ge(ada_step, 2 * KT)
            dve.sem_inc(ada_sum, 1)
            split_lo(0, 0)

            def shift_half(h):
                n = KT // 2
                dve.wait_ge(ada_psum, 2 + h)
                V.tensor_tensor(mod[:, h * n:(h + 1) * n], ps[2][:, 0, KT + h * n:KT + (h + 1) * n],
                                C("b_ada", h * n, n), ALU.add).then_inc(shift_ready, 1)
                dve.wait_ge(shift_ready, h + 1)

            shift_half(0)
            log_sigmoid_start()
            for k in range(KT):
                if k == KT // 2:
                    lru_constants()
                    shift_half(1)
                    dve.sem_inc(mod_ready, 1)
                dve.wait_ge(norm_hi, k + 1)
                V.scalar_tensor_tensor(h_split[:, k, 1, :], tn[:, k, :], mod[:, k:k + 1],
                                       h_split[:, k, 0, :].bitcast(F32), ALU.add, ALU.subtract).then_inc(norm_lo, 1)
            split_lo(0, 1)
            bd_next(0)
            dve.wait_ge(spilled, 16)

            def conv(dst, src, width, taps, step_sem, before, done):
                for d in range(1, width):
                    if d > 1:
                        ins.then_inc(step_sem, 1)
                        dve.wait_ge(step_sem, before + d - 1)
                    ins = V.scalar_tensor_tensor(dst[:, d:S], flat(src)[:, 0:S - d], taps(width - 1 - d), dst[:, d:S],
                                                 ALU.mult, ALU.add)
                ins.then_inc(done, 1)

            def rnn_tail(m):
                dve.wait_ge(w1_ready, m + 1)
                dve.wait_ge(msq_ready, m + 1)
                V.tensor_tensor(ti[:, :], ti[:, :], m2[:, :], ALU.mult).then_inc(tail_step, 1)
                dve.wait_ge(tail_step, 2 * m + 1)
                V.tensor_tensor_scan(ti[:, :], la_a[:, :], ti[:, :], 0.0, ALU.mult, ALU.add).then_inc(tail_step, 1)
                dve.wait_ge(tail_step, 2 * m + 2)
                V.tensor_tensor(ti[:, :], ti[:, :], gg[:, :], ALU.mult).then_inc(y_ready, 1)

            def ya_part(m):
                dve.wait_ge(ya_hi, m + 1)
                V.tensor_tensor(ya_split[:, bass.ds(m, 1), 1, :], ti[:, :], ya_split[:, bass.ds(m, 1), 0, :].bitcast(F32),
                                ALU.subtract).then_inc(ya_lo, 1)

            def rnn(m, first=False):
                split_lo(m + 1, 0)
                dve.wait_ge(tap0, m + 1)
                conv(xc, ps[0], CW, lambda k: C("rnn_conv_w", k * KT + m), conv_step, (CW - 2) * m, conv_done)
                dve.wait_ge(xc_hi, m + 1)
                V.tensor_tensor(xc_split[:, 1, :], xc[:, :], xc_split[:, 0, :].bitcast(F32), ALU.subtract)\
                 .then_inc(xc_lo, 1)
                if not first:
                    ya_part(m - 1)
                dve.wait_ge(gates_read, 2 * m + 2)
                V.scalar_tensor_tensor(ti[:, :], ti[:, :], 1.0, xc[:, :], ALU.add, ALU.mult).then_inc(w1_ready, 1)
                dve.wait_ge(th_ready, m + 1)
                V.scalar_tensor_tensor(m2[:, :], m2[:, :], 1.0, th[:, :], ALU.add, ALU.mult).then_inc(m2_ready, 1)
                split_lo(m + 1, 1)
                rnn_tail(m)

            rnn(0, True)
            with dve.Fori(1, KT) as m:
                bd_next(m)
                rnn(m)
            ya_part(KT - 1)

            with dve.Fori(0, KT // 2) as part:
                for e in range(2):
                    m = 2 * part + e
                    n2 = N_MA // 2 + m
                    split_lo(n2 + 1, 0)
                    for k in range(4):
                        kk = 4 * e + k
                        dve.wait_ge(ring_landed[k % 2], 64 * part + 32 * e + 16 * (k // 2) + 16)
                        if kk == 0:
                            dve.wait_ge(ada_psum, part + 3)
                        else:
                            dve.wait_ge(ring_used, 8 * part + kk + 2)
                        ins = ada_piece(ada_ring[k % 2][:, :], kk, kk == 0)
                        ins.then_inc(ring_used, 1)
                    if e == 1:
                        dve.wait_ge(ring_used, 8 * part + 10)
                        dve.sem_inc(ada_sum, 1)
                    split_lo(n2 + 1, 1)
                    dve.wait_ge(tga_ready, m + 2)
                    V.scalar_tensor_tensor(xT[:, bass.ds(m, 1), :], tg[:, :], 1.0, flat(ps[1]), ALU.add, ALU.mult)\
                     .then_inc(ma_done, 1)
                mod_part(part + 2, part + 4)
            dve.wait_ge(mod_ready, 6)
            V.tensor_scalar(g1h[:, :], mod[:, 2 * KT:3 * KT], 0.5, None, ALU.mult).then_inc(g1h_ready, 1)

            for s in range(2):
                split_lo(N_ZV // 2 + 1, s)
            for s in range(2):
                split_lo(N_ZV // 2 + 2, s)
            dve.wait_ge(r_psum, 1)
            dve.wait_ge(bs_landed, 16)
            for g in range(G):
                last = V.scalar_tensor_tensor(sbias[:, g, :], blocks(ps[3])[:, g, :], C("sgu_ln_b", g), sbias[:, g, :],
                                              ALU.mult, ALU.add)
            last.then_inc(sbias_ready, 1)
            with dve.Fori(2, KT // 2) as i:
                for s in range(2):
                    split_lo(N_ZV // 2 + i + 1, s)

            def zu(i):
                for s in range(2):
                    b = 2 * i + s
                    dve.wait_ge(v_psum, b + 1)
                    for h in range(2):
                        V.bn_stats(stats[:, h, :], ps[2][:, h, :]).then_inc(ln_step, 1)
                    dve.wait_ge(ln_step, 4 * b + 2)
                    settled(dve)
                    V.bn_aggr(mv[:, :], stats[:, :, :].rearrange("p a b -> p (a b)")).then_inc(var_ready, 1)
                    dve.wait_ge(sd_ready, b + 1)
                    V.reciprocal(rsd[:, :], sd[:, :]).then_inc(ln_step, 1)
                    dve.wait_ge(ln_step, 4 * b + 3)
                    V.tensor_scalar(vhat[:, :, :], blocks(ps[2]), mv[:, 0:1], rsd[:, 0:1], ALU.subtract, ALU.mult)\
                     .then_inc(vhat_ready, 1)
                    split_lo(N_ZU // 2 + i + 1, s)
                    dve.wait_ge(mix_psum, b + 1)
                    V.tensor_tensor(blocks(ps[3]), blocks(ps[3]),
                                    pc[:, col["sgu_ln_g"]:col["sgu_ln_g"] + G].unsqueeze(2).to_broadcast([P, G, P]),
                                    ALU.mult).then_inc(ln_step, 1)
                    dve.wait_ge(ln_step, 4 * b + 4)
                    V.tensor_tensor(zuv[:, :, 1, bass.ds(b * P, P)], blocks(ps[3]), sbias[:, :, :], ALU.add)\
                     .then_inc(mixed_ready, 1)

            with dve.Fori(0, KT // 2) as i:
                zu(i)

            dve.wait_ge(zu_ready, KT)
            dve.wait_ge(mixed_ready, KT)
            dve.wait_ge(ma_done, KT + 1)

            def yb_mul(m):
                if m >= 2:
                    dve.wait_ge(yb_lo, m - 1)
                V.tensor_tensor(ybt[YBT[m]][:, :], zuv[:, m, 0, :], zuv[:, m, 1, :], ALU.mult).then_inc(ybt_ready, 1)

            def yb_sub(m):
                dve.wait_ge(yb_hi, m + 1)
                V.tensor_tensor(yb_split[:, m, 1, :], ybt[YBT[m]][:, :], yb_split[:, m, 0, :].bitcast(F32), ALU.subtract)\
                 .then_inc(yb_lo, 1)

            yb_mul(0)
            for m in range(KT):
                yb_sub(m)
                if m % 2 == 0 and m + 2 < KT:
                    yb_mul(m + 2)
                if m == 3:
                    split_lo(N_MB // 2 + 1, 0)

            def merge_b(m):
                dve.wait_ge(tgb_ready, m + 2)
                dve.wait_ge(mb_done, m + 1)
                V.scalar_tensor_tensor(mt[:, :], tg[:, :], 1.0, flat(ps[1]), ALU.add, ALU.mult).then_inc(mb_step, 1)
                dve.wait_ge(mb_step, m + 1)
                V.tensor_tensor(xT[:, bass.ds(m, 1), :], xT[:, bass.ds(m, 1), :], mt[:, :], ALU.add).then_inc(mb_done, 1)

            split_lo(N_MB // 2 + 1, 1)
            dve.wait_ge(yb_lo, KT)
            merge_b(0)
            with dve.Fori(1, KT - 1) as m:
                split_lo(N_MB // 2 + m + 1, 0)
                split_lo(N_MB // 2 + m + 1, 1)
                merge_b(m)

            def merged_lo(m):
                dve.wait_ge(mg_hi, m + 1)
                V.tensor_tensor(merged_split[:, m, 1, :], xT[:, m, :], merged_split[:, m, 0, :].bitcast(F32),
                                ALU.subtract).then_inc(mg_lo, 1)

            m = KT - 1
            split_lo(N_MB // 2 + m + 1, 0)
            for k in range(KT - 1):
                merged_lo(k)
            split_lo(N_MB // 2 + m + 1, 1)
            merge_b(m)
            merged_lo(KT - 1)

            def proj(i, first=False):
                for s in range(2):
                    m = 2 * i + s
                    dve.wait_ge(product_done, N_OUT + m + 1)
                    V.scalar_tensor_tensor(xT[:, bass.ds(m, 1), :], flat(ps[s]), g1h[:, bass.ds(m, 1)],
                                           xT[:, bass.ds(m, 1), :], ALU.mult, ALU.add).then_inc(x2_ready, 1)
                    add_square(sq2_ready, q2_added, m, first and s == 0)
                    split_lo(N_OUT // 2 + i + 1, s)

            dve.wait_ge(g1h_ready, 1)
            dve.wait_ge(x_back[0], 16)
            def proj_half(s, h):
                m = KT - 2 + s
                dve.wait_ge(product_done if h else half_done, N_OUT + m + 1 if h else s + 1)
                V.scalar_tensor_tensor(xT[:, m, H[h]], ps[s][:, h, :], g1h[:, m:m + 1], xT[:, m, H[h]],
                                       ALU.mult, ALU.add).then_inc(x2_ready if h else x2_half, 1)

            proj(0, True)
            modulation(s2, 4, "norm_ffn_g").then_inc(s2_ready, 1)
            proj(1)
            dve.wait_ge(x_back[1], 16)
            with dve.Fori(2, KT // 2 - 1) as i:
                proj(i)
            proj_half(0, 0)
            add_square_half(0, sq2_half, 1, q2_added, KT - 2, q2_half)
            proj_half(1, 0)
            add_square_half(0, sq2_half, 2, q2_half, 1, q2_half)
            dve.wait_ge(q2_half, 2)
            rms_diag(0)
            proj_half(0, 1)
            add_square_half(1, sq2_ready, KT - 1, q2_added, KT - 2, q2_added)
            split_lo(LAST_IN + 1, 0)
            dve.wait_ge(s2_ready, 1)

            def h2_scaled(n):
                h, k = divmod(n, KT)
                if k == 0:
                    dve.wait_ge(rbc_ready, h + 1)
                if n >= 4:
                    dve.wait_ge(norm_lo, KT + n - 3)
                V.scalar_tensor_tensor(nt_half[n % 4], xT[:, k, H[h]], s2[:, k:k + 1], ps[3][:, h, :],
                                       ALU.mult, ALU.mult).then_inc(nt_ready, 1)

            def h2_lo(n):
                h, k = divmod(n, KT)
                dve.wait_ge(norm_hi, KT + n + 1)
                V.scalar_tensor_tensor(h2_split[:, k, 1, H[h]], nt_half[n % 4],
                                       mod[:, 3 * KT + k:3 * KT + k + 1], h2_split[:, k, 0, H[h]].bitcast(F32),
                                       ALU.add, ALU.subtract).then_inc(norm_lo, 1)

            for h in range(2):
                first_n = KT * h
                for k in range(2):
                    h2_scaled(first_n + k)
                for k in range(KT):
                    n = first_n + k
                    h2_lo(n)
                    if k + 2 < KT:
                        h2_scaled(n + 2)
                    if n == N2_LAST:
                        proj_half(1, 1)
                    if n == N2_LAST + 1:
                        add_square_half(1, sq2_ready, KT, q2_added, KT - 1, q2_added)
                    if n == N2_ROOT:
                        dve.wait_ge(q2_added, KT)
                        rms_diag(1)
                        split_lo(LAST_IN + 1, 1)

            dve.wait_ge(x2_ready, KT)

            def up(g, j, first=False):
                f = KT * g + j
                n2 = N_FFN // 2 + PER_G // 2 * g + j

                def taps(o):
                    def tap(k):
                        return C("ffn_conv_w01" if k < 2 else "ffn_conv_w2", (k % 2) * 2 * FT + o + f)
                    return tap

                if first:
                    split_lo(n2 + 1, 0)
                dve.wait_ge(tap0a, f + 1)
                conv(ca, ps[2] if first else ps[0], FW, taps(0), ffn_conv_step, 2 * (FW - 2) * f, ca_ready)
                if not first:
                    split_lo(n2 + 1, 0)
                dve.wait_ge(tap0b, f + 1)
                conv(cb, ps[1], FW, taps(FT), ffn_conv_step, 2 * (FW - 2) * f + FW - 2, cb_ready)
                dve.wait_ge(cb_ready, f + 1)
                dve.wait_ge(ga_ready, f + 1)
                V.tensor_tensor(gt[:, :], ca[:, :], cb[:, :], ALU.mult).then_inc(g_ready, 1)
                split_lo(n2 + 1, 1)
                dve.wait_ge(hid_hi, f + 1)
                V.tensor_tensor(hid_split[:, bass.ds(j, 1), 1, :], gt[:, :],
                                hid_split[:, bass.ds(j, 1), 0, :].bitcast(F32), ALU.subtract).then_inc(hid_lo, 1)

            def ups(g, first=False):
                if first:
                    up(0, 0, True)
                with dve.Fori(1 if first else 0, KT) as j:
                    up(g, j)

            def down(m, s):
                V.scalar_tensor_tensor(xT[:, bass.ds(m, 1), :], flat(ps[2 + s]), mod[:, bass.ds(5 * KT + m, 1)],
                                       xT[:, bass.ds(m, 1), :], ALU.mult, ALU.add).then_inc(down_used, 1)

            def downs(g):
                with dve.Fori(0, KT // 2) as i:
                    for s in range(2):
                        split_lo(N_FFN // 2 + PER_G // 2 * g + KT + i + 1, s)
                        down(2 * i + s, s)

            ups(0, True)
            downs(0)
            with dve.Fori(1, NG - 1) as g:
                ups(g)
                dve.wait_ge(down_used, KT * g + 2)
                settled(dve)
                downs(g)
            ups(NG - 1)
            dve.wait_ge(down_used, KT * (NG - 1) + 2)

            def last_down(i, first=False):
                for s in range(2):
                    m = 2 * i + s
                    split_lo(N_TILES // 2 - KT // 2 + i + 1, s)
                    down(m, s)
                    add_square(sq3_ready, q3_added, m, first and s == 0)

            last_down(0, True)
            with dve.Fori(1, KT // 2 - 1) as i:
                last_down(i)

            def down_half(s, h):
                m = KT - 2 + s
                dve.wait_ge(product_done if h else half_done, N_TILES - 1 + s if h else 3 + s)
                V.scalar_tensor_tensor(xT[:, m, H[h]], ps[2 + s][:, h, :], mod[:, 5 * KT + m:5 * KT + m + 1],
                                       xT[:, m, H[h]], ALU.mult, ALU.add).then_inc(down_used if h else x3_half, 1)

            def out_half(i, slot):
                dve.wait_ge(o_psum, i + 1)
                V.tensor_scalar(otok[:, i, H[1]], ps[slot][:, 1, :], rs[:, i:i + 1], None, ALU.mult).then_inc(o_dve, 1)

            down_half(0, 0)
            add_square_half(0, sq3_half, 1, q3_added, KT - 2, q3_half)
            down_half(1, 0)
            add_square_half(0, sq3_half, 2, q3_half, 1, q3_half)
            dve.wait_ge(ss_root, 7)
            inverse_root(0).then_inc(diag_ready, 1)
            down_half(0, 1)
            add_square_half(1, sq3_ready, KT - 1, q3_added, KT - 2, q3_added)
            dve.wait_ge(diag_ready, 3)
            for i in range(HB):
                out_half(i, i % 2)
            down_half(1, 1)
            add_square_half(1, sq3_ready, KT, q3_added, KT - 1, q3_added)
            dve.wait_ge(ss_root, 8)
            inverse_root(1).then_inc(diag_ready, 1)
            dve.wait_ge(diag_ready, 4)
            for i in range(HB, NB):
                out_half(i, (0, 1, 3, 2)[i - HB])


def kernel(**inputs):
    import numpy as np
    import concourse.bacc as bacc
    from concourse.bass_utils import run_bass_kernel_spmd

    nc = bacc.Bacc("TRN2", target_bir_lowering=False, num_devices=1)
    arrays, aps = {}, {}
    for name, value in inputs.items():
        value = np.ascontiguousarray(value)
        arrays[f"in_{name}"] = value
        aps[name] = nc.dram_tensor(f"in_{name}", value.shape, mybir.dt.from_np(value.dtype), kind="ExternalInput").ap()
    out = nc.dram_tensor("out_x", inputs["x"].shape, F32, kind="ExternalOutput").ap()
    build(nc, aps, out)
    result = run_bass_kernel_spmd(nc, [arrays], core_ids=[0])
    return result.results[0]["out_x"]
```
